# Optimizing a Trainium2 kernel written in Bass

```python
import math
import jax, jax.numpy as jnp
from jax import lax
import numpy as np

D_MODEL = 1024
BATCH = 1
SEQ = 256
DEPTH = 2

HEAD_DIM = 64
DIFF_HEADS = 4
FOX_HEADS = 8
DIFF_QK_WIDTH = 2 * DIFF_HEADS * HEAD_DIM
DIFF_V_WIDTH = DIFF_HEADS * 2 * HEAD_DIM
FOX_WIDTH = FOX_HEADS * HEAD_DIM
ROT_DIM = HEAD_DIM // 4
ROPE_THETA = 500000.0
Q_BLOCK = 128
N_GROUPS = 4
EXPERTS_PER_GROUP = 8
EXPERT_FF = 512
TOP_K_INNER = 2
EPS = 1e-6
SPLIT_SIZES = (DIFF_QK_WIDTH, DIFF_QK_WIDTH, DIFF_V_WIDTH, FOX_WIDTH, FOX_WIDTH, FOX_WIDTH, FOX_HEADS, 2 * D_MODEL)
IN_COLS = sum(SPLIT_SIZES)

kernel_name = "hybrid_diffattn_fox_hmoe_block"

def rms_norm(x, g):
    xf = x.astype(jnp.float32)
    y = xf * lax.rsqrt(jnp.mean(xf * xf, axis=-1, keepdims=True) + EPS)
    return (y * g.astype(jnp.float32)).astype(x.dtype)

def split_heads(t, n_heads):
    b, s, w = t.shape
    return t.reshape(b, s, n_heads, w // n_heads).transpose(0, 2, 1, 3)

def merge_heads(t):
    b, h, s, d = t.shape
    return t.transpose(0, 2, 1, 3).reshape(b, s, h * d)

def rotary_tables(positions, dtype):
    inv_freq = ROPE_THETA ** (-jnp.arange(0, ROT_DIM, 2, dtype=jnp.float32) / ROT_DIM)
    ang = positions.astype(jnp.float32)[..., None] * inv_freq
    return jnp.cos(ang)[:, None].astype(dtype), jnp.sin(ang)[:, None].astype(dtype)

def partial_rotary(t, cos, sin):
    half = ROT_DIM // 2
    t1, t2, rest = t[..., :half], t[..., half:ROT_DIM], t[..., ROT_DIM:]
    return jnp.concatenate([t1 * cos - t2 * sin, t2 * cos + t1 * sin, rest], axis=-1)

def causal_block_attention(q, k, v, q_bias=None, k_bias=None):
    b, h, s, dk = q.shape
    dv = v.shape[-1]
    scale = dk ** -0.5
    k_pos = jnp.arange(s)

    def one_block(i):
        start = i * Q_BLOCK
        qb = lax.dynamic_slice_in_dim(q, start, Q_BLOCK, axis=2)
        logits = jnp.einsum('bhqd,bhkd->bhqk', qb, k).astype(jnp.float32) * scale
        if q_bias is not None:
            qbb = lax.dynamic_slice_in_dim(q_bias, start, Q_BLOCK, axis=2)
            logits = logits + qbb[..., :, None] + k_bias[..., None, :]
        q_pos = start + jnp.arange(Q_BLOCK)
        mask = k_pos[None, :] <= q_pos[:, None]
        logits = jnp.where(mask, logits, -jnp.inf)
        p = jax.nn.softmax(logits, axis=-1).astype(v.dtype)
        return jnp.einsum('bhqk,bhkv->bhqv', p, v)

    out = lax.map(one_block, jnp.arange(s // Q_BLOCK))
    return out.transpose(1, 2, 0, 3, 4).reshape(b, h, s, dv)

def hierarchical_moe(h, w_rg, b_rg, w_re, b_re, w_gate, w_up, w_down):
    t = h.shape[0]
    p_group = jax.nn.softmax((h @ w_rg + b_rg).astype(jnp.float32), axis=-1)
    p_g_top, g_idx = lax.top_k(p_group, 1)
    lg_exp = (h @ w_re + b_re).astype(jnp.float32).reshape(t, N_GROUPS, EXPERTS_PER_GROUP)
    lg_sel = jnp.take_along_axis(lg_exp, g_idx[:, :, None], axis=1)[:, 0]
    p_exp = jax.nn.softmax(lg_sel, axis=-1)
    p_e_top, e_idx = lax.top_k(p_exp, TOP_K_INNER)
    p_e_top = p_e_top / jnp.sum(p_e_top, axis=-1, keepdims=True)
    w_inner = jnp.sum(jax.nn.one_hot(e_idx, EXPERTS_PER_GROUP, dtype=jnp.float32) * p_e_top[..., None], axis=1)
    gate = (jax.nn.one_hot(g_idx[:, 0], N_GROUPS, dtype=jnp.float32)[:, :, None]
            * (p_g_top[:, 0, None, None] * w_inner[:, None, :])).astype(h.dtype)
    out = jnp.zeros_like(h)
    for g in range(N_GROUPS):
        a = jnp.einsum('td,edf->tef', h, w_gate[g])
        u = jnp.einsum('td,edf->tef', h, w_up[g])
        hid = jax.nn.silu(a) * u * gate[:, g, :, None]
        out = out + jnp.einsum('tef,efd->td', hid, w_down[g])
    return out

def setup_inputs(seed: int = 0) -> dict:
    key = jax.random.key(seed)
    ks = jax.random.split(key, 26)
    f32 = jnp.float32
    L, D, d = DEPTH, D_MODEL, HEAD_DIM
    G, E, F = N_GROUPS, EXPERTS_PER_GROUP, EXPERT_FF

    def nrm(k, shape, scale):
        return jax.random.normal(k, shape, f32) * scale

    def gain(k, shape):
        return 1.0 + 0.05 * jax.random.normal(k, shape, f32)

    return {
        "x": jax.random.normal(ks[0], (BATCH, SEQ, D), f32),
        "positions": jnp.broadcast_to(jnp.arange(SEQ, dtype=jnp.int32), (BATCH, SEQ)),
        "ln1_g": gain(ks[1], (L, D)),
        "w_in": nrm(ks[2], (L, D, IN_COLS), D ** -0.5),
        "b_forget": 2.0 + 0.5 * jax.random.normal(ks[3], (L, FOX_HEADS), f32),
        "q_norm_diff_g": gain(ks[4], (L, d)),
        "k_norm_diff_g": gain(ks[5], (L, d)),
        "lam_q1": nrm(ks[6], (L, d), 0.1),
        "lam_k1": nrm(ks[7], (L, d), 0.1),
        "lam_q2": nrm(ks[8], (L, d), 0.1),
        "lam_k2": nrm(ks[9], (L, d), 0.1),
        "subln_g": gain(ks[10], (L, 2 * d)),
        "q_norm_fox_g": gain(ks[11], (L, d)),
        "k_norm_fox_g": gain(ks[12], (L, d)),
        "w_diff_out": nrm(ks[13], (L, DIFF_V_WIDTH, D), DIFF_V_WIDTH ** -0.5),
        "w_fox_out": nrm(ks[14], (L, FOX_WIDTH, D), FOX_WIDTH ** -0.5),
        "w_o": nrm(ks[15], (L, D, D), D ** -0.5),
        "ln2_g": gain(ks[16], (L, D)),
        "w_router_group": nrm(ks[17], (L, D, G), D ** -0.5),
        "b_router_group": nrm(ks[18], (L, G), 0.01),
        "w_router_expert": nrm(ks[19], (L, D, G * E), D ** -0.5),
        "b_router_expert": nrm(ks[20], (L, G * E), 0.01),
        "w_exp_gate": nrm(ks[21], (L, G, E, D, F), D ** -0.5),
        "w_exp_up": nrm(ks[22], (L, G, E, D, F), D ** -0.5),
        "w_exp_down": nrm(ks[23], (L, G, E, F, D), F ** -0.5),
    }

def reference(x, positions, ln1_g, w_in, b_forget, q_norm_diff_g, k_norm_diff_g, lam_q1, lam_k1, lam_q2, lam_k2,
              subln_g, q_norm_fox_g, k_norm_fox_g, w_diff_out, w_fox_out, w_o, ln2_g, w_router_group,
              b_router_group, w_router_expert, b_router_expert, w_exp_gate, w_exp_up, w_exp_down):
    b, s, dm = x.shape
    cos, sin = rotary_tables(positions, x.dtype)
    split_points = [int(v) for v in np.cumsum(SPLIT_SIZES)[:-1]]
    for l in range(DEPTH):
        lambda_init = 0.8 - 0.6 * math.exp(-0.3 * l)
        h = rms_norm(x, ln1_g[l])
        proj = h @ w_in[l]
        qa, ka, va, qf, kf, vf, fz, gz = jnp.split(proj, split_points, axis=-1)

        qa = partial_rotary(rms_norm(split_heads(qa, 2 * DIFF_HEADS), q_norm_diff_g[l]), cos, sin)
        ka = partial_rotary(rms_norm(split_heads(ka, 2 * DIFF_HEADS), k_norm_diff_g[l]), cos, sin)
        va = split_heads(va, DIFF_HEADS)
        oa = causal_block_attention(qa, ka, jnp.concatenate([va, va], axis=1))
        lam = (jnp.exp(jnp.sum(lam_q1[l].astype(jnp.float32) * lam_k1[l].astype(jnp.float32)))
               - jnp.exp(jnp.sum(lam_q2[l].astype(jnp.float32) * lam_k2[l].astype(jnp.float32)))
               + lambda_init)
        oa = oa[:, :DIFF_HEADS] - lam.astype(oa.dtype) * oa[:, DIFF_HEADS:]
        oa = rms_norm(oa, subln_g[l]) * (1.0 - lambda_init)
        ya = merge_heads(oa) @ w_diff_out[l]

        qf = rms_norm(split_heads(qf, FOX_HEADS), q_norm_fox_g[l])
        kf = rms_norm(split_heads(kf, FOX_HEADS), k_norm_fox_g[l])
        vf = split_heads(vf, FOX_HEADS)
        log_f = jax.nn.log_sigmoid(fz.astype(jnp.float32) + b_forget[l].astype(jnp.float32))
        cum = jnp.cumsum(log_f, axis=1).transpose(0, 2, 1)
        of = causal_block_attention(qf, kf, vf, cum, -cum)
        yf = merge_heads(of) @ w_fox_out[l]

        gates = jax.nn.sigmoid(gz.astype(jnp.float32)).astype(x.dtype)
        g_a, g_f = gates[..., :dm], gates[..., dm:]
        x = x + (g_a * ya + g_f * yf) @ w_o[l]

        h2 = rms_norm(x, ln2_g[l]).reshape(b * s, dm)
        y = hierarchical_moe(h2, w_router_group[l], b_router_group[l], w_router_expert[l], b_router_expert[l],
                             w_exp_gate[l], w_exp_up[l], w_exp_down[l])
        x = x + y.reshape(b, s, dm)
    return x


_drawn_inputs = setup_inputs


def setup_inputs(seed=0):
    import zlib

    import numpy as np

    out = dict(_drawn_inputs(seed))
    spreads = {}
    factors = {'lam_q2': 2.729, 'b_router_group': 3.937, 'b_router_expert': 3.041}
    for name, (base, spread) in spreads.items():
        noise = np.random.default_rng([zlib.crc32(name.encode()), seed]).standard_normal(out[name].shape)
        drawn = base * np.exp(spread * noise) if base else spread * noise
        out[name] = __import__('jax').numpy.asarray(drawn.astype(out[name].dtype))
    for name, factor in factors.items():
        out[name] = (out[name] * factor).astype(out[name].dtype)
    return out
```

```python
import math
from contextlib import ExitStack

import numpy as np

import concourse.bass as bass
from concourse import mybir

ALU = mybir.AluOpType
ACT = mybir.ActivationFunctionType
F32 = mybir.dt.float32
I32 = mybir.dt.int32
AX = mybir.AxisListType

P = 128
D = 1024
T = 256
TT = T // P
L = 2
HD = 64
KD = D // P
DIFF = 4
FOX = 8
MAPS = 2 * DIFF + FOX
UNITS = DIFF + FOX
ROT = HD // 4
HALF = ROT // 2
THETA = 500000.0
EPS = 1e-6
G, EG = 4, 8
E = G * EG
FF = 512
KF = FF // P
NP = E // 2
CAP = 64
SCALE = HD ** -0.5
NEG = -1.0e30
SLOTS = 6
CHUNK = 4096
FZ = 6 * 512
AUG = HD + 2

FRONT = 14
SKIP_AT, SKIP = 6, 4
POS = [n if n < SKIP_AT else n + SKIP for n in range(FRONT)]
SLOT_OF = [pos % SLOTS for pos in POS]
FRONT_FILLS = [SLOT_OF.count(s) for s in range(SLOTS)]
LAYER_FILLS = [n + NP for n in FRONT_FILLS]
assert (FRONT + SKIP) % SLOTS == 0

STATS = [TT] + 4 * [TT * 8] + [TT * DIFF] + [TT]
NORM1, QK0, SUBLN, NORM2 = 0, 1, 5, 6


def last_unit(s):
    if s < 0 or s >= MAPS:
        return None
    if s < 2 * DIFF:
        return s // 2 if s % 2 else None
    return DIFF + s - 2 * DIFF


def map_of_unit(u):
    return 2 * u + 1 if u < DIFF else 2 * DIFF + u - DIFF


def lam_init(l):
    return 0.8 - 0.6 * math.exp(-0.3 * l)


def hybrid_trunk(nc, x, positions, ln1_g, w_in, b_forget, q_norm_diff_g, k_norm_diff_g, lam_q1, lam_k1, lam_q2,
                 lam_k2, subln_g, q_norm_fox_g, k_norm_fox_g, w_diff_out, w_fox_out, w_o, ln2_g, w_router_group,
                 b_router_group, w_router_expert, b_router_expert, w_exp_gate, w_exp_up, w_exp_down, out):
    with ExitStack() as ctx:
        def sb(name, shape, dt=F32):
            return ctx.enter_context(nc.sbuf_tensor(name, shape, dt))

        def sem(name):
            return ctx.enter_context(nc.semaphore(name))

        ring = sb("ring", [P, SLOTS, CHUNK])
        xr = sb("xr", [P, TT, D])
        hn = sb("hn", [P, TT, D])
        hT = sb("hT", [P, KD, T])
        qkd = sb("qkd", [P, 2 * TT * 8 * HD])
        qkf = sb("qkf", [P, 2 * TT * 8 * AUG])
        qkT = sb("qkT", [P, (4 + 8) * 2 * T])
        val = sb("val", [P, TT, 2 * 512])
        gT = sb("gT", [P, 2 * KD, T])
        pT = sb("pT", [P, 2, 3 * P])
        qk_diff = qkd[:, :].rearrange("p (k t n) -> p k t n", k=2, t=TT)
        qk_fox = qkf[:, :].rearrange("p (k t m a) -> p k t m a", k=2, t=TT, m=8)
        headT = qkd[:, :].rearrange("p (c t) -> p c t", c=8)
        rows = qkf[:, 0:4 * 3 * P].rearrange("p (b n) -> p b n", b=4)
        dT = qkT[:, 0:4 * 2 * T].rearrange("p (b k t) -> p b k t", b=4, k=2)
        fT = qkT[:, 4 * 2 * T:12 * 2 * T].rearrange("p (m k t) -> p m k t", m=8, k=2)
        squares = gT[:, 0:4, :].rearrange("p a b -> p (a b)")
        sub_squares = qkd[:, 0:TT * 512].rearrange("p (t n) -> p t n", t=TT)

        def carve(at, n):
            return qkT[:, at:at + n]
        xg = carve(0, 1024).rearrange("p (c s) -> p c s", c=KD)
        act_gate = carve(1024, FF)
        hid = carve(1536, FF)
        hidT = carve(2048, FF).rearrange("p (f s) -> p f s", f=KF)
        down = carve(2560, D)
        pick = carve(3584, TT * P).rearrange("p (t s) -> p t s", t=TT)
        pick_gate = carve(3840, TT * P).rearrange("p (t s) -> p t s", t=TT)
        spread = carve(4096, T)
        merge = val[:, 0, :].rearrange("p (j b t) -> p j b t", j=2, b=2)
        over_hid = gT[:, 0:4, :]
        over_act = gT[:, 4:8, :]

        ident = sb("ident", [P, P])
        tri = sb("tri", [P, P])
        tri_strict = sb("tri_strict", [P, P])
        ones = sb("ones", [P, P])
        mask = sb("mask", [P, 3 * P])
        slot_no = sb("slot_no", [P, CAP])
        rank_w = sb("rank_w", [P, EG])
        minus_half = sb("minus_half", [P, 16])
        eps = sb("eps", [P, 16])
        stage = sb("stage", [2 * L * KD + L, P])
        gains = sb("gains", [P, 2 * L * KD + L])
        qk_gain = sb("qk_gain", [P, 4, L, HD])
        lam_v = sb("lam_v", [P, 4, L, HD])
        lam_p = sb("lam_p", [P, 2, L, HD])
        lam_s = sb("lam_s", [P, 2, L])
        neg_lam = sb("neg_lam", [P, L])
        sub_gain = sb("sub_gain", [P, L])
        sub_gain_now = sb("sub_gain_now", [P, 1])
        bf = sb("bf", [P, L, FOX])
        br = sb("br", [P, L, G + E])
        w_route = sb("w_route", [P, L, KD, G + E])
        w_fz = sb("w_fz", [P, L, KD, FOX])
        pos_i = sb("pos_i", [P, TT], I32)
        pos_f = sb("pos_f", [P, TT])
        freq = sb("freq", [P, HALF])
        angle = sb("angle", [P, 2, TT, HALF])
        turns = sb("turns", [P, 2, TT, HALF])
        sincos = sb("sincos", [P, 2, TT, HALF])
        rot = sb("rot", [P, 4, TT, 8, HALF])
        meansq = sb("meansq", [P, 7, 16])
        meansq_eps = sb("meansq_eps", [P, 7, 16])
        rstd = sb("rstd", [P, 7, 16])
        fz_z = sb("fz_z", [P, TT, FOX])
        fz_n = sb("fz_n", [P, TT, FOX])
        fz_e = sb("fz_e", [P, TT, FOX])
        log_f = sb("log_f", [P, TT, FOX])
        neg_max = sb("neg_max", [P, MAPS, 2])
        row_sum = sb("row_sum", [P, MAPS, 2])
        row_inv = sb("row_inv", [P, MAPS, 2])
        lg = sb("lg", [P, TT, G + E])
        r1 = sb("r1", [P, TT, 4])
        pg = sb("pg", [P, TT, G])
        ohg = sb("ohg", [P, TT, G])
        pe_ = sb("pe_", [P, TT, EG])
        oh1 = sb("oh1", [P, TT, EG])
        oh2 = sb("oh2", [P, TT, EG])
        rk = sb("rk", [P, TT, EG])
        gsel = sb("gsel", [P, TT, EG, G])
        chosen = sb("chosen", [P, TT, G, EG])
        gate = sb("gate", [P, TT, E])
        gate_over = sb("gate_over", [P, TT, E])
        place = sb("place", [P, TT, E])
        cnt = sb("cnt", [P, 1])
        flags = sb("flags", [1, 2], I32)
        flag_f = sb("flag_f", [1, 3])

        ps = ctx.enter_context(nc.psum_tensor("ps", [P, 8, 512], F32))

        slot_full = [sem(f"slot_full{i}") for i in range(SLOTS)]
        x_loaded, params_loaded = sem("x_loaded"), sem("params_loaded")
        consts_made, gains_psum, gains_sb = sem("consts_made"), sem("gains_psum"), sem("gains_sb")
        lam_sums, lam_exp, angles_ready, sincos_ready = sem("lam_sums"), sem("lam_exp"), sem("angles_ready"), sem("sincos_ready")
        meansq_ready, rstd_ready = sem("meansq_ready"), sem("rstd_ready")
        hn_ready, hT_psum, hT_act, hT_dve = sem("hn_ready"), sem("hT_psum"), sem("hT_act"), sem("hT_dve")
        fz_psum, fz_bent, fz_ln, logf_ready = sem("fz_psum"), sem("fz_bent"), sem("fz_ln"), sem("logf_ready")
        cum_psum = sem("cum_psum")
        tok_psum, tok_sb, qk_ready = sem("tok_psum"), sem("tok_sb"), sem("qk_ready")
        qkT_psum, dT_sb, fT_sb = sem("qkT_psum"), sem("dT_sb"), sem("fT_sb")
        s_psum, max_ready, exp_done, p_ready = sem("s_psum"), sem("max_ready"), sem("exp_done"), sem("p_ready")
        pT_psum, pT_sb, pv_psum, pv_sb = sem("pT_psum"), sem("pT_sb"), sem("pv_psum"), sem("pv_sb")
        subln_ready = sem("subln_ready")
        gz_psum, gz_sb = sem("gz_psum"), sem("gz_sb")
        headT_psum, headT_sb = sem("headT_psum"), sem("headT_sb")
        y_psum, merged, wo_psum = sem("y_psum"), sem("merged"), sem("wo_psum")
        logits_psum, centred, route_exp, chosen_ready, pos_psum = sem("logits_psum"), sem("centred"), sem("route_exp"), sem("chosen_ready"), sem("pos_psum")
        pick_ready, gather_psum, gather_sb = sem("pick_ready"), sem("gather_psum"), sem("gather_sb")
        gu_psum, silu_done, hid_ready = sem("gu_psum"), sem("silu_done"), sem("hid_ready")
        down_psum, down_sb = sem("down_psum"), sem("down_sb")
        hidT_psum, hidT_sb = sem("hidT_psum"), sem("hidT_sb")
        pg_ready, spread_psum, spread_sb = sem("pg_ready"), sem("spread_psum"), sem("spread_sb")
        comb_psum, comb_added = sem("comb_psum"), sem("comb_added")
        ov_loaded, ov_gu, ov_silu, ov_hid, ov_down, ov_added = (sem("ov_loaded"), sem("ov_gu"), sem("ov_silu"),
                                                               sem("ov_hid"), sem("ov_down"), sem("ov_added"))
        ov_passed = sem("ov_passed")
        x_final, out_stored = sem("x_final"), sem("out_stored")

        N_PARAMS = 20

        def slot(pos):
            return ring[:, pos % SLOTS, :]

        def front_full(l, n):
            s = SLOT_OF[n]
            return slot_full[s], (l * LAYER_FILLS[s] + SLOT_OF[:n + 1].count(s)) * 16

        def pair_full(l, p, i):
            return slot_full[i], (l * LAYER_FILLS[i] + p + (FRONT_FILLS[i] + 1)) * 16

        def by_k(n):
            return ring[:, n, :].rearrange("p (c n) -> p c n", c=KD)

        def by_f(n):
            return ring[:, n, :].rearrange("p (c n) -> p c n", c=KF)

        def front_used(l, n):
            if n < 6:
                return tok_psum, l * 12 + (2 * n + 2)
            if n < 10:
                return gz_psum, l * 16 + 4 * (n - 5)
            if n < 12:
                return y_psum, l * KD + KD
            return wo_psum, l * 4 + 2 * (n - 11)

        def pair_used(r, i):
            return (gu_psum, 2 * r + (i // 2 + 1)) if i < 4 else (down_psum, 2 * r + 2)

        def of_layer(w, l):
            return w[bass.ds(l, 1)]

        block = ctx.enter_context(nc.Block())

        @block.sync
        def _(sp):
            cols = [0, 512, 3 * 512, 4 * 512, 2 * 512, 5 * 512] + [FZ + FOX + 512 * j for j in range(4)]

            def front(l, first):
                for n in range(FRONT):
                    held = [m for m in range(n) if SLOT_OF[m] == SLOT_OF[n]]
                    if held:
                        sp.wait_ge(*front_used(l, held[-1]))
                    elif not first:
                        sp.wait_ge(*pair_used(l * NP - 1, SLOT_OF[n]))
                    dst = by_k(SLOT_OF[n])
                    if n < 10:
                        src = of_layer(w_in, l)[:, :, cols[n]:cols[n] + 512].rearrange("a (c p) n -> p (a c) n", p=P)
                    elif n < 12:
                        dst = by_f(SLOT_OF[n])
                        src = of_layer([w_diff_out, w_fox_out][n - 10], l).rearrange("a (c p) n -> p (a c) n", p=P)
                    else:
                        h = 512 * (n - 12)
                        src = of_layer(w_o, l)[:, :, h:h + 512].rearrange("a (c p) n -> p (a c) n", p=P)
                    sp.dma_start(dst, src).then_inc(slot_full[SLOT_OF[n]], 16)

            def experts(l):
                def pair_chunk(p, i):
                    w = [w_exp_gate, w_exp_up, w_exp_down][i // 2]
                    src = w[bass.ds(l * E + 2 * p + i % 2, 1)].rearrange("a (c p) n -> p (a c) n", p=P)
                    sp.dma_start(by_k(i) if i < 4 else by_f(i), src).then_inc(slot_full[i], 16)

                for i in range(6):
                    held = [m for m in range(FRONT) if SLOT_OF[m] == i]
                    sp.wait_ge(*front_used(l, held[-1]))
                    pair_chunk(0, i)
                with sp.Fori(1, NP) as p:
                    for i in range(6):
                        sp.wait_ge(*pair_used(l * NP + p - 1, i))
                        pair_chunk(p, i)
                most = sp.value_load(flags[0:1, 0:1], min_val=0, max_val=T)
                before = sp.value_load(flags[0:1, 1:2], min_val=0, max_val=L)
                with sp.If(most > CAP):
                    def load(e):
                        for i in range(3):
                            w = [w_exp_gate, w_exp_up, w_exp_down][i]
                            src = w[bass.ds(l * E + e, 1)].rearrange("a (c p) n -> p (a c) n", p=P)
                            sp.dma_start(by_k(i) if i < 2 else by_f(i), src).then_inc(ov_loaded, 16)

                    sp.wait_ge(down_psum, l * (2 * NP) + 2 * NP)
                    load(0)
                    with sp.Fori(1, E) as e:
                        sp.wait_ge(ov_down, before * (4 * E) + 4 * e)
                        load(e)
                    sp.wait_ge(ov_down, before * (4 * E) + 4 * E)
                    sp.sem_inc(ov_passed, 1)

            front(0, True)
            with sp.Fori(0, L - 1) as l:
                experts(l)
                front(l + 1, False)
            experts(L - 1)
            sp.wait_ge(x_final, 1)
            sp.dma_start(out.rearrange("b (t p) d -> p (b t) d", p=P), xr[:, :, :]).then_inc(out_stored, 16)
            sp.wait_ge(out_stored, 16)

        @block.gpsimd
        def _(pool):
            pool.memset(ident[:, :], 0.0)
            pool.memset(tri[:, :], 1.0)
            pool.memset(tri_strict[:, :], 1.0)
            pool.memset(ones[:, :], 1.0)
            pool.memset(mask[:, :], 0.0)
            pool.memset(minus_half[:, :], -0.5)
            pool.memset(eps[:, :], EPS)
            for j in range(HALF):
                pool.memset(freq[:, j:j + 1], float(np.float32(THETA) ** np.float32(-2.0 * j / ROT)))
            pool.iota(slot_no[:, :], [[1, CAP]], 0, 0, allow_small_or_imprecise_dtypes=True)
            pool.iota(rank_w[:, :], [[-1, EG]], EG, 0, allow_small_or_imprecise_dtypes=True)
            pool.drain()
            pool.affine_select(out=ident[:, :], in_=ident[:, :], compare_op=ALU.not_equal, fill=1.0, base=0,
                               pattern=[[-1, P]], channel_multiplier=1)
            pool.affine_select(out=tri[:, :], in_=tri[:, :], compare_op=ALU.is_ge, fill=0.0, base=0,
                               pattern=[[1, P]], channel_multiplier=-1)
            pool.affine_select(out=tri_strict[:, :], in_=tri_strict[:, :], compare_op=ALU.is_gt, fill=0.0, base=0,
                               pattern=[[1, P]], channel_multiplier=-1)
            for at in (0, 2 * P):
                last = pool.affine_select(out=mask[:, at:at + P], in_=mask[:, at:at + P], compare_op=ALU.is_ge,
                                          fill=NEG, base=0, pattern=[[-1, P]], channel_multiplier=1)
            last.then_inc(consts_made, 1)
            pool.drain()
            with pool.Fori(0, L) as l:
                for k, n in enumerate(STATS):
                    pool.wait_ge(meansq_ready, l * len(STATS) + k + 1)
                    pool.tensor_tensor(meansq_eps[:, k, 0:n], meansq[:, k, 0:n], eps[:, 0:n], ALU.add)
                    pool.drain()
                    pool.tensor_tensor(rstd[:, k, 0:n], meansq_eps[:, k, 0:n], minus_half[:, 0:n],
                                       ALU.pow).then_inc(rstd_ready, 1)

        @block.scalar
        def _(act):
            act.dma_start(xr[:, :, :], x.rearrange("b (t p) d -> p (b t) d", p=P)).then_inc(x_loaded, 16)

            def param(dst, src):
                act.dma_start(dst, src).then_inc(params_loaded, 16)

            def to_all(a):
                flat = a.rearrange("l n -> (l n)").unsqueeze(0)
                return flat.broadcast_to([P, flat.shape[1]]).rearrange("p (l n) -> p l n", l=L)

            param(stage[0:L * KD, :], ln1_g.rearrange("l (c p) -> (l c) p", p=P))
            param(stage[L * KD:2 * L * KD, :], ln2_g.rearrange("l (c p) -> (l c) p", p=P))
            param(stage[2 * L * KD:2 * L * KD + L, :], subln_g)
            param(w_fz[:, 0, :, :], w_in[0, :, FZ:FZ + FOX].rearrange("(c p) n -> p c n", p=P))
            param(w_fz[:, 1, :, :], w_in[1, :, FZ:FZ + FOX].rearrange("(c p) n -> p c n", p=P))
            param(bf[:, :, :], to_all(b_forget))
            for i, g in enumerate((q_norm_diff_g, k_norm_diff_g, q_norm_fox_g, k_norm_fox_g)):
                param(qk_gain[:, i, :, :], to_all(g))
            for t in range(TT):
                param(pos_i[:, t:t + 1], positions[:, P * t:P * (t + 1)].rearrange("b p -> p b"))
            for i, g in enumerate((lam_q1, lam_k1, lam_q2, lam_k2)):
                param(lam_v[:, i, :, :], to_all(g))
            param(br[:, :, 0:G], to_all(b_router_group))
            param(br[:, :, G:G + E], to_all(b_router_expert))
            param(w_route[:, :, :, 0:G].rearrange("p l c n -> p (l c) n"), w_router_group.rearrange("l (c p) n -> p (l c) n", p=P))
            param(w_route[:, :, :, G:G + E].rearrange("p l c n -> p (l c) n"), w_router_expert.rearrange("l (c p) n -> p (l c) n", p=P))

            act.wait_ge(gains_psum, 1)
            act.activation(gains[:, :], ps[:, 0, 0:2 * L * KD + L], ACT.Copy).then_inc(gains_sb, 1)
            act.wait_ge(angles_ready, 1)
            act.activation(sincos[:, :, :, :], angle[:, :, :, :], ACT.Sin).then_inc(sincos_ready, 1)
            act.wait_ge(lam_sums, 1)
            act.activation(lam_s[:, :, :], lam_s[:, :, :], ACT.Exp).then_inc(lam_exp, 1)
            act.drain()

            with act.Fori(0, L) as l:
                def evac_hT(norm, col0):
                    for b in range(2):
                        act.wait_ge(hT_psum, l * 8 + 4 * norm + b + 1)
                        for c in (2 * b, 2 * b + 1):
                            last = act.activation(hT[:, c, :], ps[:, b, (c % 2) * T:(c % 2 + 1) * T], ACT.Copy,
                                                  scale=gains[:, bass.ds(l * KD + (col0 + c), 1)])
                        last.then_inc(hT_act, 1)

                evac_hT(0, 0)
                act.wait_ge(fz_bent, l + 1)
                act.activation(fz_e[:, :, :], fz_n[:, :, :], ACT.Exp)
                act.drain()
                act.activation(fz_e[:, :, :], fz_e[:, :, :], ACT.Ln, bias=1.0).then_inc(fz_ln, 1)
                for j in range(6):
                    for t in range(TT):
                        act.wait_ge(tok_psum, l * 12 + 2 * j + t + 1)
                        src = ps[:, t, :]
                        if j < 2:
                            dst = qk_diff[:, j, t, :]
                        elif j < 4:
                            dst, src = qk_fox[:, j - 2, t, :, 0:HD], src.rearrange("p (m d) -> p m d", m=8)
                        else:
                            dst = val[:, t, 512 * (j - 4):512 * (j - 3)]
                        act.activation(dst, src, ACT.Copy).then_inc(tok_sb, 1)
                for m in range(FOX):
                    act.wait_ge(qkT_psum, l * 12 + 4 + m + 1)
                    act.activation(fT[0:AUG, m, :, :].rearrange("p k t -> p (k t)"), ps[0:AUG, 4 + m % 4, :],
                                   ACT.Copy).then_inc(fT_sb, 1)
                for s in range(MAPS + 2):
                    if s < MAPS:
                        buf = rows[:, s % 4, :]
                        act.wait_ge(max_ready, l * MAPS + s + 1)
                        act.activation(buf[:, 0:P], buf[:, 0:P], ACT.Exp, bias=neg_max[:, s, 0:1],
                                       accum_out=row_sum[:, s, 0:1])
                        act.activation(buf[:, P:3 * P], buf[:, P:3 * P], ACT.Exp, bias=neg_max[:, s, 1:2],
                                       accum_out=row_sum[:, s, 1:2]).then_inc(exp_done, 1)
                        act.wait_ge(gz_psum, l * 16 + s + 1)
                        act.activation(gT[:, s, :], ps[:, s % 2, 0:T], ACT.Tanh, scale=0.5).then_inc(gz_sb, 1)
                    u = last_unit(s - 1)
                    if u is not None:
                        act.wait_ge(pT_psum, l * UNITS + u + 1)
                        if u >= 2:
                            act.wait_ge(pv_psum, l * UNITS + u - 1)
                        act.activation(pT[:, u % 2, :], ps[:, 4 + u % 2, 0:3 * P], ACT.Copy).then_inc(pT_sb, 1)
                for b in range(4):
                    act.wait_ge(headT_psum, l * 4 + b + 1)
                    src, dst = ps[:, 2 + b, :], headT[:, 2 * b:2 * b + 2, :].rearrange("p c t -> p (c t)")
                    if b < 2:
                        act.activation(dst, src, ACT.Copy, scale=sub_gain_now[:, :]).then_inc(headT_sb, 1)
                    else:
                        act.activation(dst, src, ACT.Copy).then_inc(headT_sb, 1)
                evac_hT(1, L * KD)
                act.wait_ge(centred, l + 1)
                act.activation(pg[:, :, :], pg[:, :, :], ACT.Exp)
                act.activation(pe_[:, :, :], pe_[:, :, :], ACT.Exp).then_inc(route_exp, 1)

                def pair(r):
                    act.wait_ge(gu_psum, 2 * r + 1)
                    act.activation(act_gate, ps[:, 2, :], ACT.Silu).then_inc(silu_done, 1)
                    act.wait_ge(hidT_psum, r + 1)
                    act.activation(hidT.rearrange("p f s -> p (f s)"), ps[:, 2, :], ACT.Copy).then_inc(hidT_sb, 1)
                    for h in range(2):
                        act.wait_ge(down_psum, 2 * r + (h + 1))
                        act.activation(down[:, 512 * h:512 * (h + 1)], ps[:, 4 + h, :], ACT.Copy).then_inc(down_sb, 1)

                with act.Fori(0, NP) as p:
                    pair(l * NP + p)

                most = act.value_load(flags[0:1, 0:1], min_val=0, max_val=T)
                before = act.value_load(flags[0:1, 1:2], min_val=0, max_val=L)
                with act.If(most > CAP):
                    with act.Fori(0, E) as e:
                        for f in range(KF):
                            act.wait_ge(ov_gu, before * (4 * E) + 4 * e + (f + 1))
                            act.activation(over_act[:, f, :], ps[:, f, 0:T], ACT.Silu).then_inc(ov_silu, 1)

        @block.vector
        def _(dve):
            done = dve.drain

            dve.memset(flag_f[:, :], 0.0)
            dve.wait_ge(consts_made, 1)
            dve.wait_ge(params_loaded, 16 * N_PARAMS)
            dve.tensor_copy(pos_f[:, :], pos_i[:, :])
            done()
            for t in range(TT):
                dve.tensor_scalar(angle[:, 0, t, :], freq[:, :], pos_f[:, t:t + 1], None, ALU.mult)
            done()
            big = 12582912.0
            dve.tensor_scalar(turns[:, 0, :, :], angle[:, 0, :, :], 1.0 / (2 * math.pi), big, ALU.mult, ALU.add)
            dve.tensor_scalar(turns[:, 1, :, :], angle[:, 0, :, :], 1.0 / (2 * math.pi), 0.25, ALU.mult, ALU.add)
            done()
            dve.tensor_scalar(turns[:, 1, :, :], turns[:, 1, :, :], big, None, ALU.add)
            done()
            dve.tensor_scalar(turns[:, :, :, :], turns[:, :, :, :], -big, None, ALU.add)
            dve.tensor_copy(angle[:, 1, :, :], angle[:, 0, :, :])
            done()
            parts, rest = [], 2 * math.pi
            for step in (2.0 ** -5, 2.0 ** -16):
                parts.append(math.floor(rest / step) * step)
                rest -= parts[-1]
            parts.append(float(np.float32(rest)))
            for part in parts:
                dve.scalar_tensor_tensor(out=angle[:, :, :, :].rearrange("p a t j -> p (a t j)"),
                                         in0=turns[:, :, :, :].rearrange("p a t j -> p (a t j)"), scalar=-part,
                                         in1=angle[:, :, :, :].rearrange("p a t j -> p (a t j)"),
                                         op0=ALU.mult, op1=ALU.add)
                done()
            dve.tensor_scalar(angle[:, 1, :, :], angle[:, 1, :, :], math.pi / 2, None, ALU.add)
            done()
            dve.tensor_scalar(angle[:, :, :, :], angle[:, :, :, :], 3.1415925, -3.1415925, ALU.min,
                              ALU.max).then_inc(angles_ready, 1)
            dve.tensor_tensor(lam_p[:, 0, :, :], lam_v[:, 0, :, :], lam_v[:, 1, :, :], ALU.mult)
            dve.tensor_tensor(lam_p[:, 1, :, :], lam_v[:, 2, :, :], lam_v[:, 3, :, :], ALU.mult)
            done()
            dve.tensor_reduce(lam_s[:, :, :], lam_p[:, :, :, :], AX.X, ALU.add).then_inc(lam_sums, 1)
            dve.wait_ge(lam_exp, 1)
            dve.tensor_tensor(neg_lam[:, :], lam_s[:, 1, :], lam_s[:, 0, :], ALU.subtract)
            dve.wait_ge(gains_sb, 1)
            for l in range(L):
                dve.tensor_scalar(sub_gain[:, l:l + 1], gains[:, 2 * L * KD + l:2 * L * KD + l + 1],
                                  1.0 - lam_init(l), None, ALU.mult)
            done()
            for l in range(L):
                dve.tensor_scalar(neg_lam[:, l:l + 1], neg_lam[:, l:l + 1], -lam_init(l), None, ALU.add)
            dve.wait_ge(sincos_ready, 1)
            dve.wait_ge(x_loaded, 16)
            done()

            with dve.Fori(0, L) as l:
                def norm(k):
                    for t in range(TT):
                        last = dve.tensor_tensor_reduce(out=hn[:, t, :], in0=xr[:, t, :], in1=xr[:, t, :], scale=1.0 / D,
                                                        scalar=0.0, op0=ALU.mult, op1=ALU.add,
                                                        accum_out=meansq[:, k, t:t + 1])
                    last.then_inc(meansq_ready, 1)
                    dve.wait_ge(rstd_ready, l * len(STATS) + k + 1)
                    for t in range(TT):
                        dve.tensor_scalar(hn[:, t, :], xr[:, t, :], rstd[:, k, t:t + 1], None,
                                          ALU.mult).then_inc(hn_ready, 1)

                def evac_hT(norm_no, col0):
                    for b in range(2, 4):
                        dve.wait_ge(hT_psum, l * 8 + 4 * norm_no + b + 1)
                        for c in (2 * b, 2 * b + 1):
                            last = dve.tensor_scalar(hT[:, c, :], ps[:, b, (c % 2) * T:(c % 2 + 1) * T],
                                                     gains[:, bass.ds(l * KD + (col0 + c), 1)], None, ALU.mult)
                        last.then_inc(hT_dve, 1)

                dve.tensor_copy(sub_gain_now[:, :], sub_gain[:, bass.ds(l, 1)])
                norm(NORM1)
                evac_hT(0, 0)

                dve.wait_ge(fz_psum, l + 1)
                for t in range(TT):
                    dve.tensor_tensor(fz_z[:, t, :], ps[:, 7, FOX * t:FOX * (t + 1)], bf[:, bass.ds(l, 1), :].rearrange("p a n -> p (a n)"), ALU.add)
                done()
                dve.tensor_scalar(fz_n[:, :, :], fz_z[:, :, :], -1.0, None, ALU.mult)
                done()
                dve.tensor_tensor(fz_n[:, :, :], fz_n[:, :, :], fz_z[:, :, :], ALU.min).then_inc(fz_bent, 1)
                dve.tensor_scalar(fz_z[:, :, :], fz_z[:, :, :], 0.0, None, ALU.min)
                done()
                dve.wait_ge(fz_ln, l + 1)
                dve.tensor_tensor(log_f[:, :, :], fz_z[:, :, :], fz_e[:, :, :], ALU.subtract).then_inc(logf_ready, 1)

                for j in range(4):
                    dve.wait_ge(tok_sb, l * 12 + 2 * j + 2)
                    if j < 2:
                        heads = [qk_diff[:, j, t, :].rearrange("p (m d) -> p m d", m=8) for t in range(TT)]
                    else:
                        heads = [qk_fox[:, j - 2, t, :, 0:HD] for t in range(TT)]
                    sq = squares.rearrange("p (t m d) -> p t m d", t=TT, m=8)
                    for t in range(TT):
                        dve.scalar_tensor_tensor(out=sq[:, t], in0=heads[t], scalar=1.0 / HD, in1=heads[t],
                                                 op0=ALU.mult, op1=ALU.mult)
                    done()
                    k = QK0 + j
                    dve.tensor_reduce(meansq[:, k, :], squares.rearrange("p (m d) -> p m d", d=HD), AX.X,
                                      ALU.add).then_inc(meansq_ready, 1)
                    dve.wait_ge(rstd_ready, l * len(STATS) + k + 1)
                    for t in range(TT):
                        scale = rstd[:, k, 8 * t:8 * (t + 1)].unsqueeze(2).broadcast_to([P, 8, HD])
                        dve.tensor_tensor(heads[t], heads[t], scale, ALU.mult)
                    done()
                    gain = qk_gain[:, j, bass.ds(l, 1), :].broadcast_to([P, 8, HD])
                    for t in range(TT):
                        last = dve.tensor_tensor(heads[t], heads[t], gain, ALU.mult)
                    if j < 2:
                        done()
                        for t in range(TT):
                            sin, cos = [sincos[:, i, t:t + 1, :].broadcast_to([P, 8, HALF]) for i in range(2)]
                            a, b = heads[t][:, :, 0:HALF], heads[t][:, :, HALF:ROT]
                            dve.tensor_tensor(rot[:, 0, t], a, cos, ALU.mult)
                            dve.tensor_tensor(rot[:, 1, t], b, sin, ALU.mult)
                            dve.tensor_tensor(rot[:, 2, t], b, cos, ALU.mult)
                            dve.tensor_tensor(rot[:, 3, t], a, sin, ALU.mult)
                        done()
                        for t in range(TT):
                            a, b = heads[t][:, :, 0:HALF], heads[t][:, :, HALF:ROT]
                            dve.tensor_tensor(a, rot[:, 0, t], rot[:, 1, t], ALU.subtract)
                            last = dve.tensor_tensor(b, rot[:, 2, t], rot[:, 3, t], ALU.add)
                    elif j == 2:
                        dve.wait_ge(cum_psum, l + 1)
                        for t in range(TT):
                            cum = ps[:, 7, 64 + FOX * t:64 + FOX * (t + 1)]
                            dve.tensor_scalar(qk_fox[:, 0, t, :, HD], cum, 1.0 / SCALE, None, ALU.mult)
                            dve.memset(qk_fox[:, 0, t, :, HD + 1], 1.0)
                            dve.memset(qk_fox[:, 1, t, :, HD], 1.0)
                            last = dve.tensor_scalar(qk_fox[:, 1, t, :, HD + 1], cum, -1.0 / SCALE, None, ALU.mult)
                    last.then_inc(qk_ready, 1)
                for b in range(4):
                    dve.wait_ge(qkT_psum, l * 12 + b + 1)
                    dve.tensor_copy(dT[:, b, :, :].rearrange("p k t -> p (k t)"), ps[:, 2 + b, :]).then_inc(dT_sb, 1)

                for s in range(MAPS + 2):
                    if s < MAPS:
                        buf = rows[:, s % 4, :]
                        dve.wait_ge(s_psum, l * MAPS + s + 1)
                        if s >= 4:
                            prev = s - 4 if s - 4 >= 2 * DIFF else 2 * ((s - 4) // 2) + 1
                            dve.wait_ge(pT_psum, l * UNITS + last_unit(prev) + 1)
                        dve.scalar_tensor_tensor(out=buf, in0=ps[:, 2 + s % 2, 0:3 * P], scalar=SCALE,
                                                 in1=mask[:, :], op0=ALU.mult, op1=ALU.add)
                        done()
                        dve.tensor_reduce(neg_max[:, s, 0:1], buf[:, 0:P], AX.X, ALU.max, negate=True)
                        dve.tensor_reduce(neg_max[:, s, 1:2], buf[:, P:3 * P], AX.X, ALU.max,
                                          negate=True).then_inc(max_ready, 1)
                    u = last_unit(s - 1)
                    if u is not None:
                        dve.wait_ge(exp_done, l * MAPS + s)
                        if u < DIFF:
                            m1, m2 = s - 2, s - 1
                            dve.reciprocal(row_inv[:, m1:m2 + 1, :], row_sum[:, m1:m2 + 1, :])
                            done()
                            dve.tensor_scalar(row_inv[:, m2, :], row_inv[:, m2, :], neg_lam[:, bass.ds(l, 1)], None,
                                              ALU.mult)
                            for q, (a, b) in enumerate(((0, P), (P, 3 * P))):
                                dve.tensor_scalar(rows[:, m1 % 4, a:b], rows[:, m1 % 4, a:b],
                                                  row_inv[:, m1, q:q + 1], None, ALU.mult)
                            done()
                            for q, (a, b) in enumerate(((0, P), (P, 3 * P))):
                                last = dve.scalar_tensor_tensor(
                                    out=rows[:, m2 % 4, a:b], in0=rows[:, m2 % 4, a:b], scalar=row_inv[:, m2, q:q + 1],
                                    in1=rows[:, m1 % 4, a:b], op0=ALU.mult, op1=ALU.add)
                            last.then_inc(p_ready, 1)
                        else:
                            dve.reciprocal(row_inv[:, s - 1, :], row_sum[:, s - 1, :])
                    u = last_unit(s - 2)
                    if u is not None:
                        done()
                        dve.wait_ge(pv_psum, l * UNITS + u + 1)
                        if u < DIFF:
                            dve.tensor_copy(hn[:, :, 128 * u:128 * (u + 1)],
                                            ps[:, 6 + u % 2, 0:256].rearrange("p (t d) -> p t d", t=TT)).then_inc(pv_sb, 1)
                        else:
                            m = u - DIFF
                            dve.tensor_tensor(hn[:, :, 512 + HD * m:512 + HD * (m + 1)],
                                              ps[:, 6 + u % 2, 0:128].rearrange("p (t d) -> p t d", t=TT),
                                              row_inv[:, s - 2, :].unsqueeze(2).broadcast_to([P, TT, HD]),
                                              ALU.mult).then_inc(pv_sb, 1)
                    if s == 10:
                        for t in range(TT):
                            dve.scalar_tensor_tensor(out=sub_squares[:, t, :], in0=hn[:, t, 0:512],
                                                     scalar=1.0 / (2 * HD), in1=hn[:, t, 0:512], op0=ALU.mult,
                                                     op1=ALU.mult)
                        done()
                        dve.tensor_reduce(meansq[:, SUBLN, 0:TT * DIFF],
                                          sub_squares.rearrange("p t (h d) -> p (t h) d", h=DIFF), AX.X,
                                          ALU.add).then_inc(meansq_ready, 1)
                    if s == 12:
                        dve.wait_ge(rstd_ready, l * len(STATS) + SUBLN + 1)
                        for t in range(TT):
                            o = hn[:, t, 0:512].rearrange("p (h d) -> p h d", h=DIFF)
                            sc = rstd[:, SUBLN, DIFF * t:DIFF * (t + 1)].unsqueeze(2).broadcast_to([P, DIFF, 2 * HD])
                            last = dve.tensor_tensor(o, o, sc, ALU.mult)
                        last.then_inc(subln_ready, 1)

                for j in range(KD):
                    dve.wait_ge(y_psum, l * KD + j + 1)
                    dve.scalar_tensor_tensor(out=merge[:, j % 2, 0, :], in0=gT[:, j, :], scalar=1.0,
                                             in1=ps[:, j % 2, 0:T], op0=ALU.add, op1=ALU.mult)
                    dve.scalar_tensor_tensor(out=merge[:, j % 2, 1, :], in0=gT[:, KD + j, :], scalar=1.0,
                                             in1=ps[:, j % 2, T:2 * T], op0=ALU.add, op1=ALU.mult)
                    done()
                    dve.tensor_tensor(gT[:, j, :], merge[:, j % 2, 0, :], merge[:, j % 2, 1, :],
                                      ALU.add).then_inc(merged, 1)
                for g in range(4):
                    t, h = g % 2, g // 2
                    dve.wait_ge(wo_psum, l * 4 + g + 1)
                    xh = xr[:, t, 512 * h:512 * (h + 1)]
                    dve.scalar_tensor_tensor(out=xh, in0=ps[:, 4 + g, :], scalar=0.5, in1=xh, op0=ALU.mult,
                                             op1=ALU.add)
                done()

                norm(NORM2)
                evac_hT(1, L * KD)
                dve.wait_ge(logits_psum, l + 1)
                for t in range(TT):
                    dve.tensor_tensor(lg[:, t, :], ps[:, 4, (G + E) * t:(G + E) * (t + 1)],
                                      br[:, bass.ds(l, 1), :].rearrange("p a n -> p (a n)"), ALU.add)
                done()

                def bc(a, n):
                    return a.broadcast_to([P, TT, n])

                def first_of(onehot, score, best, n):
                    dve.tensor_tensor(onehot, score, bc(best, n), ALU.is_equal)
                    done()
                    dve.tensor_tensor(rk[:, :, 0:n], onehot, rank_w[:, 0:n].unsqueeze(1).broadcast_to([P, TT, n]),
                                      ALU.mult)
                    done()
                    dve.tensor_reduce(r1[:, :, 3:4], rk[:, :, 0:n], AX.X, ALU.max)
                    done()
                    dve.tensor_tensor(onehot, rk[:, :, 0:n], bc(r1[:, :, 3:4], n), ALU.is_equal)
                    done()

                dve.tensor_reduce(r1[:, :, 0:1], lg[:, :, 0:G], AX.X, ALU.max)
                done()
                dve.tensor_tensor(pg[:, :, :], lg[:, :, 0:G], bc(r1[:, :, 0:1], G), ALU.subtract)
                first_of(ohg[:, :, :], lg[:, :, 0:G], r1[:, :, 0:1], G)
                for t in range(TT):
                    dve.tensor_tensor(gsel[:, t], lg[:, t, G:G + E].rearrange("p (g e) -> p e g", g=G),
                                      ohg[:, t:t + 1, :].broadcast_to([P, EG, G]), ALU.mult)
                done()
                dve.tensor_reduce(pe_[:, :, :], gsel[:, :, :, :], AX.X, ALU.add)
                done()
                dve.tensor_reduce(r1[:, :, 1:2], pe_[:, :, :], AX.X, ALU.max)
                done()
                dve.tensor_tensor(pe_[:, :, :], pe_[:, :, :], bc(r1[:, :, 1:2], EG), ALU.subtract).then_inc(centred, 1)
                dve.wait_ge(route_exp, l + 1)
                dve.tensor_reduce(r1[:, :, 0:1], pg[:, :, :], AX.X, ALU.add)
                dve.tensor_reduce(r1[:, :, 1:2], pe_[:, :, :], AX.X, ALU.add)
                done()
                dve.reciprocal(r1[:, :, 0:2], r1[:, :, 0:2])
                done()
                dve.tensor_tensor(pe_[:, :, :], pe_[:, :, :], bc(r1[:, :, 1:2], EG), ALU.mult)
                done()
                dve.tensor_reduce(r1[:, :, 2:3], pe_[:, :, :], AX.X, ALU.max)
                done()
                first_of(oh1[:, :, :], pe_[:, :, :], r1[:, :, 2:3], EG)
                dve.scalar_tensor_tensor(out=gsel[:, :, :, 0], in0=oh1[:, :, :], scalar=-2.0, in1=pe_[:, :, :],
                                         op0=ALU.mult, op1=ALU.add)
                done()
                dve.tensor_reduce(r1[:, :, 2:3], gsel[:, :, :, 0], AX.X, ALU.max)
                done()
                first_of(oh2[:, :, :], gsel[:, :, :, 0], r1[:, :, 2:3], EG)
                dve.tensor_tensor(oh1[:, :, :], oh1[:, :, :], oh2[:, :, :], ALU.add)
                done()
                for t in range(TT):
                    last = dve.tensor_tensor(chosen[:, t], ohg[:, t, :].unsqueeze(2).broadcast_to([P, G, EG]),
                                             oh1[:, t:t + 1, :].broadcast_to([P, G, EG]), ALU.mult)
                last.then_inc(chosen_ready, 1)
                dve.tensor_tensor(pe_[:, :, :], pe_[:, :, :], oh1[:, :, :], ALU.mult)
                done()
                dve.tensor_reduce(r1[:, :, 2:3], pe_[:, :, :], AX.X, ALU.add)
                done()
                dve.reciprocal(r1[:, :, 2:3], r1[:, :, 2:3])
                done()
                dve.tensor_tensor(pe_[:, :, :], pe_[:, :, :], bc(r1[:, :, 2:3], EG), ALU.mult)
                done()
                dve.tensor_tensor(pe_[:, :, :], pe_[:, :, :], bc(r1[:, :, 0:1], EG), ALU.mult)
                done()
                for t in range(TT):
                    dve.tensor_tensor(gate[:, t, :].rearrange("p (g e) -> p g e", g=G), chosen[:, t],
                                      pe_[:, t:t + 1, :].broadcast_to([P, G, EG]), ALU.mult)
                dve.wait_ge(pos_psum, l + 1)
                flat = chosen[:, :, :, :].rearrange("p t g e -> p t (g e)")
                dve.scalar_tensor_tensor(out=place[:, :, :], in0=ps[:, 5, 0:TT * E].rearrange("p (t e) -> p t e", t=TT),
                                         scalar=1.0, in1=flat, op0=ALU.add, op1=ALU.mult)
                dve.tensor_reduce(cnt[:, :], ps[:, 5, TT * E:TT * E + E], AX.X, ALU.max)
                done()
                dve.tensor_scalar(place[:, :, :], place[:, :, :], -1.0, None, ALU.add)
                dve.tensor_copy(flag_f[:, 0:1], cnt[0:1, :])
                dve.tensor_scalar(flag_f[:, 2:3], cnt[0:1, :], float(CAP), None, ALU.is_gt)
                done()
                dve.tensor_copy(flags[:, :], flag_f[:, 0:2])
                dve.scalar_tensor_tensor(out=gate_over[:, :, :], in0=place[:, :, :], scalar=float(CAP),
                                         in1=gate[:, :, :], op0=ALU.is_ge, op1=ALU.mult)
                done()
                dve.tensor_tensor(flag_f[:, 1:2], flag_f[:, 1:2], flag_f[:, 2:3], ALU.add)

                def make_pick(p):
                    for t in range(TT):
                        for e in range(2):
                            last = dve.tensor_scalar(pick[:, t, CAP * e:CAP * (e + 1)], slot_no[:, :],
                                                     place[:, t, bass.ds(2 * p + e, 1)], None, ALU.is_equal)
                    last.then_inc(pick_ready, 1)

                def make_pick_gate(p):
                    for t in range(TT):
                        for e in range(2):
                            last = dve.tensor_scalar(pick_gate[:, t, CAP * e:CAP * (e + 1)], slot_no[:, :],
                                                     place[:, t, bass.ds(2 * p + e, 1)],
                                                     gate[:, t, bass.ds(2 * p + e, 1)], ALU.is_equal, ALU.mult)
                    last.then_inc(pg_ready, 1)

                def gathered(r):
                    g2 = gains[:, bass.ds(l * KD + L * KD, KD)].unsqueeze(2).broadcast_to([P, KD, P])
                    for h in range(2):
                        dve.wait_ge(gather_psum, 2 * r + (h + 1))
                        cs = slice(4 * h, 4 * h + 4)
                        dve.tensor_tensor(xg[:, cs, :], ps[:, h, :].rearrange("p (c s) -> p c s", c=4), g2[:, cs, :],
                                          ALU.mult).then_inc(gather_sb, 1)

                def hidden(r):
                    dve.wait_ge(silu_done, r + 1)
                    dve.wait_ge(gu_psum, 2 * r + 2)
                    dve.tensor_tensor(hid, act_gate, ps[:, 3, :], ALU.mult).then_inc(hid_ready, 1)

                def spread_out(r):
                    dve.wait_ge(spread_psum, r + 1)
                    dve.tensor_copy(spread, ps[:, 3, 0:T]).then_inc(spread_sb, 1)

                def add_pair(r):
                    for g in range(4):
                        t, h = g // 2, g % 2
                        dve.wait_ge(comb_psum, 4 * r + (g + 1))
                        xh = xr[:, t, 512 * h:512 * (h + 1)]
                        dve.tensor_tensor(xh, xh, ps[:, 6 + h, :], ALU.add).then_inc(comb_added, 1)

                def pair(p, first, last):
                    r = l * NP + p
                    if not last:
                        make_pick(p + 1)
                    hidden(r)
                    if not first:
                        add_pair(r - 1)
                    spread_out(r)
                    if not last:
                        make_pick_gate(p + 1)
                        gathered(r + 1)

                make_pick(0)
                make_pick_gate(0)
                gathered(l * NP)
                pair(0, True, False)
                with dve.Fori(1, NP - 1) as p:
                    pair(p, False, False)
                pair(NP - 1, False, True)
                add_pair(l * NP + NP - 1)

                most = dve.value_load(flags[0:1, 0:1], min_val=0, max_val=T)
                before = dve.value_load(flags[0:1, 1:2], min_val=0, max_val=L)
                with dve.If(most > CAP):
                    with dve.Fori(0, E) as e:
                        for f in range(KF):
                            dve.wait_ge(ov_silu, before * (4 * E) + 4 * e + (f + 1))
                            dve.tensor_tensor(over_hid[:, f, :], over_act[:, f, :], ps[:, f, T:2 * T],
                                              ALU.mult).then_inc(ov_hid, 1)
                        for g in range(4):
                            t, h = g // 2, g % 2
                            dve.wait_ge(ov_down, before * (4 * E) + 4 * e + (g + 1))
                            xh = xr[:, t, 512 * h:512 * (h + 1)]
                            dve.scalar_tensor_tensor(out=xh, in0=ps[:, 4 + g, :],
                                                     scalar=gate_over[:, t, bass.ds(e, 1)], in1=xh, op0=ALU.mult,
                                                     op1=ALU.add).then_inc(ov_added, 1)
                done()
            dve.drain().then_inc(x_final, 1)

        @block.tensor
        def _(pe):
            mm = nc.tensor.matmul

            def group(out_ap, pairs):
                for i, (a, b) in enumerate(pairs):
                    last = mm(out_ap, a, b, start=(i == 0), stop=(i == len(pairs) - 1))
                return last

            pe.wait_ge(consts_made, 1)
            pe.wait_ge(params_loaded, 16 * N_PARAMS)
            rows_n = 2 * L * KD + L
            nc.tensor.transpose(ps[:, 0, 0:rows_n], stage[:, :], ident[0:rows_n, 0:rows_n]).then_inc(gains_psum, 1)
            pe.wait_ge(gains_sb, 1)

            with pe.Fori(0, L) as l:
                def transposes(norm):
                    pe.wait_ge(hn_ready, l * 4 + 2 * norm + 2)
                    for c in range(KD):
                        for t in range(TT):
                            last = nc.tensor.transpose(ps[:, c // 2, (c % 2) * T + t * P:(c % 2) * T + (t + 1) * P],
                                                       hn[:, t, P * c:P * (c + 1)], ident[:, :])
                        if c % 2:
                            last.then_inc(hT_psum, 1)
                    pe.wait_ge(hT_act, l * 4 + 2 * norm + 2)
                    pe.wait_ge(hT_dve, l * 4 + 2 * norm + 2)

                transposes(0)
                for t in range(TT):
                    last = group(ps[:, 7, FOX * t:FOX * (t + 1)],
                                 [(hT[:, c, P * t:P * (t + 1)], w_fz[:, bass.ds(l, 1), c, :].rearrange("p a n -> p (a n)"))
                                  for c in range(KD)])
                last.then_inc(fz_psum, 1)
                def project(j):
                    pe.wait_ge(*front_full(l, j))
                    w = by_k(SLOT_OF[j])
                    for t in range(TT):
                        if j >= 1:
                            pe.wait_ge(tok_sb, l * 12 + 2 * (j - 1) + t + 1)
                        last = group(ps[:, t, :], [(hT[:, c, P * t:P * (t + 1)], w[:, c, :]) for c in range(KD)])
                        last.then_inc(tok_psum, 1)

                project(0)
                project(1)
                pe.wait_ge(logf_ready, l + 1)
                group(ps[:, 7, 64:64 + FOX], [(tri[:, :], log_f[:, 0, :])])
                group(ps[:, 7, 64 + FOX:64 + 2 * FOX],
                      [(ones[:, :], log_f[:, 0, :]), (tri[:, :], log_f[:, 1, :])]).then_inc(cum_psum, 1)
                project(2)
                project(3)
                project(4)
                pe.wait_ge(qk_ready, l * 4 + 2)
                for b in range(4):
                    for k in range(2):
                        for t in range(TT):
                            last = nc.tensor.transpose(ps[:, 2 + b, T * k + P * t:T * k + P * (t + 1)],
                                                       qk_diff[:, k, t, P * b:P * (b + 1)], ident[:, :])
                    last.then_inc(qkT_psum, 1)
                project(5)
                pe.wait_ge(qk_ready, l * 4 + 4)
                pe.wait_ge(dT_sb, l * 4 + 4)
                for m in range(FOX):
                    if m >= 4:
                        pe.wait_ge(fT_sb, l * FOX + m - 3)
                    for k in range(2):
                        for t in range(TT):
                            last = nc.tensor.transpose(ps[0:AUG, 4 + m % 4, T * k + P * t:T * k + P * (t + 1)],
                                                       qk_fox[:, k, t, m, :], ident[:, :])
                    last.then_inc(qkT_psum, 1)

                for s in range(MAPS + 2):
                    if s < MAPS:
                        if s < 2 * DIFF:
                            m = s // 2 + DIFF * (s % 2)
                            half = slice(HD * (m % 2), HD * (m % 2 + 1))
                            q, k = dT[half, m // 2, 0, :], dT[half, m // 2, 1, :]
                        else:
                            q, k = fT[0:AUG, s - 2 * DIFF, 0, :], fT[0:AUG, s - 2 * DIFF, 1, :]
                        if s >= 2:
                            pe.wait_ge(max_ready, l * MAPS + s - 1)
                        if s == 2 * DIFF:
                            pe.wait_ge(fT_sb, l * FOX + FOX)
                        group(ps[:, 2 + s % 2, 0:P], [(q[:, 0:P], k[:, 0:P])])
                        group(ps[:, 2 + s % 2, P:3 * P], [(q[:, P:T], k)]).then_inc(s_psum, 1)
                        n = 6 + s // 4
                        if s % 4 == 0:
                            pe.wait_ge(*front_full(l, n))
                        if s >= 2:
                            pe.wait_ge(gz_sb, l * 16 + s - 1)
                        else:
                            pe.wait_ge(tok_sb, l * 12 + 11 + s)
                        w = by_k(SLOT_OF[n])
                        last = group(ps[:, s % 2, 0:T], [(w[:, c, P * (s % 4):P * (s % 4 + 1)], hT[:, c, :])
                                                         for c in range(KD)])
                        last.then_inc(gz_psum, 1)
                    u = last_unit(s - 1)
                    if u is not None:
                        if u < DIFF:
                            pe.wait_ge(p_ready, l * DIFF + u + 1)
                            if u == 0:
                                pe.wait_ge(fT_sb, l * FOX + FOX)
                        else:
                            pe.wait_ge(exp_done, l * MAPS + s)
                        for i in range(3):
                            last = nc.tensor.transpose(ps[:, 4 + u % 2, P * i:P * (i + 1)],
                                                       rows[:, (s - 1) % 4, P * i:P * (i + 1)], ident[:, :])
                        last.then_inc(pT_psum, 1)
                    u = last_unit(s - 2)
                    if u is not None:
                        pe.wait_ge(pT_sb, l * UNITS + u + 1)
                        if u >= 2:
                            pe.wait_ge(pv_sb, l * UNITS + u - 1)
                        v0, dv = (2 * HD * u, 2 * HD) if u < DIFF else (512 + HD * (u - DIFF), HD)
                        b = pT[:, u % 2, :]
                        group(ps[:, 6 + u % 2, 0:dv], [(b[:, 0:P], val[:, 0, v0:v0 + dv])])
                        group(ps[:, 6 + u % 2, dv:2 * dv], [(b[:, P:2 * P], val[:, 0, v0:v0 + dv]),
                                                           (b[:, 2 * P:3 * P], val[:, 1, v0:v0 + dv])]).then_inc(pv_psum, 1)
                for b in range(4):
                    if b == 0:
                        pe.wait_ge(subln_ready, l + 1)
                    if b == 2:
                        pe.wait_ge(pv_sb, l * UNITS + UNITS)
                    for c in (2 * b, 2 * b + 1):
                        for t in range(TT):
                            last = nc.tensor.transpose(ps[:, 2 + b, (c % 2) * T + P * t:(c % 2) * T + P * (t + 1)],
                                                       hn[:, t, P * c:P * (c + 1)], ident[:, :])
                    last.then_inc(headT_psum, 1)
                pe.wait_ge(headT_sb, l * 4 + 4)
                pe.wait_ge(gz_sb, l * 16 + 16)
                pe.wait_ge(*front_full(l, 10))
                pe.wait_ge(*front_full(l, 11))
                wd, wf = by_f(SLOT_OF[10]), by_f(SLOT_OF[11])
                for j in range(KD):
                    if j >= 2:
                        pe.wait_ge(merged, l * KD + j - 1)
                    group(ps[:, j % 2, 0:T], [(wd[:, c, P * j:P * (j + 1)], headT[:, c, :]) for c in range(4)])
                    last = group(ps[:, j % 2, T:2 * T], [(wf[:, c, P * j:P * (j + 1)], headT[:, 4 + c, :])
                                                         for c in range(4)])
                    last.then_inc(y_psum, 1)
                for g in range(4):
                    t, h = g % 2, g // 2
                    if t == 0:
                        pe.wait_ge(*front_full(l, 12 + h))
                        pe.wait_ge(merged, l * KD + KD)
                    w = by_k(SLOT_OF[12 + h])
                    last = group(ps[:, 4 + g, :], [(gT[:, c, P * t:P * (t + 1)], w[:, c, :]) for c in range(KD)])
                    last.then_inc(wo_psum, 1)
                transposes(1)
                for t in range(TT):
                    last = group(ps[:, 4, (G + E) * t:(G + E) * (t + 1)],
                                 [(hT[:, c, P * t:P * (t + 1)],
                                   w_route[:, bass.ds(l, 1), c, :].rearrange("p a n -> p (a n)")) for c in range(KD)])
                last.then_inc(logits_psum, 1)
                pe.wait_ge(chosen_ready, l + 1)
                ch = [chosen[:, t].rearrange("p g e -> p (g e)") for t in range(TT)]
                group(ps[:, 5, 0:E], [(tri_strict[:, :], ch[0])])
                group(ps[:, 5, E:2 * E], [(ones[:, :], ch[0]), (tri_strict[:, :], ch[1])])
                group(ps[:, 5, 2 * E:3 * E], [(ones[:, :], ch[0]), (ones[:, :], ch[1])]).then_inc(pos_psum, 1)

                def gather(r):
                    pe.wait_ge(pick_ready, r + 1)
                    for c in range(KD):
                        last = group(ps[:, c // 4, P * (c % 4):P * (c % 4 + 1)],
                                     [(hn[:, t, P * c:P * (c + 1)], pick[:, t, :]) for t in range(TT)])
                        if c % 4 == 3:
                            last.then_inc(gather_psum, 1)

                def both(bank, parts):
                    for i, (a, bs) in enumerate(parts):
                        for e in range(2):
                            half = slice(CAP * e, CAP * (e + 1))
                            last = mm(ps[half, bank, :], a[:, half], bs[e], start=(i == 0), stop=(i == len(parts) - 1))
                    return last

                def pair(p, first, last):
                    r = l * NP + p
                    if first:
                        gather(r)
                    pe.wait_ge(gather_sb, 2 * r + 2)
                    for i in range(2):
                        pe.wait_ge(*pair_full(l, p, 2 * i))
                        pe.wait_ge(*pair_full(l, p, 2 * i + 1))
                        both(2 + i, [(xg[:, c, :], [by_k(2 * i + e)[:, c, :] for e in range(2)]) for c in range(KD)]
                             ).then_inc(gu_psum, 1)
                    if not first:
                        combine(r - 1)
                    pe.wait_ge(hid_ready, r + 1)
                    for f in range(KF):
                        last_t = nc.tensor.transpose(ps[:, 2, P * f:P * (f + 1)], hid[:, P * f:P * (f + 1)], ident[:, :])
                    last_t.then_inc(hidT_psum, 1)
                    pe.wait_ge(pg_ready, r + 1)
                    for t in range(TT):
                        last_t = nc.tensor.transpose(ps[:, 3, P * t:P * (t + 1)], pick_gate[:, t, :], ident[:, :])
                    last_t.then_inc(spread_psum, 1)
                    if not last:
                        gather(r + 1)
                    pe.wait_ge(hidT_sb, r + 1)
                    pe.wait_ge(*pair_full(l, p, 4))
                    pe.wait_ge(*pair_full(l, p, 5))
                    for h in range(2):
                        cols = slice(512 * h, 512 * (h + 1))
                        both(4 + h, [(hidT[:, f, :], [by_f(4 + e)[:, f, cols] for e in range(2)]) for f in range(KF)]
                             ).then_inc(down_psum, 1)
                    if not first:
                        pe.wait_ge(comb_added, 4 * r)

                def combine(r):
                    pe.wait_ge(down_sb, 2 * r + 2)
                    pe.wait_ge(spread_sb, r + 1)
                    for g in range(4):
                        t, h = g // 2, g % 2
                        if g >= 2:
                            pe.wait_ge(comb_added, 4 * r + (g - 1))
                        group(ps[:, 6 + h, :], [(spread[:, P * t:P * (t + 1)], down[:, 512 * h:512 * (h + 1)])]
                              ).then_inc(comb_psum, 1)

                pair(0, True, False)
                with pe.Fori(1, NP - 1) as p:
                    pair(p, False, False)
                pair(NP - 1, False, True)
                combine(l * NP + NP - 1)

                most = pe.value_load(flags[0:1, 0:1], min_val=0, max_val=T)
                before = pe.value_load(flags[0:1, 1:2], min_val=0, max_val=L)
                with pe.If(most > CAP):
                    def over(e, first):
                        n = before * (4 * E) + 4 * e
                        pe.wait_ge(ov_loaded, before * (48 * E) + 48 * e + 48)
                        for f in range(KF):
                            for i in range(2):
                                last = group(ps[:, f, T * i:T * (i + 1)],
                                             [(by_k(i)[:, c, P * f:P * (f + 1)], hT[:, c, :]) for c in range(KD)])
                            last.then_inc(ov_gu, 1)
                        pe.wait_ge(ov_hid, n + 4)
                        if first:
                            pe.wait_ge(comb_added, l * (4 * NP) + 4 * NP)
                        else:
                            pe.wait_ge(ov_added, n)
                        for g in range(4):
                            t, h = g // 2, g % 2
                            group(ps[:, 4 + g, :], [(over_hid[:, f, P * t:P * (t + 1)],
                                                     by_f(2)[:, f, 512 * h:512 * (h + 1)]) for f in range(KF)]
                                  ).then_inc(ov_down, 1)

                    over(0, True)
                    with pe.Fori(1, E) as e:
                        over(e, False)


_INS = ['x', 'positions', 'ln1_g', 'w_in', 'b_forget', 'q_norm_diff_g', 'k_norm_diff_g', 'lam_q1', 'lam_k1', 'lam_q2',
        'lam_k2', 'subln_g', 'q_norm_fox_g', 'k_norm_fox_g', 'w_diff_out', 'w_fox_out', 'w_o', 'ln2_g',
        'w_router_group', 'b_router_group', 'w_router_expert', 'b_router_expert', 'w_exp_gate', 'w_exp_up',
        'w_exp_down']


def kernel(**inputs):
    import numpy as _np
    import concourse.bacc as _bacc
    from concourse import mybir as _mybir
    from concourse.bass_utils import run_bass_kernel_spmd as _run

    nc = _bacc.Bacc("TRN2", target_bir_lowering=False, num_devices=1)
    arrays, args = {}, []
    for name in _INS:
        a = _np.ascontiguousarray(inputs[name])
        if name.startswith("w_exp"):
            a = a.reshape(-1, *a.shape[3:])
        arrays[f"in_{name}_dram"] = a
        args.append(nc.dram_tensor(f"in_{name}_dram", a.shape, _mybir.dt.from_np(a.dtype), kind="ExternalInput").ap())
    args.append(nc.dram_tensor("out_dram", (1, T, D), _mybir.dt.float32, kind="ExternalOutput").ap())
    hybrid_trunk(nc, *args)
    r = _run(nc, [arrays], core_ids=[0])
    return r.results[0]["out_dram"]
```

```python
import math
from contextlib import ExitStack

import numpy as np

import concourse.bass as bass
from concourse import mybir

ALU = mybir.AluOpType
ACT = mybir.ActivationFunctionType
F32 = mybir.dt.float32
F32R = mybir.dt.float32r
I32 = mybir.dt.int32
AX = mybir.AxisListType

P = 128
D = 1024
T = 256
TT = T // P
L = 2
HD = 64
KD = D // P
DIFF = 4
FOX = 8
MAPS = 2 * DIFF + FOX
UNITS = DIFF + FOX
ROT = HD // 4
HALF = ROT // 2
THETA = 500000.0
EPS = 1e-6
G, EG = 4, 8
E = G * EG
FF = 512
KF = FF // P
NP = E // 2
CAP = 64
SCALE = HD ** -0.5
NEG = -1.0e30
SLOTS = 6
CHUNK = 4096
FZ = 6 * 512
AUG = HD + 2

FRONT = 14
DIFF_OUT, FOX_OUT, W_O = 10, 11, 12
SLOT_OF = [(n + 2) % 3 for n in range(FRONT)]
HI_SLOT = [4 + n % 2 for n in range(W_O)] + [3, 4]
HT_SLOT = 3
PAIR_SLOT = [[1, 5, 2, 3, 0, 4], [0, 4, 1, 5, 2, 3]]
EXTRA = 2
FRONT_FILLS = [SLOT_OF.count(s) for s in range(SLOTS)]
LAYER_FILLS = [FRONT_FILLS[s] + NP - (s in PAIR_SLOT[1][:EXTRA]) for s in range(SLOTS)]
QUARTERS = 4
SPLITS = FRONT * QUARTERS
DIFF_BANK = [2, 3, 0, 1]

STATS = [1, 1] + 4 * [TT * 8] + [TT * DIFF] + [1, 1]
NORM1, QK0, SUBLN, NORM2 = 0, 2, 6, 7


def last_unit(s):
    if s < 0 or s >= MAPS:
        return None
    if s < 2 * DIFF:
        return s // 2 if s % 2 else None
    return DIFF + s - 2 * DIFF


def map_of_unit(u):
    return 2 * u + 1 if u < DIFF else 2 * DIFF + u - DIFF


HI_STEP = {0: (7, 0, 2), 1: (7, 2, 2)}
LO_STEP = {}
for _n in range(8, 11):
    _a = 4 * (_n - 7)
    HI_STEP.update({_a - 1: (_n, 0, 2), _a: (_n, 2, 1), _a + 1: (_n, 3, 1)})
    LO_STEP.update({_a: (_n, 0, 1), _a + 1: (_n, 1, 2), _a + 2: (_n, 3, 1)})
HI_STEP.update({16: (11, 0, 2), 17: (11, 2, 2)})
LO_STEP.update({1: (7, 0, 2), 2: (7, 2, 2), 17: (11, 0, 2), 18: (11, 2, 2)})


def lam_init(l):
    return 0.8 - 0.6 * math.exp(-0.3 * l)


def hybrid_trunk(nc, x, positions, ln1_g, w_in, b_forget, q_norm_diff_g, k_norm_diff_g, lam_q1, lam_k1, lam_q2,
                 lam_k2, subln_g, q_norm_fox_g, k_norm_fox_g, w_diff_out, w_fox_out, w_o, ln2_g, w_router_group,
                 b_router_group, w_router_expert, b_router_expert, w_exp_gate, w_exp_up, w_exp_down, out):
    with ExitStack() as ctx:
        def sb(name, shape, dt=F32):
            return ctx.enter_context(nc.sbuf_tensor(name, shape, dt))

        def sem(name):
            return ctx.enter_context(nc.semaphore(name))

        def sb_and_split(name, shape):
            at = -(-nc.sbuf_base // 32) * 32
            return sb(name, shape), nc.alloc_sbuf_tensor_at(name + "_split", shape, F32R, offset=at)

        ring, ring_split = sb_and_split("ring", [P, SLOTS, CHUNK])
        xr = sb("xr", [P, TT, D])
        hn = sb("hn", [P, TT, D])
        hT = sb("hT", [P, KD, T])
        qkd, qkd_split = sb_and_split("qkd", [P, 2 * TT * 8 * HD])
        vq, vq_split = sb_and_split("vq", [P, TT * 2 * 512 + 2 * TT * 8 * AUG])
        qkf, qkf_split = vq[:, TT * 1024:TT * 1024 + 2 * TT * 8 * AUG], vq_split[:, TT * 1024:TT * 1024 + 2 * TT * 8 * AUG]
        val = vq[:, 0:TT * 1024].rearrange("p (t n) -> p t n", t=TT)
        qkT = sb("qkT", [P, (4 + 8) * 2 * T])
        gT, gT_split = sb_and_split("gT", [P, 2 * KD, T])
        pT = sb("pT", [P, 2, 3 * P])
        qk_diff = qkd[:, :].rearrange("p (k t n) -> p k t n", k=2, t=TT)
        qk_fox = qkf.rearrange("p (k t m a) -> p k t m a", k=2, t=TT, m=8)
        head_lo = qkd_split[:, :].rearrange("p (c t) -> p c t", c=8)
        head_hi = qkf_split[:, 0:8 * T].rearrange("p (c t) -> p c t", c=8)
        h_hi, h_lo = [ring_split[:, HT_SLOT, KD * T * i:KD * T * (i + 1)].rearrange("p (c t) -> p c t", c=KD)
                      for i in range(2)]
        merged_lo, merged_hi = gT_split[:, 0:KD, :], gT_split[:, KD:2 * KD, :]
        rows = qkf[:, 0:4 * 3 * P].rearrange("p (b n) -> p b n", b=4)
        dT = qkT[:, 0:4 * 2 * T].rearrange("p (b k t) -> p b k t", b=4, k=2)
        fT = qkT[:, 4 * 2 * T:12 * 2 * T].rearrange("p (m k t) -> p m k t", m=8, k=2)
        squares = gT[:, 0:4, :].rearrange("p a b -> p (a b)")
        sub_squares = qkd[:, 0:TT * 512].rearrange("p (t n) -> p t n", t=TT)

        extra = [vq[:, 0:CHUNK], gT[:, :, :].rearrange("p c t -> p (c t)")]

        def carve(at, n):
            return qkT[:, at:at + n]
        xg = carve(0, 1024).rearrange("p (c s) -> p c s", c=KD)
        act_gate = carve(1024, FF)
        hid = carve(1536, FF)
        hidT = carve(2048, FF).rearrange("p (f s) -> p f s", f=KF)
        down = carve(2560, D)
        pick = carve(3584, TT * P).rearrange("p (t s) -> p t s", t=TT)
        pick_gate = carve(3840, TT * P).rearrange("p (t s) -> p t s", t=TT)
        spread = carve(4096, T)
        over_hid = gT[:, 0:4, :]
        over_act = gT[:, 4:8, :]

        ident = sb("ident", [P, P])
        tri = sb("tri", [P, P])
        tri_strict = sb("tri_strict", [P, P])
        ones = sb("ones", [P, P])
        mask = sb("mask", [P, 3 * P])
        slot_no = sb("slot_no", [P, CAP])
        rank_w = sb("rank_w", [P, EG])
        minus_half = sb("minus_half", [P, 16])
        eps = sb("eps", [P, 16])
        stage = sb("stage", [2 * L * KD + L, P])
        gains = sb("gains", [P, 2 * L * KD + L])
        qk_gain = sb("qk_gain", [P, 4, L, HD])
        lam_v = sb("lam_v", [P, 4, L, HD])
        lam_p = sb("lam_p", [P, 2, L, HD])
        lam_s = sb("lam_s", [P, 2, L])
        neg_lam = sb("neg_lam", [P, L])
        sub_gain = sb("sub_gain", [P, L])
        gain2_now = sb("gain2_now", [P, KD])
        sub_gain_now = sb("sub_gain_now", [P, 1])
        bf = sb("bf", [FOX, L])
        br = sb("br", [P, L, G + E])
        w_route = sb("w_route", [P, L, KD, G + E])
        w_fz = sb("w_fz", [P, L, KD, FOX])
        w_fz_hi = ctx.enter_context(nc.sbuf_tensor("w_fz_hi", [P, KD, FOX], F32R))
        w_fz_lo = ctx.enter_context(nc.sbuf_tensor("w_fz_lo", [P, KD, FOX], F32R))
        pos_i = sb("pos_i", [P, TT], I32)
        pos_f = sb("pos_f", [P, TT])
        freq = sb("freq", [P, HALF])
        angle = sb("angle", [P, 2, TT, HALF])
        turns = sb("turns", [P, 2, TT, HALF])
        sincos = sb("sincos", [P, 2, TT, HALF])
        rot = sb("rot", [P, 4, TT, 8, HALF])
        meansq = sb("meansq", [P, len(STATS), 16])
        meansq_eps = sb("meansq_eps", [P, len(STATS), 16])
        rstd = sb("rstd", [P, len(STATS), 16])
        fz_z, fz_n, fz_e = hT[0:FOX, 0, :], hT[0:FOX, 1, :], hT[0:FOX, 2, :]
        log_f = sb("log_f", [P, TT, FOX])
        neg_max = sb("neg_max", [P, MAPS, 2])
        row_sum = sb("row_sum", [P, MAPS, 2])
        row_inv = sb("row_inv", [P, MAPS, 2])
        lg = sb("lg", [P, TT, G + E])
        r1 = sb("r1", [P, TT, 4])
        pg = sb("pg", [P, TT, G])
        ohg = sb("ohg", [P, TT, G])
        pe_ = sb("pe_", [P, TT, EG])
        lg_e = sb("lg_e", [P, TT, EG])
        oh1 = sb("oh1", [P, TT, EG])
        oh2 = sb("oh2", [P, TT, EG])
        rk = sb("rk", [P, TT, EG])
        gsel = sb("gsel", [P, TT, EG, G])
        chosen = sb("chosen", [P, TT, G, EG])
        gate = sb("gate", [P, TT, E])
        gate_over = sb("gate_over", [P, TT, E])
        place = sb("place", [P, TT, E])
        cnt = sb("cnt", [P, 1])
        flags = sb("flags", [1, 2], I32)
        flag_f = sb("flag_f", [1, 3])

        ps = ctx.enter_context(nc.psum_tensor("ps", [P, 8, 512], F32))

        slot_full = [sem(f"slot_full{i}") for i in range(SLOTS)]
        angles_in, rows_in, x_loaded, params_in = sem("angles_in"), sem("rows_in"), sem("x_loaded"), sem("params_in")
        late_in = sem("late_in")
        w_hi, w_lo = sem("w_hi"), sem("w_lo")
        fz_w_hi, fz_w_lo = sem("fz_w_hi"), sem("fz_w_lo")
        consts_made, gains_psum, gains_sb = sem("consts_made"), sem("gains_psum"), sem("gains_sb")
        lam_sums, lam_exp, angles_ready, sincos_ready = sem("lam_sums"), sem("lam_exp"), sem("angles_ready"), sem("sincos_ready")
        meansq_ready, rstd_ready = sem("meansq_ready"), sem("rstd_ready")
        hn_ready, hT_psum, hT_act, hT_dve = sem("hn_ready"), sem("hT_psum"), sem("hT_act"), sem("hT_dve")
        h_hi_ready, h_lo_ready = sem("h_hi_ready"), sem("h_lo_ready")
        fz_psum, fz_bent, fz_ln, logf_ready = sem("fz_psum"), sem("fz_bent"), sem("fz_ln"), sem("logf_ready")
        logfT_psum, logf_sb, cum_psum = sem("logfT_psum"), sem("logf_sb"), sem("cum_psum")
        CUM = T + TT * FOX
        tok_psum, tok_sb, qk_ready = sem("tok_psum"), sem("tok_sb"), sem("qk_ready")
        qkT_psum, dT_sb, fT_sb = sem("qkT_psum"), sem("dT_sb"), sem("fT_sb")
        s_psum, max_ready, exp_done, p_ready = sem("s_psum"), sem("max_ready"), sem("exp_done"), sem("p_ready")
        pT_psum, pT_sb, pv_psum, pv_sb = sem("pT_psum"), sem("pT_sb"), sem("pv_psum"), sem("pv_sb")
        subln_ready = sem("subln_ready")
        gz_psum, gz_sb = sem("gz_psum"), sem("gz_sb")
        headT_psum, head_hi_ready, head_lo_ready = sem("headT_psum"), sem("head_hi_ready"), sem("head_lo_ready")
        y_psum, sum_ready, merged_hi_ready, merged_lo_ready, wo_psum = (sem("y_psum"), sem("sum_ready"),
                                                                       sem("merged_hi_ready"), sem("merged_lo_ready"), sem("wo_psum"))
        logits_psum, centred, route_exp, chosen_ready, pos_psum = sem("logits_psum"), sem("centred"), sem("route_exp"), sem("chosen_ready"), sem("pos_psum")
        pick_ready, gather_psum, gather_sb = sem("pick_ready"), sem("gather_psum"), sem("gather_sb")
        gu_psum, silu_done, hid_ready = sem("gu_psum"), sem("silu_done"), sem("hid_ready")
        down_psum, down_sb = sem("down_psum"), sem("down_sb")
        hidT_psum, hidT_sb = sem("hidT_psum"), sem("hidT_sb")
        pg_ready, spread_psum, spread_sb = sem("pg_ready"), sem("spread_psum"), sem("spread_sb")
        comb_psum, comb_added = sem("comb_psum"), sem("comb_added")
        ov_loaded, ov_gu, ov_silu, ov_hid, ov_down, ov_added = (sem("ov_loaded"), sem("ov_gu"), sem("ov_silu"),
                                                               sem("ov_hid"), sem("ov_down"), sem("ov_added"))
        ANGLES, ROWS, PARAMS, LATE = TT + 4, 3, 2 * L + 4, 4
        ov_passed = sem("ov_passed")
        extra_full = [sem(f"extra_full{i}") for i in range(EXTRA)]
        x_final, out_stored = sem("x_final"), sem("out_stored")

        def front_full(l, n):
            s = SLOT_OF[n]
            return slot_full[s], (l * LAYER_FILLS[s] + SLOT_OF[:n + 1].count(s)) * 16

        def is_pair(p, n):
            return isinstance(p, int) and p == n

        def pair_slot(p, i):
            return PAIR_SLOT[0 if is_pair(p, 0) else 1][i]

        def pair_full(l, p, i):
            if is_pair(p, 1) and i < EXTRA:
                return extra_full[i], (l + 1) * 16
            s = pair_slot(p, i)
            missed = 1 if i < EXTRA and not is_pair(p, 0) else 0
            return slot_full[s], (l * LAYER_FILLS[s] + p + (FRONT_FILLS[s] + 1 - missed)) * 16

        def by_k(s, memory=ring):
            return memory[:, s, :].rearrange("p (c n) -> p c n", c=KD)

        def by_f(s, memory=ring):
            return memory[:, s, :].rearrange("p (c n) -> p c n", c=KF)

        def part_of(memory, s, q, n):
            return memory[:, s, CHUNK // QUARTERS * q:CHUNK // QUARTERS * (q + n)]

        def front_used(l, n):
            if n < 6:
                return tok_psum, l * 12 + (2 * n + 2)
            if n < 10:
                return gz_psum, l * 16 + 4 * (n - 5)
            if n < W_O:
                return y_psum, l * KD + 4 * (n - 9)
            return wo_psum, l * 4 + (n - W_O + 3)

        def pair_used(r, i):
            return (gu_psum, 4 * r + (i + 1)) if i < 4 else (down_psum, 2 * r + (i - 3))

        def of_layer(w, l):
            return w[bass.ds(l, 1)]

        block = ctx.enter_context(nc.Block())

        @block.sync
        def _(sp):
            cols = [0, 512, 3 * 512, 4 * 512, 2 * 512, 5 * 512] + [FZ + FOX + 512 * j for j in range(4)]

            def load(dst, src, landed):
                sp.dma_start(dst, src).then_inc(landed, 16)

            def to_all(a):
                flat = a.rearrange("l n -> (l n)").unsqueeze(0)
                return flat.broadcast_to([P, flat.shape[1]]).rearrange("p (l n) -> p l n", l=L)

            def first_params():
                for t in range(TT):
                    load(pos_i[:, t:t + 1], positions[:, P * t:P * (t + 1)].rearrange("b p -> p b"), angles_in)
                for i, g in enumerate((lam_q1, lam_k1, lam_q2, lam_k2)):
                    load(lam_v[:, i, :, :], to_all(g), angles_in)
                load(xr[:, :, :], x.rearrange("b (t p) d -> p (b t) d", p=P), x_loaded)
                load(stage[0:L * KD, :], ln1_g.rearrange("l (c p) -> (l c) p", p=P), rows_in)
                load(stage[L * KD:2 * L * KD, :], ln2_g.rearrange("l (c p) -> (l c) p", p=P), rows_in)
                load(stage[2 * L * KD:2 * L * KD + L, :], subln_g, rows_in)

            def later_params():
                for i in range(L):
                    load(w_fz[:, i, :, :], w_in[i, :, FZ:FZ + FOX].rearrange("(c p) n -> p c n", p=P), params_in)
                for i in range(L):
                    load(bf[:, i:i + 1], b_forget[i:i + 1, :].rearrange("l n -> n l"), params_in)
                for i, g in enumerate((q_norm_diff_g, k_norm_diff_g, q_norm_fox_g, k_norm_fox_g)):
                    load(qk_gain[:, i, :, :], to_all(g), params_in)

            def router_params():
                load(br[:, :, 0:G], to_all(b_router_group), late_in)
                load(br[:, :, G:G + E], to_all(b_router_expert), late_in)
                load(w_route[:, :, :, 0:G].rearrange("p l c n -> p (l c) n"),
                     w_router_group.rearrange("l (c p) n -> p (l c) n", p=P), late_in)
                load(w_route[:, :, :, G:G + E].rearrange("p l c n -> p (l c) n"),
                     w_router_expert.rearrange("l (c p) n -> p (l c) n", p=P), late_in)

            def front(l, first):
                for n in range(FRONT):
                    held = [m for m in range(n) if SLOT_OF[m] == SLOT_OF[n]]
                    if held:
                        sp.wait_ge(*front_used(l, held[-1]))
                    elif not first:
                        sp.wait_ge(*pair_used(l * NP - 1, PAIR_SLOT[1].index(SLOT_OF[n])))
                    dst = by_k(SLOT_OF[n])
                    if n < 10:
                        src = of_layer(w_in, l)[:, :, cols[n]:cols[n] + 512].rearrange("a (c p) n -> p (a c) n", p=P)
                    elif n < W_O:
                        dst = by_f(SLOT_OF[n])
                        src = of_layer([w_diff_out, w_fox_out][n - 10], l).rearrange("a (c p) n -> p (a c) n", p=P)
                    else:
                        h = 512 * (n - W_O)
                        src = of_layer(w_o, l)[:, :, h:h + 512].rearrange("a (c p) n -> p (a c) n", p=P)
                    sp.dma_start(dst, src).then_inc(slot_full[SLOT_OF[n]], 16)
                    if first and n == 0:
                        later_params()
                    if first and n == 2:
                        router_params()

            def experts(l):
                def pair_chunk(p, i):
                    w = [w_exp_gate, w_exp_up, w_exp_down][i // 2][bass.ds(l * E + 2 * p, 2)]
                    if i < 4:
                        src = w.rearrange("a (c k p) n -> p k (a c) n", k=2, p=P)[:, i % 2]
                    else:
                        src = w[:, :, 512 * (i % 2):512 * (i % 2 + 1)].rearrange("a (c p) n -> p (a c) n", p=P)
                    first_extra = is_pair(p, 1) and i < EXTRA
                    dst = extra[i] if first_extra else ring[:, pair_slot(p, i), :]
                    sp.dma_start(dst.rearrange("p (c n) -> p c n", c=8), src).then_inc(
                        extra_full[i] if first_extra else slot_full[pair_slot(p, i)], 16)

                for i in range(6):
                    held = [m for m in range(FRONT) if pair_slot(0, i) in (SLOT_OF[m], HI_SLOT[m])]
                    sp.wait_ge(*front_used(l, held[-1]))
                    pair_chunk(0, i)
                for i in range(EXTRA):
                    pair_chunk(1, i)
                for i in range(EXTRA, 6):
                    sp.wait_ge(*pair_used(l * NP, PAIR_SLOT[0].index(pair_slot(1, i))))
                    pair_chunk(1, i)
                for i in range(6):
                    sp.wait_ge(*(pair_used(l * NP, PAIR_SLOT[0].index(pair_slot(2, i))) if i < EXTRA
                                 else pair_used(l * NP + 1, i)))
                    pair_chunk(2, i)
                with sp.Fori(3, NP) as p:
                    for i in range(6):
                        sp.wait_ge(*pair_used(l * NP + p - 1, i))
                        pair_chunk(p, i)
                most = sp.value_load(flags[0:1, 0:1], min_val=0, max_val=T)
                before = sp.value_load(flags[0:1, 1:2], min_val=0, max_val=L)
                with sp.If(most > CAP):
                    def load_expert(e):
                        for i in range(3):
                            w = [w_exp_gate, w_exp_up, w_exp_down][i]
                            src = w[bass.ds(l * E + e, 1)].rearrange("a (c p) n -> p (a c) n", p=P)
                            sp.dma_start(by_k(i) if i < 2 else by_f(i), src).then_inc(ov_loaded, 16)

                    sp.wait_ge(down_psum, l * (2 * NP) + 2 * NP)
                    load_expert(0)
                    with sp.Fori(1, E) as e:
                        sp.wait_ge(ov_down, before * (4 * E) + 4 * e)
                        load_expert(e)
                    sp.wait_ge(ov_down, before * (4 * E) + 4 * E)
                    sp.sem_inc(ov_passed, 1)

            first_params()
            front(0, True)
            with sp.Fori(0, L - 1) as l:
                experts(l)
                front(l + 1, False)
            experts(L - 1)
            sp.wait_ge(x_final, 1)
            sp.dma_start(out.rearrange("b (t p) d -> p (b t) d", p=P), xr[:, :, :]).then_inc(out_stored, 16)
            sp.wait_ge(out_stored, 16)

        @block.gpsimd
        def _(pool):
            pool.memset(ident[:, :], 0.0)
            pool.memset(tri[:, :], 1.0)
            pool.memset(tri_strict[:, :], 1.0)
            pool.memset(ones[:, :], 1.0)
            pool.memset(mask[:, :], 0.0)
            pool.memset(minus_half[:, :], -0.5)
            pool.memset(eps[:, :], EPS)
            for j in range(HALF):
                pool.memset(freq[:, j:j + 1], float(np.float32(THETA) ** np.float32(-2.0 * j / ROT)))
            pool.iota(slot_no[:, :], [[1, CAP]], 1, 0, allow_small_or_imprecise_dtypes=True)
            pool.iota(rank_w[:, :], [[-1, EG]], EG, 0, allow_small_or_imprecise_dtypes=True)
            pool.drain()
            pool.affine_select(out=ident[:, :], in_=ident[:, :], compare_op=ALU.not_equal, fill=1.0, base=0,
                               pattern=[[-1, P]], channel_multiplier=1)
            pool.affine_select(out=tri[:, :], in_=tri[:, :], compare_op=ALU.is_ge, fill=0.0, base=0,
                               pattern=[[1, P]], channel_multiplier=-1)
            pool.affine_select(out=tri_strict[:, :], in_=tri_strict[:, :], compare_op=ALU.is_gt, fill=0.0, base=0,
                               pattern=[[1, P]], channel_multiplier=-1)
            for at in (0, 2 * P):
                last = pool.affine_select(out=mask[:, at:at + P], in_=mask[:, at:at + P], compare_op=ALU.is_ge,
                                          fill=NEG, base=0, pattern=[[-1, P]], channel_multiplier=1)
            last.then_inc(consts_made, 1)
            pool.drain()
            with pool.Fori(0, L) as l:
                for k, n in enumerate(STATS):
                    pool.wait_ge(meansq_ready, l * len(STATS) + k + 1)
                    pool.tensor_tensor(meansq_eps[:, k, 0:n], meansq[:, k, 0:n], eps[:, 0:n], ALU.add)
                    pool.drain()
                    pool.tensor_tensor(rstd[:, k, 0:n], meansq_eps[:, k, 0:n], minus_half[:, 0:n],
                                       ALU.pow).then_inc(rstd_ready, 1)

        @block.scalar
        def _(act):
            act.wait_ge(lam_sums, 1)
            act.activation(lam_s[:, :, :], lam_s[:, :, :], ACT.Exp).then_inc(lam_exp, 1)
            act.wait_ge(gains_psum, 1)
            act.activation(gains[:, :], ps[:, 0, 0:2 * L * KD + L], ACT.Copy).then_inc(gains_sb, 1)
            act.wait_ge(angles_ready, 1)
            act.activation(sincos[:, :, :, :], angle[:, :, :, :], ACT.Sin).then_inc(sincos_ready, 1)
            act.drain()

            with act.Fori(0, L) as l:
                def split_hi(n, q, quarters):
                    if q == 0:
                        act.wait_ge(*front_full(l, n))
                        before = [m for m in range(n) if HI_SLOT[m] == HI_SLOT[n]]
                        if before:
                            act.wait_ge(*front_used(l, before[-1]))
                        elif n == W_O:
                            act.wait_ge(*front_used(l, 9))
                    act.activation(part_of(ring_split, HI_SLOT[n], q, quarters), part_of(ring, SLOT_OF[n], q, quarters),
                                   ACT.Copy).then_inc(w_hi, quarters)

                split_hi(0, 0, 2)
                for b in range(4):
                    act.wait_ge(hT_psum, l * 8 + b + 1)
                    for c in (2 * b, 2 * b + 1):
                        last = act.activation(h_hi[:, c, :], ps[:, b, (c % 2) * T:(c % 2 + 1) * T], ACT.Copy,
                                              scale=gains[:, bass.ds(l * KD + c, 1)])
                    last.then_inc(h_hi_ready, 1)
                split_hi(0, 2, 2)
                act.activation(gain2_now[:, :], gains[:, bass.ds(l * KD + L * KD, KD)], ACT.Copy)
                act.wait_ge(params_in, 16 * PARAMS)
                act.activation(w_fz_hi[:, :, :], w_fz[:, bass.ds(l, 1), :, :].rearrange("p a c n -> p (a c) n"),
                               ACT.Copy).then_inc(fz_w_hi, 1)
                split_hi(1, 0, 2)
                split_hi(1, 2, 2)
                for j in range(6):
                    for t in range(TT):
                        act.wait_ge(tok_psum, l * 12 + 2 * j + t + 1)
                        src = ps[:, t, :]
                        if j < 2:
                            dst = qk_diff[:, j, t, :]
                        elif j < 4:
                            dst, src = qk_fox[:, j - 2, t, :, 0:HD], src.rearrange("p (m d) -> p m d", m=8)
                        else:
                            dst = val[:, t, 512 * (j - 4):512 * (j - 3)]
                        act.activation(dst, src, ACT.Copy).then_inc(tok_sb, 1)
                    if j < 5:
                        split_hi(j + 2, 0, 2)
                        split_hi(j + 2, 2, 2)
                    if j == 1:
                        act.wait_ge(fz_bent, l + 1)
                        act.activation(fz_e[:, :], fz_n[:, :], ACT.Exp)
                        act.drain()
                        act.activation(fz_e[:, :], fz_e[:, :], ACT.Ln, bias=1.0).then_inc(fz_ln, 1)
                for m in range(FOX):
                    act.wait_ge(qkT_psum, l * 12 + 4 + m + 1)
                    act.activation(fT[0:AUG, m, :, :].rearrange("p k t -> p (k t)"), ps[0:AUG, 4 + m % 4, :],
                                   ACT.Copy).then_inc(fT_sb, 1)
                for s in range(MAPS + 2):
                    if s < MAPS:
                        buf = rows[:, s % 4, :]
                        act.wait_ge(max_ready, l * MAPS + s + 1)
                        act.activation(buf[:, 0:P], buf[:, 0:P], ACT.Exp, bias=neg_max[:, s, 0:1],
                                       accum_out=row_sum[:, s, 0:1])
                        act.activation(buf[:, P:3 * P], buf[:, P:3 * P], ACT.Exp, bias=neg_max[:, s, 1:2],
                                       accum_out=row_sum[:, s, 1:2]).then_inc(exp_done, 1)
                        act.wait_ge(gz_psum, l * 16 + s + 1)
                        act.activation(gT[:, s, :], ps[:, s % 2, 0:T], ACT.Tanh, scale=0.5).then_inc(gz_sb, 1)
                    if s == MAPS:
                        for b in range(2):
                            act.wait_ge(headT_psum, l * 4 + b + 1)
                            act.activation(head_hi[:, 2 * b:2 * b + 2, :].rearrange("p c t -> p (c t)"), ps[:, b, :],
                                           ACT.Copy, scale=sub_gain_now[:, :]).then_inc(head_hi_ready, 1)
                    u = last_unit(s - 1)
                    if u is not None:
                        act.wait_ge(pT_psum, l * UNITS + u + 1)
                        if u >= 2:
                            act.wait_ge(pv_psum, l * UNITS + u - 1)
                        act.activation(pT[:, u % 2, :], ps[:, 4 + u % 2, 0:3 * P], ACT.Copy).then_inc(pT_sb, 1)
                    if s in HI_STEP:
                        split_hi(*HI_STEP[s])
                split_hi(W_O, 0, 2)
                for b in range(2, 4):
                    act.wait_ge(headT_psum, l * 4 + b + 1)
                    act.activation(head_hi[:, 2 * b:2 * b + 2, :].rearrange("p c t -> p (c t)"), ps[:, 4 + b, :],
                                   ACT.Copy).then_inc(head_hi_ready, 1)
                split_hi(W_O, 2, 2)
                for b in range(4):
                    act.wait_ge(sum_ready, l * 4 + b + 1)
                    act.activation(merged_hi[:, 2 * b:2 * b + 2, :], gT[:, 2 * b:2 * b + 2, :],
                                   ACT.Copy).then_inc(merged_hi_ready, 1)
                    if b >= 2:
                        split_hi(W_O + 1, 2 * (b - 2), 2)
                for t in range(TT):
                    act.wait_ge(hT_psum, l * 8 + 4 + 2 * t + 2)
                    for c in range(KD // 2, KD):
                        last = act.activation(hT[:, c, P * t:P * (t + 1)], ps[:, 2 * t + 1, P * (c % 4):P * (c % 4 + 1)],
                                              ACT.Copy, scale=gain2_now[:, c:c + 1])
                    last.then_inc(hT_act, 1)
                act.wait_ge(centred, l + 1)
                act.activation(pg[:, :, :], pg[:, :, :], ACT.Exp)
                act.activation(pe_[:, :, :], pe_[:, :, :], ACT.Exp).then_inc(route_exp, 1)

                def pair(r):
                    act.wait_ge(gu_psum, 4 * r + 2)
                    act.activation(act_gate, ps[:, 2, :], ACT.Silu).then_inc(silu_done, 1)
                    act.wait_ge(hidT_psum, r + 1)
                    act.activation(hidT.rearrange("p f s -> p (f s)"), ps[:, 2, :], ACT.Copy).then_inc(hidT_sb, 1)
                    for h in range(2):
                        act.wait_ge(down_psum, 2 * r + (h + 1))
                        act.activation(down[:, 512 * h:512 * (h + 1)], ps[:, 4 + h, :], ACT.Copy).then_inc(down_sb, 1)

                with act.Fori(0, NP) as p:
                    pair(l * NP + p)

                most = act.value_load(flags[0:1, 0:1], min_val=0, max_val=T)
                before = act.value_load(flags[0:1, 1:2], min_val=0, max_val=L)
                with act.If(most > CAP):
                    with act.Fori(0, E) as e:
                        for f in range(KF):
                            act.wait_ge(ov_gu, before * (4 * E) + 4 * e + (f + 1))
                            act.activation(over_act[:, f, :], ps[:, f, 0:T], ACT.Silu).then_inc(ov_silu, 1)

        @block.vector
        def _(dve):
            done = dve.drain

            dve.memset(flag_f[:, :], 0.0)
            dve.wait_ge(consts_made, 1)
            dve.wait_ge(angles_in, 16 * ANGLES)
            dve.tensor_tensor(lam_p[:, 0, :, :], lam_v[:, 0, :, :], lam_v[:, 1, :, :], ALU.mult)
            dve.tensor_tensor(lam_p[:, 1, :, :], lam_v[:, 2, :, :], lam_v[:, 3, :, :], ALU.mult)
            done()
            dve.tensor_reduce(lam_s[:, :, :], lam_p[:, :, :, :], AX.X, ALU.add).then_inc(lam_sums, 1)
            dve.tensor_copy(pos_f[:, :], pos_i[:, :])
            done()
            for t in range(TT):
                dve.tensor_scalar(angle[:, 0, t, :], freq[:, :], pos_f[:, t:t + 1], None, ALU.mult)
            done()
            big = 12582912.0
            dve.tensor_scalar(turns[:, 0, :, :], angle[:, 0, :, :], 1.0 / (2 * math.pi), big, ALU.mult, ALU.add)
            dve.tensor_scalar(turns[:, 1, :, :], angle[:, 0, :, :], 1.0 / (2 * math.pi), 0.25, ALU.mult, ALU.add)
            done()
            dve.tensor_scalar(turns[:, 1, :, :], turns[:, 1, :, :], big, None, ALU.add)
            done()
            dve.tensor_scalar(turns[:, :, :, :], turns[:, :, :, :], -big, None, ALU.add)
            dve.tensor_copy(angle[:, 1, :, :], angle[:, 0, :, :])
            done()
            parts, rest = [], 2 * math.pi
            for step in (2.0 ** -5, 2.0 ** -16):
                parts.append(math.floor(rest / step) * step)
                rest -= parts[-1]
            parts.append(float(np.float32(rest)))
            for part in parts:
                dve.scalar_tensor_tensor(out=angle[:, :, :, :].rearrange("p a t j -> p (a t j)"),
                                         in0=turns[:, :, :, :].rearrange("p a t j -> p (a t j)"), scalar=-part,
                                         in1=angle[:, :, :, :].rearrange("p a t j -> p (a t j)"),
                                         op0=ALU.mult, op1=ALU.add)
                done()
            dve.tensor_scalar(angle[:, 1, :, :], angle[:, 1, :, :], math.pi / 2, None, ALU.add)
            done()
            dve.tensor_scalar(angle[:, :, :, :], angle[:, :, :, :], 3.1415925, -3.1415925, ALU.min,
                              ALU.max).then_inc(angles_ready, 1)
            dve.wait_ge(lam_exp, 1)
            dve.tensor_tensor(neg_lam[:, :], lam_s[:, 1, :], lam_s[:, 0, :], ALU.subtract)
            dve.wait_ge(gains_sb, 1)
            for l in range(L):
                dve.tensor_scalar(sub_gain[:, l:l + 1], gains[:, 2 * L * KD + l:2 * L * KD + l + 1],
                                  1.0 - lam_init(l), None, ALU.mult)
            done()
            for l in range(L):
                dve.tensor_scalar(neg_lam[:, l:l + 1], neg_lam[:, l:l + 1], -lam_init(l), None, ALU.add)
            dve.wait_ge(sincos_ready, 1)
            dve.wait_ge(x_loaded, 16)
            done()

            with dve.Fori(0, L) as l:
                def square_mean(k, t):
                    dve.tensor_tensor_reduce(out=hn[:, t, :], in0=xr[:, t, :], in1=xr[:, t, :], scale=1.0 / D, scalar=0.0,
                                             op0=ALU.mult, op1=ALU.add,
                                             accum_out=meansq[:, k + t, 0:1]).then_inc(meansq_ready, 1)

                def normed(k, t):
                    dve.wait_ge(rstd_ready, l * len(STATS) + (k + t + 1))
                    dve.tensor_scalar(hn[:, t, :], xr[:, t, :], rstd[:, k + t, 0:1], None, ALU.mult).then_inc(hn_ready, 1)

                def split_lo(n, q, quarters):
                    dve.wait_ge(w_hi, l * SPLITS + (QUARTERS * n + q + quarters))
                    dve.tensor_tensor(part_of(ring_split, SLOT_OF[n], q, quarters), part_of(ring, SLOT_OF[n], q, quarters),
                                      part_of(ring_split, HI_SLOT[n], q, quarters).bitcast(F32),
                                      ALU.subtract).then_inc(w_lo, quarters)

                dve.tensor_copy(sub_gain_now[:, :], sub_gain[:, bass.ds(l, 1)])
                for t in range(TT):
                    square_mean(NORM1, t)
                for t in range(TT):
                    normed(NORM1, t)
                split_lo(0, 0, 2)
                for b in range(4):
                    dve.wait_ge(h_hi_ready, l * 4 + b + 1)
                    for c in (2 * b, 2 * b + 1):
                        last = dve.scalar_tensor_tensor(out=h_lo[:, c, :], in0=ps[:, b, (c % 2) * T:(c % 2 + 1) * T],
                                                        scalar=gains[:, bass.ds(l * KD + c, 1)],
                                                        in1=h_hi[:, c, :].bitcast(F32), op0=ALU.mult, op1=ALU.subtract)
                    last.then_inc(h_lo_ready, 1)
                split_lo(0, 2, 2)
                dve.wait_ge(fz_w_hi, l + 1)
                dve.tensor_tensor(w_fz_lo[:, :, :], w_fz[:, bass.ds(l, 1), :, :].rearrange("p a c n -> p (a c) n"),
                                  w_fz_hi[:, :, :].bitcast(F32), ALU.subtract).then_inc(fz_w_lo, 1)
                split_lo(1, 0, 2)
                split_lo(1, 2, 2)

                def forget_bent():
                    dve.wait_ge(fz_psum, l + 1)
                    dve.tensor_scalar(fz_z[:, :], ps[0:FOX, 7, 0:T], bf[:, bass.ds(l, 1)], None, ALU.add)
                    done()
                    dve.tensor_scalar(fz_n[:, :], fz_z[:, :], -1.0, None, ALU.mult)
                    done()
                    dve.tensor_tensor(fz_n[:, :], fz_n[:, :], fz_z[:, :], ALU.min).then_inc(fz_bent, 1)
                    dve.tensor_scalar(fz_z[:, :], fz_z[:, :], 0.0, None, ALU.min)

                def forget_log():
                    dve.wait_ge(fz_ln, l + 1)
                    dve.tensor_tensor(fz_n[:, :], fz_z[:, :], fz_e[:, :], ALU.subtract).then_inc(logf_ready, 1)

                for j in range(4):
                    dve.wait_ge(tok_sb, l * 12 + 2 * j + 2)
                    if j == 0:
                        dve.wait_ge(params_in, 16 * PARAMS)
                    if j < 2:
                        heads = [qk_diff[:, j, t, :].rearrange("p (m d) -> p m d", m=8) for t in range(TT)]
                    else:
                        heads = [qk_fox[:, j - 2, t, :, 0:HD] for t in range(TT)]
                    sq = squares.rearrange("p (t m d) -> p t m d", t=TT, m=8)
                    for t in range(TT):
                        dve.scalar_tensor_tensor(out=sq[:, t], in0=heads[t], scalar=1.0 / HD, in1=heads[t],
                                                 op0=ALU.mult, op1=ALU.mult)
                    done()
                    k = QK0 + j
                    dve.tensor_reduce(meansq[:, k, :], squares.rearrange("p (m d) -> p m d", d=HD), AX.X,
                                      ALU.add).then_inc(meansq_ready, 1)
                    split_lo(j + 2, 0, 2)
                    split_lo(j + 2, 2, 2)
                    if j == 1:
                        forget_log()
                    dve.wait_ge(rstd_ready, l * len(STATS) + k + 1)
                    for t in range(TT):
                        scale = rstd[:, k, 8 * t:8 * (t + 1)].unsqueeze(2).broadcast_to([P, 8, HD])
                        dve.tensor_tensor(heads[t], heads[t], scale, ALU.mult)
                    done()
                    gain = qk_gain[:, j, bass.ds(l, 1), :].broadcast_to([P, 8, HD])
                    for t in range(TT):
                        last = dve.tensor_tensor(heads[t], heads[t], gain, ALU.mult)
                    if j < 2:
                        done()
                        for t in range(TT):
                            sin, cos = [sincos[:, i, t:t + 1, :].broadcast_to([P, 8, HALF]) for i in range(2)]
                            a, b = heads[t][:, :, 0:HALF], heads[t][:, :, HALF:ROT]
                            dve.tensor_tensor(rot[:, 0, t], a, cos, ALU.mult)
                            dve.tensor_tensor(rot[:, 1, t], b, sin, ALU.mult)
                            dve.tensor_tensor(rot[:, 2, t], b, cos, ALU.mult)
                            dve.tensor_tensor(rot[:, 3, t], a, sin, ALU.mult)
                        done()
                        for t in range(TT):
                            a, b = heads[t][:, :, 0:HALF], heads[t][:, :, HALF:ROT]
                            dve.tensor_tensor(a, rot[:, 0, t], rot[:, 1, t], ALU.subtract)
                            last = dve.tensor_tensor(b, rot[:, 2, t], rot[:, 3, t], ALU.add)
                    elif j == 3:
                        dve.wait_ge(cum_psum, l + 1)
                        for t in range(TT):
                            cum = ps[:, 7, CUM + FOX * t:CUM + FOX * (t + 1)]
                            dve.tensor_scalar(qk_fox[:, 0, t, :, HD], cum, 1.0 / SCALE, None, ALU.mult)
                            dve.memset(qk_fox[:, 0, t, :, HD + 1], 1.0)
                            dve.memset(qk_fox[:, 1, t, :, HD], 1.0)
                            last = dve.tensor_scalar(qk_fox[:, 1, t, :, HD + 1], cum, -1.0 / SCALE, None, ALU.mult)
                    last.then_inc(qk_ready, 1)
                    if j == 0:
                        forget_bent()
                    if j == 2:
                        dve.wait_ge(logfT_psum, l + 1)
                        dve.tensor_copy(log_f[:, :, :].rearrange("p t m -> p (t m)"),
                                        ps[:, 7, T:T + TT * FOX]).then_inc(logf_sb, 1)
                split_lo(6, 0, 2)
                split_lo(6, 2, 2)
                for b in range(4):
                    dve.wait_ge(qkT_psum, l * 12 + b + 1)
                    dve.tensor_copy(dT[:, b, :, :].rearrange("p k t -> p (k t)"), ps[:, 2 + b, :]).then_inc(dT_sb, 1)

                def head_low(b):
                    dve.wait_ge(head_hi_ready, l * 4 + b + 1)
                    hi, lo = [a[:, 2 * b:2 * b + 2, :].rearrange("p c t -> p (c t)") for a in (head_hi, head_lo)]
                    if b < 2:
                        dve.scalar_tensor_tensor(out=lo, in0=ps[:, b, :], scalar=sub_gain_now[:, :],
                                                 in1=hi.bitcast(F32), op0=ALU.mult,
                                                 op1=ALU.subtract).then_inc(head_lo_ready, 1)
                    else:
                        dve.tensor_tensor(lo, ps[:, 4 + b, :], hi.bitcast(F32),
                                          ALU.subtract).then_inc(head_lo_ready, 1)

                for s in range(MAPS + 2):
                    if s < MAPS:
                        buf = rows[:, s % 4, :]
                        dve.wait_ge(s_psum, l * MAPS + s + 1)
                        if s >= 4:
                            prev = s - 4 if s - 4 >= 2 * DIFF else 2 * ((s - 4) // 2) + 1
                            dve.wait_ge(pT_psum, l * UNITS + last_unit(prev) + 1)
                        dve.scalar_tensor_tensor(out=buf, in0=ps[:, 2 + s % 2, 0:3 * P], scalar=SCALE,
                                                 in1=mask[:, :], op0=ALU.mult, op1=ALU.add)
                        done()
                        dve.tensor_reduce(neg_max[:, s, 0:1], buf[:, 0:P], AX.X, ALU.max, negate=True)
                        dve.tensor_reduce(neg_max[:, s, 1:2], buf[:, P:3 * P], AX.X, ALU.max,
                                          negate=True).then_inc(max_ready, 1)
                    u = last_unit(s - 1)
                    if u is not None:
                        dve.wait_ge(exp_done, l * MAPS + s)
                        if u < DIFF:
                            m1, m2 = s - 2, s - 1
                            dve.reciprocal(row_inv[:, m1:m2 + 1, :], row_sum[:, m1:m2 + 1, :])
                            done()
                            dve.tensor_scalar(row_inv[:, m2, :], row_inv[:, m2, :], neg_lam[:, bass.ds(l, 1)], None,
                                              ALU.mult)
                            for q, (a, b) in enumerate(((0, P), (P, 3 * P))):
                                dve.tensor_scalar(rows[:, m1 % 4, a:b], rows[:, m1 % 4, a:b],
                                                  row_inv[:, m1, q:q + 1], None, ALU.mult)
                            done()
                            for q, (a, b) in enumerate(((0, P), (P, 3 * P))):
                                last = dve.scalar_tensor_tensor(
                                    out=rows[:, m2 % 4, a:b], in0=rows[:, m2 % 4, a:b], scalar=row_inv[:, m2, q:q + 1],
                                    in1=rows[:, m1 % 4, a:b], op0=ALU.mult, op1=ALU.add)
                            last.then_inc(p_ready, 1)
                        else:
                            dve.reciprocal(row_inv[:, s - 1, :], row_sum[:, s - 1, :])
                    u = last_unit(s - 2)
                    if u is not None:
                        done()
                        dve.wait_ge(pv_psum, l * UNITS + u + 1)
                        if u < DIFF:
                            dve.tensor_copy(hn[:, :, 128 * u:128 * (u + 1)],
                                            ps[:, 6 + u % 2, 0:256].rearrange("p (t d) -> p t d", t=TT)).then_inc(pv_sb, 1)
                        else:
                            m = u - DIFF
                            dve.tensor_tensor(hn[:, :, 512 + HD * m:512 + HD * (m + 1)],
                                              ps[:, 6 + u % 2, 0:128].rearrange("p (t d) -> p t d", t=TT),
                                              row_inv[:, s - 2, :].unsqueeze(2).broadcast_to([P, TT, HD]),
                                              ALU.mult).then_inc(pv_sb, 1)
                    if s == 10:
                        for t in range(TT):
                            dve.scalar_tensor_tensor(out=sub_squares[:, t, :], in0=hn[:, t, 0:512],
                                                     scalar=1.0 / (2 * HD), in1=hn[:, t, 0:512], op0=ALU.mult,
                                                     op1=ALU.mult)
                        done()
                        dve.tensor_reduce(meansq[:, SUBLN, 0:TT * DIFF],
                                          sub_squares.rearrange("p t (h d) -> p (t h) d", h=DIFF), AX.X,
                                          ALU.add).then_inc(meansq_ready, 1)
                    if s == 12:
                        dve.wait_ge(rstd_ready, l * len(STATS) + SUBLN + 1)
                        for t in range(TT):
                            o = hn[:, t, 0:512].rearrange("p (h d) -> p h d", h=DIFF)
                            sc = rstd[:, SUBLN, DIFF * t:DIFF * (t + 1)].unsqueeze(2).broadcast_to([P, DIFF, 2 * HD])
                            last = dve.tensor_tensor(o, o, sc, ALU.mult)
                        last.then_inc(subln_ready, 1)
                    if s in LO_STEP:
                        split_lo(*LO_STEP[s])
                    if s == MAPS:
                        for b in range(2):
                            head_low(b)

                def gated(branch, b):
                    g = gT[:, KD * branch + 2 * b:KD * branch + 2 * b + 2, :].rearrange("p c t -> p (c t)")
                    dve.wait_ge(y_psum, l * KD + (4 * branch + b + 1))
                    dve.scalar_tensor_tensor(out=g, in0=g, scalar=1.0, in1=ps[:, 4 + b if branch else DIFF_BANK[b], :],
                                             op0=ALU.add, op1=ALU.mult)

                def merged_low(b):
                    dve.wait_ge(merged_hi_ready, l * 4 + b + 1)
                    dve.tensor_tensor(merged_lo[:, 2 * b:2 * b + 2, :], gT[:, 2 * b:2 * b + 2, :],
                                      merged_hi[:, 2 * b:2 * b + 2, :].bitcast(F32),
                                      ALU.subtract).then_inc(merged_lo_ready, 1)

                for s in range(MAPS + 2, max(LO_STEP) + 1):
                    split_lo(*LO_STEP[s])
                for b in range(3):
                    gated(0, b)
                head_low(2)
                head_low(3)
                split_lo(W_O, 0, 2)
                gated(0, 3)
                split_lo(W_O, 2, 2)
                for b in range(4):
                    gated(1, b)
                    done()
                    dve.tensor_tensor(gT[:, 2 * b:2 * b + 2, :], gT[:, 2 * b:2 * b + 2, :],
                                      gT[:, KD + 2 * b:KD + 2 * b + 2, :], ALU.add).then_inc(sum_ready, 1)
                    if b:
                        merged_low(b - 1)
                merged_low(3)
                split_lo(W_O + 1, 0, 2)
                split_lo(W_O + 1, 2, 2)

                def residual(t, h):
                    dve.wait_ge(wo_psum, l * 4 + 2 * t + h + 1)
                    xh = xr[:, t, 512 * h:512 * (h + 1)]
                    dve.scalar_tensor_tensor(out=xh, in0=ps[:, 4 + 2 * t + h, :], scalar=0.5, in1=xh, op0=ALU.mult,
                                             op1=ALU.add)

                def transposed(t):
                    g2 = gains[:, bass.ds(l * KD + L * KD, KD // 2)].unsqueeze(2).broadcast_to([P, KD // 2, P])
                    dve.wait_ge(hT_psum, l * 8 + 4 + 2 * t + 1)
                    dve.tensor_tensor(hT[:, 0:KD // 2, P * t:P * (t + 1)],
                                      ps[:, 2 * t, :].rearrange("p (c s) -> p c s", c=4), g2,
                                      ALU.mult).then_inc(hT_dve, 1)

                for t in range(TT):
                    residual(t, 0)
                    if t:
                        transposed(t - 1)
                    residual(t, 1)
                    done()
                    square_mean(NORM2, t)
                    normed(NORM2, t)
                transposed(TT - 1)

                dve.wait_ge(late_in, 16 * LATE)
                dve.wait_ge(logits_psum, l + 1)
                for t in range(TT):
                    dve.tensor_tensor(lg[:, t, :], ps[:, 4 + t, 0:G + E],
                                      br[:, bass.ds(l, 1), :].rearrange("p a n -> p (a n)"), ALU.add)
                done()

                def bc(a, n):
                    return a.broadcast_to([P, TT, n])

                def first_of(onehot, score, best, n):
                    for t in range(TT):
                        dve.scalar_tensor_tensor(out=rk[:, t, 0:n], in0=score[:, t], scalar=best[:, t, :],
                                                 in1=rank_w[:, 0:n], op0=ALU.is_equal, op1=ALU.mult)
                    done()
                    dve.tensor_reduce(r1[:, :, 3:4], rk[:, :, 0:n], AX.X, ALU.max)
                    done()
                    dve.tensor_tensor(onehot, rk[:, :, 0:n], bc(r1[:, :, 3:4], n), ALU.is_equal)
                    done()

                dve.tensor_reduce(r1[:, :, 0:1], lg[:, :, 0:G], AX.X, ALU.max)
                done()
                dve.tensor_tensor(pg[:, :, :], lg[:, :, 0:G], bc(r1[:, :, 0:1], G), ALU.subtract)
                first_of(ohg[:, :, :], lg[:, :, 0:G], r1[:, :, 0:1], G)
                for t in range(TT):
                    dve.tensor_tensor(gsel[:, t], lg[:, t, G:G + E].rearrange("p (g e) -> p e g", g=G),
                                      ohg[:, t:t + 1, :].broadcast_to([P, EG, G]), ALU.mult)
                done()
                dve.tensor_reduce(lg_e[:, :, :], gsel[:, :, :, :], AX.X, ALU.add)
                done()
                dve.tensor_reduce(r1[:, :, 1:2], lg_e[:, :, :], AX.X, ALU.max)
                done()
                dve.tensor_tensor(pe_[:, :, :], lg_e[:, :, :], bc(r1[:, :, 1:2], EG), ALU.subtract).then_inc(centred, 1)
                first_of(oh1[:, :, :], lg_e[:, :, :], r1[:, :, 1:2], EG)
                dve.scalar_tensor_tensor(out=gsel[:, :, :, 0], in0=oh1[:, :, :], scalar=NEG, in1=lg_e[:, :, :],
                                         op0=ALU.mult, op1=ALU.add)
                done()
                dve.tensor_reduce(r1[:, :, 2:3], gsel[:, :, :, 0], AX.X, ALU.max)
                done()
                first_of(oh2[:, :, :], gsel[:, :, :, 0], r1[:, :, 2:3], EG)
                dve.tensor_tensor(oh1[:, :, :], oh1[:, :, :], oh2[:, :, :], ALU.add)
                done()
                for t in range(TT):
                    last = dve.tensor_tensor(chosen[:, t], ohg[:, t, :].unsqueeze(2).broadcast_to([P, G, EG]),
                                             oh1[:, t:t + 1, :].broadcast_to([P, G, EG]), ALU.mult)
                last.then_inc(chosen_ready, 1)
                dve.wait_ge(route_exp, l + 1)
                dve.tensor_reduce(r1[:, :, 0:1], pg[:, :, :], AX.X, ALU.add)
                dve.tensor_reduce(r1[:, :, 1:2], pe_[:, :, :], AX.X, ALU.add)
                done()
                dve.reciprocal(r1[:, :, 0:2], r1[:, :, 0:2])
                done()
                dve.tensor_tensor(pe_[:, :, :], pe_[:, :, :], bc(r1[:, :, 1:2], EG), ALU.mult)
                done()
                dve.tensor_tensor(pe_[:, :, :], pe_[:, :, :], oh1[:, :, :], ALU.mult)
                done()
                dve.tensor_reduce(r1[:, :, 2:3], pe_[:, :, :], AX.X, ALU.add)
                done()
                dve.reciprocal(r1[:, :, 2:3], r1[:, :, 2:3])
                done()
                dve.tensor_tensor(pe_[:, :, :], pe_[:, :, :], bc(r1[:, :, 2:3], EG), ALU.mult)
                done()
                dve.tensor_tensor(pe_[:, :, :], pe_[:, :, :], bc(r1[:, :, 0:1], EG), ALU.mult)
                done()
                for t in range(TT):
                    dve.tensor_tensor(gate[:, t, :].rearrange("p (g e) -> p g e", g=G), chosen[:, t],
                                      pe_[:, t:t + 1, :].broadcast_to([P, G, EG]), ALU.mult)
                dve.wait_ge(pos_psum, l + 1)
                flat = chosen[:, :, :, :].rearrange("p t g e -> p t (g e)")
                dve.scalar_tensor_tensor(out=place[:, :, :], in0=ps[:, 6, 0:TT * E].rearrange("p (t e) -> p t e", t=TT),
                                         scalar=1.0, in1=flat, op0=ALU.add, op1=ALU.mult)
                done()

                def make_pick(p):
                    pairs = place[:, :, bass.ds(2 * p, 2)].unsqueeze(3).broadcast_to([P, TT, 2, CAP])
                    for t in range(TT):
                        last = dve.tensor_tensor(pick[:, t, :].rearrange("p (e s) -> p e s", e=2),
                                                 slot_no[:, :].unsqueeze(1).broadcast_to([P, 2, CAP]), pairs[:, t],
                                                 ALU.is_equal)
                    last.then_inc(pick_ready, 1)

                def make_pick_gate(p):
                    for t in range(TT):
                        for e in range(2):
                            last = dve.tensor_scalar(pick_gate[:, t, CAP * e:CAP * (e + 1)], slot_no[:, :],
                                                     place[:, t, bass.ds(2 * p + e, 1)],
                                                     gate[:, t, bass.ds(2 * p + e, 1)], ALU.is_equal, ALU.mult)
                    last.then_inc(pg_ready, 1)

                def gathered(r):
                    g2 = gains[:, bass.ds(l * KD + L * KD, KD)].unsqueeze(2).broadcast_to([P, KD, P])
                    for h in range(2):
                        dve.wait_ge(gather_psum, 2 * r + (h + 1))
                        cs = slice(4 * h, 4 * h + 4)
                        dve.tensor_tensor(xg[:, cs, :], ps[:, h, :].rearrange("p (c s) -> p c s", c=4), g2[:, cs, :],
                                          ALU.mult).then_inc(gather_sb, 1)

                def hidden(r):
                    dve.wait_ge(silu_done, r + 1)
                    dve.wait_ge(gu_psum, 4 * r + 4)
                    dve.tensor_tensor(hid, act_gate, ps[:, 3, :], ALU.mult).then_inc(hid_ready, 1)

                def spread_out(r):
                    dve.wait_ge(spread_psum, r + 1)
                    dve.tensor_copy(spread, ps[:, 3, 0:T]).then_inc(spread_sb, 1)

                def add_pair(r):
                    for g in range(4):
                        t, h = g // 2, g % 2
                        dve.wait_ge(comb_psum, 4 * r + (g + 1))
                        xh = xr[:, t, 512 * h:512 * (h + 1)]
                        dve.tensor_tensor(xh, xh, ps[:, 6 + h, :], ALU.add).then_inc(comb_added, 1)

                def pair(p, first, last):
                    r = l * NP + p
                    if not last:
                        make_pick(p + 1)
                    if not first:
                        add_pair(r - 1)
                    hidden(r)
                    spread_out(r)
                    if not last:
                        make_pick_gate(p + 1)
                        gathered(r + 1)

                make_pick(0)
                dve.tensor_reduce(cnt[:, :], ps[:, 6, TT * E:TT * E + E], AX.X, ALU.max)
                make_pick_gate(0)
                done()
                dve.tensor_copy(flag_f[:, 0:1], cnt[0:1, :])
                dve.tensor_scalar(flag_f[:, 2:3], cnt[0:1, :], float(CAP), None, ALU.is_gt)
                dve.scalar_tensor_tensor(out=gate_over[:, :, :], in0=place[:, :, :], scalar=float(CAP),
                                         in1=gate[:, :, :], op0=ALU.is_gt, op1=ALU.mult)
                done()
                dve.tensor_copy(flags[:, :], flag_f[:, 0:2])
                done()
                dve.tensor_tensor(flag_f[:, 1:2], flag_f[:, 1:2], flag_f[:, 2:3], ALU.add)
                gathered(l * NP)
                pair(0, True, False)
                with dve.Fori(1, NP - 1) as p:
                    pair(p, False, False)
                pair(NP - 1, False, True)
                add_pair(l * NP + NP - 1)

                most = dve.value_load(flags[0:1, 0:1], min_val=0, max_val=T)
                before = dve.value_load(flags[0:1, 1:2], min_val=0, max_val=L)
                with dve.If(most > CAP):
                    with dve.Fori(0, E) as e:
                        for f in range(KF):
                            dve.wait_ge(ov_silu, before * (4 * E) + 4 * e + (f + 1))
                            dve.tensor_tensor(over_hid[:, f, :], over_act[:, f, :], ps[:, f, T:2 * T],
                                              ALU.mult).then_inc(ov_hid, 1)
                        for g in range(4):
                            t, h = g // 2, g % 2
                            dve.wait_ge(ov_down, before * (4 * E) + 4 * e + (g + 1))
                            xh = xr[:, t, 512 * h:512 * (h + 1)]
                            dve.scalar_tensor_tensor(out=xh, in0=ps[:, 4 + g, :],
                                                     scalar=gate_over[:, t, bass.ds(e, 1)], in1=xh, op0=ALU.mult,
                                                     op1=ALU.add).then_inc(ov_added, 1)
                done()
            dve.drain().then_inc(x_final, 1)

        @block.tensor
        def _(pe):
            mm = nc.tensor.matmul

            def group(out_ap, pairs):
                for i, (a, b) in enumerate(pairs):
                    last = mm(out_ap, a, b, start=(i == 0), stop=(i == len(pairs) - 1))
                return last

            pe.wait_ge(consts_made, 1)
            pe.wait_ge(rows_in, 16 * ROWS)
            rows_n = 2 * L * KD + L
            nc.tensor.transpose(ps[:, 0, 0:rows_n], stage[:, :], ident[0:rows_n, 0:rows_n]).then_inc(gains_psum, 1)
            pe.wait_ge(gains_sb, 1)

            def group3(out_ap, parts, before=None):
                for i, ((a_hi, a_lo), (b_hi, b_lo)) in enumerate(parts):
                    if before:
                        before(i)
                    mm(out_ap, a_hi, b_hi, start=(i == 0), stop=False)
                    mm(out_ap, a_hi, b_lo, start=False, stop=False)
                    last = mm(out_ap, a_lo, b_hi, start=False, stop=(i == len(parts) - 1))
                return last

            with pe.Fori(0, L) as l:
                def transposes():
                    pe.wait_ge(hn_ready, l * 4 + 2)
                    for c in range(KD):
                        for t in range(TT):
                            last = nc.tensor.transpose(ps[:, c // 2, (c % 2) * T + t * P:(c % 2) * T + (t + 1) * P],
                                                       hn[:, t, P * c:P * (c + 1)], ident[:, :])
                        if c % 2:
                            last.then_inc(hT_psum, 1)

                def chunk(n, columns, by=by_k):
                    hi, lo = by(HI_SLOT[n], ring_split), by(SLOT_OF[n], ring_split)
                    return [(hi[:, c, columns], lo[:, c, columns]) for c in range(hi.shape[1])]

                def split_done(n, quarters):
                    pe.wait_ge(w_lo, l * SPLITS + (QUARTERS * n + quarters))

                transposes()
                def h_tile(t):
                    return [(h_hi[:, c, P * t:P * (t + 1)], h_lo[:, c, P * t:P * (t + 1)]) for c in range(KD)]

                def project(j, also=None):
                    def before(c):
                        if j == 0 and c % 2 == 0:
                            pe.wait_ge(h_lo_ready, l * 4 + (c // 2 + 1))
                        if c % 4 == 0:
                            split_done(j, 2 + c // 2)
                    for t in range(TT):
                        if also and t == TT - 1:
                            pe.wait_ge(also, l + 1)
                        if j >= 1:
                            pe.wait_ge(tok_sb, l * 12 + 2 * (j - 1) + t + 1)
                        group3(ps[:, t, :], list(zip(h_tile(t), chunk(j, slice(0, 512)))),
                               before if t == 0 else None).then_inc(tok_psum, 1)

                project(0)
                pe.wait_ge(fz_w_lo, l + 1)
                group3(ps[0:FOX, 7, 0:T], [((w_fz_hi[:, c, :], w_fz_lo[:, c, :]), (h_hi[:, c, :], h_lo[:, c, :]))
                                           for c in range(KD)]).then_inc(fz_psum, 1)
                project(1)
                project(2)
                project(3, logf_ready)
                for t in range(TT):
                    last = nc.tensor.transpose(ps[:, 7, T + FOX * t:T + FOX * (t + 1)], fz_n[:, P * t:P * (t + 1)],
                                               ident[0:FOX, 0:FOX])
                last.then_inc(logfT_psum, 1)
                project(4)
                pe.wait_ge(logf_sb, l + 1)
                group(ps[:, 7, CUM:CUM + FOX], [(tri[:, :], log_f[:, 0, :])])
                group(ps[:, 7, CUM + FOX:CUM + 2 * FOX],
                      [(ones[:, :], log_f[:, 0, :]), (tri[:, :], log_f[:, 1, :])]).then_inc(cum_psum, 1)
                pe.wait_ge(qk_ready, l * 4 + 2)
                for b in range(4):
                    for k in range(2):
                        for t in range(TT):
                            last = nc.tensor.transpose(ps[:, 2 + b, T * k + P * t:T * k + P * (t + 1)],
                                                       qk_diff[:, k, t, P * b:P * (b + 1)], ident[:, :])
                    last.then_inc(qkT_psum, 1)
                project(5)
                pe.wait_ge(qk_ready, l * 4 + 4)
                pe.wait_ge(dT_sb, l * 4 + 4)
                for m in range(FOX):
                    if m >= 4:
                        pe.wait_ge(fT_sb, l * FOX + m - 3)
                    for k in range(2):
                        for t in range(TT):
                            last = nc.tensor.transpose(ps[0:AUG, 4 + m % 4, T * k + P * t:T * k + P * (t + 1)],
                                                       qk_fox[:, k, t, m, :], ident[:, :])
                    last.then_inc(qkT_psum, 1)

                def head_transposes(b):
                    for c in (2 * b, 2 * b + 1):
                        for t in range(TT):
                            last = nc.tensor.transpose(
                                ps[:, b if b < 2 else 4 + b, (c % 2) * T + P * t:(c % 2) * T + P * (t + 1)],
                                hn[:, t, P * c:P * (c + 1)], ident[:, :])
                    last.then_inc(headT_psum, 1)

                def branch(i, b):
                    heads = [(head_hi[:, 4 * i + c, :], head_lo[:, 4 * i + c, :]) for c in range(KF)]
                    bank = 4 + b if i else DIFF_BANK[b]
                    for j in (2 * b, 2 * b + 1):
                        last = group3(ps[:, bank, T * (j % 2):T * (j % 2 + 1)],
                                      list(zip(chunk(DIFF_OUT + i, slice(P * j, P * (j + 1)), by_f), heads)))
                    last.then_inc(y_psum, 1)

                for s in range(MAPS + 2):
                    if s < MAPS:
                        if s < 2 * DIFF:
                            m = s // 2 + DIFF * (s % 2)
                            half = slice(HD * (m % 2), HD * (m % 2 + 1))
                            q, k = dT[half, m // 2, 0, :], dT[half, m // 2, 1, :]
                        else:
                            q, k = fT[0:AUG, s - 2 * DIFF, 0, :], fT[0:AUG, s - 2 * DIFF, 1, :]
                        if s >= 2:
                            pe.wait_ge(max_ready, l * MAPS + s - 1)
                        if s == 2 * DIFF:
                            pe.wait_ge(fT_sb, l * FOX + FOX)
                        group(ps[:, 2 + s % 2, 0:P], [(q[:, 0:P], k[:, 0:P])])
                        group(ps[:, 2 + s % 2, P:3 * P], [(q[:, P:T], k)]).then_inc(s_psum, 1)
                        n = 6 + s // 4
                        if s % 4 == 0:
                            split_done(n, QUARTERS)
                        if s >= 2:
                            pe.wait_ge(gz_sb, l * 16 + s - 1)
                        else:
                            pe.wait_ge(tok_sb, l * 12 + 11 + s)
                        group3(ps[:, s % 2, 0:T], list(zip(chunk(n, slice(P * (s % 4), P * (s % 4 + 1))),
                                                           [(h_hi[:, c, :], h_lo[:, c, :]) for c in range(KD)]))
                               ).then_inc(gz_psum, 1)
                    if s == MAPS:
                        pe.wait_ge(subln_ready, l + 1)
                        pe.wait_ge(gz_sb, l * 16 + 16)
                        head_transposes(0)
                        head_transposes(1)
                    u = last_unit(s - 1)
                    if u is not None:
                        if u < DIFF:
                            pe.wait_ge(p_ready, l * DIFF + u + 1)
                            if u == 0:
                                pe.wait_ge(fT_sb, l * FOX + FOX)
                        else:
                            pe.wait_ge(exp_done, l * MAPS + s)
                        for i in range(3):
                            last = nc.tensor.transpose(ps[:, 4 + u % 2, P * i:P * (i + 1)],
                                                       rows[:, (s - 1) % 4, P * i:P * (i + 1)], ident[:, :])
                        last.then_inc(pT_psum, 1)
                    u = last_unit(s - 2)
                    if u is not None:
                        pe.wait_ge(pT_sb, l * UNITS + u + 1)
                        if u >= 2:
                            pe.wait_ge(pv_sb, l * UNITS + u - 1)
                        v0, dv = (2 * HD * u, 2 * HD) if u < DIFF else (512 + HD * (u - DIFF), HD)
                        b = pT[:, u % 2, :]
                        group(ps[:, 6 + u % 2, 0:dv], [(b[:, 0:P], val[:, 0, v0:v0 + dv])])
                        group(ps[:, 6 + u % 2, dv:2 * dv], [(b[:, P:2 * P], val[:, 0, v0:v0 + dv]),
                                                           (b[:, 2 * P:3 * P], val[:, 1, v0:v0 + dv])]).then_inc(pv_psum, 1)
                    if s == MAPS:
                        split_done(DIFF_OUT, QUARTERS)
                        pe.wait_ge(head_lo_ready, l * 4 + 2)
                        branch(0, 0)
                branch(0, 1)
                branch(0, 2)
                pe.wait_ge(pv_sb, l * UNITS + UNITS)
                head_transposes(2)
                head_transposes(3)
                branch(0, 3)
                split_done(FOX_OUT, QUARTERS)
                pe.wait_ge(head_lo_ready, l * 4 + 4)
                for b in range(4):
                    branch(1, b)
                def normed_transposes(t):
                    pe.wait_ge(hn_ready, l * 4 + 2 + t + 1)
                    for c in range(KD):
                        last = nc.tensor.transpose(ps[:, 2 * t + c // 4, P * (c % 4):P * (c % 4 + 1)],
                                                   hn[:, t, P * c:P * (c + 1)], ident[:, :])
                        if c % 4 == 3:
                            last.then_inc(hT_psum, 1)

                def router_logits(t):
                    pe.wait_ge(hT_act, l * 2 + t + 1)
                    pe.wait_ge(hT_dve, l * 2 + t + 1)
                    last = group(ps[:, 4 + t, 0:G + E],
                                 [(hT[:, c, P * t:P * (t + 1)],
                                   w_route[:, bass.ds(l, 1), c, :].rearrange("p a n -> p (a n)")) for c in range(KD)])
                    if t == TT - 1:
                        last.then_inc(logits_psum, 1)

                for g in range(4):
                    t, h = g // 2, g % 2

                    def before(c):
                        if h == 0 and c % 2 == 0:
                            pe.wait_ge(merged_lo_ready, l * 4 + (c // 2 + 1))
                        if c % 4 == 0:
                            split_done(W_O + h, 2 + c // 2)
                    m = [(merged_hi[:, c, P * t:P * (t + 1)], merged_lo[:, c, P * t:P * (t + 1)]) for c in range(KD)]
                    group3(ps[:, 4 + g, :], list(zip(m, chunk(W_O + h, slice(0, 512)))),
                           before if t == 0 else None).then_inc(wo_psum, 1)
                    if g == 2:
                        normed_transposes(0)
                pe.wait_ge(late_in, 16 * LATE)
                router_logits(0)
                normed_transposes(1)
                router_logits(1)
                pe.wait_ge(chosen_ready, l + 1)
                ch = [chosen[:, t].rearrange("p g e -> p (g e)") for t in range(TT)]
                group(ps[:, 6, 0:E], [(tri_strict[:, :], ch[0])])
                group(ps[:, 6, E:2 * E], [(ones[:, :], ch[0]), (tri_strict[:, :], ch[1])])
                group(ps[:, 6, 2 * E:3 * E], [(ones[:, :], ch[0]), (ones[:, :], ch[1])]).then_inc(pos_psum, 1)

                def gather(r):
                    pe.wait_ge(pick_ready, r + 1)
                    for c in range(KD):
                        last = group(ps[:, c // 4, P * (c % 4):P * (c % 4 + 1)],
                                     [(hn[:, t, P * c:P * (c + 1)], pick[:, t, :]) for t in range(TT)])
                        if c % 4 == 3:
                            last.then_inc(gather_psum, 1)

                def both(bank, parts):
                    for i, (a, b) in enumerate(parts):
                        for e in range(2):
                            half = slice(CAP * e, CAP * (e + 1))
                            last = mm(ps[half, bank, :], a[:, half], b[e], start=(i == 0), stop=(i == len(parts) - 1))
                        yield i, last

                def pair(p, first, last):
                    r = l * NP + p
                    if first:
                        gather(r)
                    pe.wait_ge(gather_sb, 2 * r + 2)

                    def weights(i):
                        w = extra[i] if i < EXTRA and is_pair(p, 1) else ring[:, pair_slot(p, i), :]
                        w = w.rearrange("p (a c n) -> p a c n", a=2, c=4)
                        return [[w[:, e, c, :] for e in range(2)] for c in range(4)]

                    for i in range(2):
                        pe.wait_ge(*pair_full(l, p, 2 * i))
                        ws = weights(2 * i) + weights(2 * i + 1)
                        for c, done_c in both(2 + i, [(xg[:, 2 * (c % 4) + c // 4, :], ws[c]) for c in range(KD)]):
                            if c == 3:
                                done_c.then_inc(gu_psum, 1)
                                pe.wait_ge(*pair_full(l, p, 2 * i + 1))
                        done_c.then_inc(gu_psum, 1)
                        if i == 0 and not first:
                            combine(r - 1, p)
                    pe.wait_ge(hid_ready, r + 1)
                    for f in range(KF):
                        last_t = nc.tensor.transpose(ps[:, 2, P * f:P * (f + 1)], hid[:, P * f:P * (f + 1)], ident[:, :])
                    last_t.then_inc(hidT_psum, 1)
                    pe.wait_ge(pg_ready, r + 1)
                    for t in range(TT):
                        last_t = nc.tensor.transpose(ps[:, 3, P * t:P * (t + 1)], pick_gate[:, t, :], ident[:, :])
                    last_t.then_inc(spread_psum, 1)
                    if not last:
                        gather(r + 1)
                    pe.wait_ge(hidT_sb, r + 1)
                    for h in range(2):
                        pe.wait_ge(*pair_full(l, p, 4 + h))
                        for f, done_f in both(4 + h, [(hidT[:, f, :], weights(4 + h)[f]) for f in range(KF)]):
                            pass
                        done_f.then_inc(down_psum, 1)

                def combine(r, after):
                    if not is_pair(after, 1):
                        pe.wait_ge(comb_added, 4 * r)
                    pe.wait_ge(down_sb, 2 * r + 2)
                    pe.wait_ge(spread_sb, r + 1)
                    for g in range(4):
                        t, h = g // 2, g % 2
                        if g >= 2:
                            pe.wait_ge(comb_added, 4 * r + (g - 1))
                        group(ps[:, 6 + h, :], [(spread[:, P * t:P * (t + 1)], down[:, 512 * h:512 * (h + 1)])]
                              ).then_inc(comb_psum, 1)

                pair(0, True, False)
                pair(1, False, False)
                with pe.Fori(2, NP - 1) as p:
                    pair(p, False, False)
                pair(NP - 1, False, True)
                combine(l * NP + NP - 1, NP)

                most = pe.value_load(flags[0:1, 0:1], min_val=0, max_val=T)
                before = pe.value_load(flags[0:1, 1:2], min_val=0, max_val=L)
                with pe.If(most > CAP):
                    def over(e, first):
                        n = before * (4 * E) + 4 * e
                        pe.wait_ge(ov_loaded, before * (48 * E) + 48 * e + 48)
                        for f in range(KF):
                            for i in range(2):
                                last = group(ps[:, f, T * i:T * (i + 1)],
                                             [(by_k(i)[:, c, P * f:P * (f + 1)], hT[:, c, :]) for c in range(KD)])
                            last.then_inc(ov_gu, 1)
                        pe.wait_ge(ov_hid, n + 4)
                        if first:
                            pe.wait_ge(comb_added, l * (4 * NP) + 4 * NP)
                        else:
                            pe.wait_ge(ov_added, n)
                        for g in range(4):
                            t, h = g // 2, g % 2
                            group(ps[:, 4 + g, :], [(over_hid[:, f, P * t:P * (t + 1)],
                                                     by_f(2)[:, f, 512 * h:512 * (h + 1)]) for f in range(KF)]
                                  ).then_inc(ov_down, 1)

                    over(0, True)
                    with pe.Fori(1, E) as e:
                        over(e, False)


_INS = ['x', 'positions', 'ln1_g', 'w_in', 'b_forget', 'q_norm_diff_g', 'k_norm_diff_g', 'lam_q1', 'lam_k1', 'lam_q2',
        'lam_k2', 'subln_g', 'q_norm_fox_g', 'k_norm_fox_g', 'w_diff_out', 'w_fox_out', 'w_o', 'ln2_g',
        'w_router_group', 'b_router_group', 'w_router_expert', 'b_router_expert', 'w_exp_gate', 'w_exp_up',
        'w_exp_down']


def kernel(**inputs):
    import numpy as _np
    import concourse.bacc as _bacc
    from concourse import mybir as _mybir
    from concourse.bass_utils import run_bass_kernel_spmd as _run

    nc = _bacc.Bacc("TRN2", target_bir_lowering=False, num_devices=1)
    arrays, args = {}, []
    for name in _INS:
        a = _np.ascontiguousarray(inputs[name])
        if name.startswith("w_exp"):
            a = a.reshape(-1, *a.shape[3:])
        arrays[f"in_{name}_dram"] = a
        args.append(nc.dram_tensor(f"in_{name}_dram", a.shape, _mybir.dt.from_np(a.dtype), kind="ExternalInput").ap())
    args.append(nc.dram_tensor("out_dram", (1, T, D), _mybir.dt.float32, kind="ExternalOutput").ap())
    hybrid_trunk(nc, *args)
    r = _run(nc, [arrays], core_ids=[0])
    return r.results[0]["out_dram"]
```

```python
import math
from contextlib import ExitStack

import numpy as np

import concourse.bass as bass
from concourse import mybir

ALU = mybir.AluOpType
ACT = mybir.ActivationFunctionType
F32 = mybir.dt.float32
F32R = mybir.dt.float32r
I32 = mybir.dt.int32
AX = mybir.AxisListType

P = 128
D = 1024
T = 256
TT = T // P
L = 2
HD = 64
KD = D // P
DIFF = 4
FOX = 8
MAPS = 2 * DIFF + FOX
UNITS = DIFF + FOX
ROT = HD // 4
HALF = ROT // 2
THETA = 500000.0
EPS = 1e-6
G, EG = 4, 8
E = G * EG
FF = 512
KF = FF // P
NP = E // 2
CAP = 64
SCALE = HD ** -0.5
NEG = -1.0e30
SLOTS = 6
CHUNK = 4096
FZ = 6 * 512
AUG = HD + 2

FRONT = 14
DIFF_OUT, FOX_OUT, W_O = 10, 11, 12
SLOT_OF = [(n + 2) % 3 for n in range(FRONT)]
HI_SLOT = [4 + n % 2 for n in range(W_O)] + [3, 4]
HT_SLOT = 3
FIRST_PAIRS = [["C", 1, 5, "A", 2, 3], [0, 4, "B", "C", 1, 5], ["A", 2, 3, 0, 4, "B"], ["C", 1, 5, "A", 2, 3]]
LATER_PAIRS = [0, 4, 1, 5, 2, 3]
FIRSTS = sum(FIRST_PAIRS, [])
PLACES = list(range(SLOTS)) + ["A", "B", "C"]
FRONT_FILLS = {m: SLOT_OF.count(m) for m in PLACES}
FIRST_FILLS = {m: FIRSTS.count(m) for m in PLACES}
LAYER_FILLS = {m: FRONT_FILLS[m] + FIRST_FILLS[m] + (NP - len(FIRST_PAIRS) if m in LATER_PAIRS else 0) for m in PLACES}
QUARTERS = 4
SPLITS = FRONT * QUARTERS
DIFF_BANK = [2, 3, 0, 1]
LAST_BANK = [[6, 7], [0, 1]]

STATS = [1, 1] + 4 * [TT * 8] + [TT * DIFF] + [1, 1]
NORM1, QK0, SUBLN, NORM2 = 0, 2, 6, 7


def last_unit(s):
    if s < 0 or s >= MAPS:
        return None
    if s < 2 * DIFF:
        return s // 2 if s % 2 else None
    return DIFF + s - 2 * DIFF


HI_STEP = {0: (7, 0, 2), 1: (7, 2, 2)}
LO_STEP = {}
for _n in (8, 10):
    _a = 4 * (_n - 7)
    HI_STEP.update({_a - 1: (_n, 0, 2), _a: (_n, 2, 1), _a + 1: (_n, 3, 1)})
    LO_STEP.update({_a: (_n, 0, 1), _a + 1: (_n, 1, 2), _a + 2: (_n, 3, 1)})
HI_STEP.update({7: (9, 0, 2), 8: (9, 2, 2), 16: (11, 0, 2), 17: (11, 2, 2)})
LO_STEP.update({9: (9, 0, 2), 10: (9, 2, 2), 1: (7, 0, 2), 2: (7, 2, 2), 17: (11, 0, 2), 18: (11, 2, 2)})


def lam_init(l):
    return 0.8 - 0.6 * math.exp(-0.3 * l)


def hybrid_trunk(nc, x, positions, ln1_g, w_in, b_forget, q_norm_diff_g, k_norm_diff_g, lam_q1, lam_k1, lam_q2,
                 lam_k2, subln_g, q_norm_fox_g, k_norm_fox_g, w_diff_out, w_fox_out, w_o, ln2_g, w_router_group,
                 b_router_group, w_router_expert, b_router_expert, w_exp_gate, w_exp_up, w_exp_down, out):
    with ExitStack() as ctx:
        def sb(name, shape, dt=F32):
            return ctx.enter_context(nc.sbuf_tensor(name, shape, dt))

        def sem(name):
            return ctx.enter_context(nc.semaphore(name))

        def sb_and_split(name, shape):
            at = -(-nc.sbuf_base // 32) * 32
            return sb(name, shape), nc.alloc_sbuf_tensor_at(name + "_split", shape, F32R, offset=at)

        ring, ring_split = sb_and_split("ring", [P, SLOTS, CHUNK])
        xr = sb("xr", [P, TT, D])
        hn = sb("hn", [P, TT, D])
        hT = sb("hT", [P, KD, T])
        qkd, qkd_split = sb_and_split("qkd", [P, 2 * TT * 8 * HD])
        vq, vq_split = sb_and_split("vq", [P, TT * 2 * 512 + 2 * TT * 8 * AUG])
        qkf, qkf_split = vq[:, TT * 1024:TT * 1024 + 2 * TT * 8 * AUG], vq_split[:, TT * 1024:TT * 1024 + 2 * TT * 8 * AUG]
        val = vq[:, 0:TT * 1024].rearrange("p (t n) -> p t n", t=TT)
        qkT = sb("qkT", [P, (4 + 8) * 2 * T])
        gT, gT_split = sb_and_split("gT", [P, 2 * KD, T])
        pT = sb("pT", [P, 2, 3 * P])
        qk_diff = qkd[:, :].rearrange("p (k t n) -> p k t n", k=2, t=TT)
        qk_fox = qkf.rearrange("p (k t m a) -> p k t m a", k=2, t=TT, m=8)
        head_lo = qkd_split[:, :].rearrange("p (c t) -> p c t", c=8)
        head_hi = qkf_split[:, 0:8 * T].rearrange("p (c t) -> p c t", c=8)
        h_hi, h_lo = [ring_split[:, HT_SLOT, KD * T * i:KD * T * (i + 1)].rearrange("p (c t) -> p c t", c=KD)
                      for i in range(2)]
        merged_lo, merged_hi = gT_split[:, 0:KD, :], gT_split[:, KD:2 * KD, :]
        ROWS_AT = 2 * TT * 8 * AUG - 4 * 3 * P
        rows = qkf[:, ROWS_AT:ROWS_AT + 4 * 3 * P].rearrange("p (b n) -> p b n", b=4)
        dT = qkT[:, 0:4 * 2 * T].rearrange("p (b k t) -> p b k t", b=4, k=2)
        fT = qkT[:, 4 * 2 * T:12 * 2 * T].rearrange("p (m k t) -> p m k t", m=8, k=2)
        squares = gT[:, 0:4, :].rearrange("p a b -> p (a b)")
        sub_squares = qkd[:, 0:TT * 512].rearrange("p (t n) -> p t n", t=TT)

        chunk_at = {m: ring[:, m, :] for m in range(SLOTS)}
        chunk_at.update({"A": vq[:, 0:CHUNK], "B": gT[:, :, :].rearrange("p c t -> p (c t)"), "C": qkT[:, 0:CHUNK]})
        pT_flat = pT[:, :, :].rearrange("p a b -> p (a b)")
        xg = qkd[:, 0:D].rearrange("p (c s) -> p c s", c=KD)
        down = qkd[:, D:2 * D]
        act_gate = qkT[:, CHUNK:CHUNK + FF]
        hid = qkT[:, CHUNK + FF:CHUNK + 2 * FF]
        hidT = qkT[:, CHUNK + 2 * FF:CHUNK + 3 * FF].rearrange("p (f s) -> p f s", f=KF)
        pick = pT_flat[:, 0:TT * P].rearrange("p (t s) -> p t s", t=TT)
        pick_gate = pT_flat[:, TT * P:2 * TT * P].rearrange("p (t s) -> p t s", t=TT)
        spread = pT_flat[:, 2 * TT * P:2 * TT * P + T]
        over_hid = gT[:, 0:4, :]
        over_act = gT[:, 4:8, :]

        ident = sb("ident", [P, P])
        tri = sb("tri", [P, P])
        tri_strict = sb("tri_strict", [P, P])
        tri_strict_r = ctx.enter_context(nc.sbuf_tensor("tri_strict_r", [P, P], F32R))
        ones_r = ctx.enter_context(nc.sbuf_tensor("ones_r", [P, P], F32R))
        ones = sb("ones", [P, P])
        mask = sb("mask", [P, 3 * P])
        slot_no = sb("slot_no", [P, CAP])
        rank_w = sb("rank_w", [P, EG])
        minus_half = sb("minus_half", [P, 16])
        eps = sb("eps", [P, 16])
        stage = sb("stage", [2 * L * KD + L, P])
        gains = sb("gains", [P, 2 * L * KD + L])
        qk_gain = sb("qk_gain", [P, 4, L, HD])
        lam_v = hT[:, 0:2, :].rearrange("p c t -> p (c t)").rearrange("p (i l d) -> p i l d", i=4, l=L)
        lam_p = hT[:, 2, :].rearrange("p (i l d) -> p i l d", i=2, l=L)
        lam_s = sb("lam_s", [P, 2, L])
        neg_lam = sb("neg_lam", [P, L])
        sub_gain = sb("sub_gain", [P, L])
        gain2_now = sb("gain2_now", [P, KD])
        sub_gain_now = sb("sub_gain_now", [P, 1])
        bf = sb("bf", [FOX, L])
        br = sb("br", [P, L, G + E])
        w_route = sb("w_route", [P, L, KD, G + E])
        w_fz = sb("w_fz", [P, L, KD, FOX])
        w_fz_hi = ctx.enter_context(nc.sbuf_tensor("w_fz_hi", [P, KD, FOX], F32R))
        w_fz_lo = ctx.enter_context(nc.sbuf_tensor("w_fz_lo", [P, KD, FOX], F32R))
        pos_i = sb("pos_i", [P, TT], I32)
        pos_f = sb("pos_f", [P, TT])
        freq = sb("freq", [P, HALF])
        angle = sb("angle", [P, 2, TT, HALF])
        turns = sb("turns", [P, 2, TT, HALF])
        sincos = sb("sincos", [P, 2, TT, HALF])
        rot = sb("rot", [P, 4, TT, 8, HALF])
        meansq = sb("meansq", [P, len(STATS), 16])
        meansq_eps = sb("meansq_eps", [P, len(STATS), 16])
        rstd = sb("rstd", [P, len(STATS), 16])
        fz_z, fz_n, fz_e = hT[0:FOX, 0, :], hT[0:FOX, 1, :], hT[0:FOX, 2, :]
        log_f = sb("log_f", [P, TT, FOX])
        neg_max = sb("neg_max", [P, MAPS, 2])
        row_sum = sb("row_sum", [P, MAPS, 2])
        row_inv = sb("row_inv", [P, MAPS, 2])
        lg_g = sb("lg_g", [P, TT, G])
        lg_x = sb("lg_x", [P, TT, G, EG])
        best_g = sb("best_g", [P, TT, 2])
        best_x = sb("best_x", [P, TT, G, 3])
        rank_g = sb("rank_g", [P, TT])
        rank_x = sb("rank_x", [P, TT, G])
        exp_g = sb("exp_g", [P, TT, G])
        exp_x = sb("exp_x", [P, TT, G, EG])
        is_g = sb("is_g", [P, TT, G])
        is_x = sb("is_x", [P, TT, G, EG])
        is_1 = sb("is_1", [P, TT, G, EG])
        rest_x = sb("rest_x", [P, TT, G, EG])
        chosen = ctx.enter_context(nc.sbuf_tensor("chosen", [P, TT, G, EG], F32R))
        gate = sb("gate", [P, TT, E])
        gate_over = sb("gate_over", [P, TT, E])
        place = sb("place", [P, TT, E])
        cnt = sb("cnt", [P, 1])
        flags = sb("flags", [1, 2], I32)
        flag_f = sb("flag_f", [1, 3])

        ps = ctx.enter_context(nc.psum_tensor("ps", [P, 8, 512], F32))

        landed = {m: sem(f"landed_{m}") for m in PLACES}
        angles_in, rows_in, x_loaded, params_in = sem("angles_in"), sem("rows_in"), sem("x_loaded"), sem("params_in")
        late_in = sem("late_in")
        w_hi, w_lo = sem("w_hi"), sem("w_lo")
        fz_w_hi, fz_w_lo = sem("fz_w_hi"), sem("fz_w_lo")
        consts_made, gains_psum, gains_sb = sem("consts_made"), sem("gains_psum"), sem("gains_sb")
        lam_sums, lam_exp, angles_ready, sincos_ready = sem("lam_sums"), sem("lam_exp"), sem("angles_ready"), sem("sincos_ready")
        meansq_ready, rstd_ready = sem("meansq_ready"), sem("rstd_ready")
        hn_ready, hT_psum, hT_act, hT_dve = sem("hn_ready"), sem("hT_psum"), sem("hT_act"), sem("hT_dve")
        h_hi_ready, h_lo_ready = sem("h_hi_ready"), sem("h_lo_ready")
        fz_psum, fz_bent, fz_ln, logf_ready = sem("fz_psum"), sem("fz_bent"), sem("fz_ln"), sem("logf_ready")
        logfT_psum, logf_sb, cum_psum = sem("logfT_psum"), sem("logf_sb"), sem("cum_psum")
        CUM = T + TT * FOX
        tok_psum, tok_sb, qk_ready = sem("tok_psum"), sem("tok_sb"), sem("qk_ready")
        qkT_psum, dT_sb, fT_sb = sem("qkT_psum"), sem("dT_sb"), sem("fT_sb")
        s_psum, max_ready, exp_done, p_ready = sem("s_psum"), sem("max_ready"), sem("exp_done"), sem("p_ready")
        pT_psum, pT_sb, pv_psum, pv_sb = sem("pT_psum"), sem("pT_sb"), sem("pv_psum"), sem("pv_sb")
        subln_ready = sem("subln_ready")
        gz_psum, gz_sb = sem("gz_psum"), sem("gz_sb")
        headT_psum, head_hi_ready, head_lo_ready = sem("headT_psum"), sem("head_hi_ready"), sem("head_lo_ready")
        y_psum, sum_ready, merged_hi_ready, merged_lo_ready, wo_psum = (sem("y_psum"), sem("sum_ready"),
                                                                       sem("merged_hi_ready"), sem("merged_lo_ready"), sem("wo_psum"))
        logits_psum, centred, route_exp, chosen_ready, pos_psum = sem("logits_psum"), sem("centred"), sem("route_exp"), sem("chosen_ready"), sem("pos_psum")
        count_psum = sem("count_psum")
        pick_ready, gather_psum, gather_sb = sem("pick_ready"), sem("gather_psum"), sem("gather_sb")
        gu_psum, silu_done, hid_ready = sem("gu_psum"), sem("silu_done"), sem("hid_ready")
        down_psum, down_sb = sem("down_psum"), sem("down_sb")
        hidT_psum, hidT_sb = sem("hidT_psum"), sem("hidT_sb")
        pg_ready, spread_psum, spread_sb = sem("pg_ready"), sem("spread_psum"), sem("spread_sb")
        comb_psum, comb_added = sem("comb_psum"), sem("comb_added")
        ov_loaded, ov_gu, ov_silu, ov_hid, ov_down, ov_added = (sem("ov_loaded"), sem("ov_gu"), sem("ov_silu"),
                                                               sem("ov_hid"), sem("ov_down"), sem("ov_added"))
        ANGLES, ROWS, PARAMS, LATE = TT + 4, 3, 2 * L + 4, 4
        ov_passed = sem("ov_passed")
        x_final, out_stored = sem("x_final"), sem("out_stored")

        def front_full(l, n):
            s = SLOT_OF[n]
            return landed[s], (l * LAYER_FILLS[s] + SLOT_OF[:n + 1].count(s)) * 16

        def is_pair(p, n):
            return isinstance(p, int) and p == n

        def is_first(p):
            return isinstance(p, int) and p < len(FIRST_PAIRS)

        def place_of(p, i):
            return FIRST_PAIRS[p][i] if is_first(p) else LATER_PAIRS[i]

        def pair_full(l, p, i):
            m = place_of(p, i)
            if is_first(p):
                return landed[m], (l * LAYER_FILLS[m] + (FRONT_FILLS[m] + FIRSTS[:6 * p + i + 1].count(m))) * 16
            return landed[m], (l * LAYER_FILLS[m] + p + (FRONT_FILLS[m] + FIRST_FILLS[m] + 1 - len(FIRST_PAIRS))) * 16

        def by_k(s, memory=ring):
            return memory[:, s, :].rearrange("p (c n) -> p c n", c=KD)

        def by_f(s, memory=ring):
            return memory[:, s, :].rearrange("p (c n) -> p c n", c=KF)

        def part_of(memory, s, q, n):
            return memory[:, s, CHUNK // QUARTERS * q:CHUNK // QUARTERS * (q + n)]

        def front_used(l, n):
            if n < 6:
                return tok_psum, l * 12 + (2 * n + 2)
            if n < 10:
                return gz_psum, l * 16 + 4 * (n - 5)
            if n < W_O:
                return y_psum, l * KD + 4 * (n - 9)
            return wo_psum, l * 4 + (n - W_O + 3)

        def pair_used(r, i):
            return (gu_psum, 4 * r + (i + 1)) if i < 4 else (down_psum, 2 * r + (i - 3))

        def of_layer(w, l):
            return w[bass.ds(l, 1)]

        block = ctx.enter_context(nc.Block())

        @block.sync
        def _(sp):
            cols = [0, 512, 3 * 512, 4 * 512, 2 * 512, 5 * 512] + [FZ + FOX + 512 * j for j in range(4)]

            def load(dst, src, landed):
                sp.dma_start(dst, src).then_inc(landed, 16)

            def to_all(a):
                flat = a.rearrange("l n -> (l n)").unsqueeze(0)
                return flat.broadcast_to([P, flat.shape[1]]).rearrange("p (l n) -> p l n", l=L)

            def first_params():
                for t in range(TT):
                    load(pos_i[:, t:t + 1], positions[:, P * t:P * (t + 1)].rearrange("b p -> p b"), angles_in)
                for i, g in enumerate((lam_q1, lam_k1, lam_q2, lam_k2)):
                    load(lam_v[:, i, :, :], to_all(g), angles_in)
                load(xr[:, :, :], x.rearrange("b (t p) d -> p (b t) d", p=P), x_loaded)
                load(stage[0:L * KD, :], ln1_g.rearrange("l (c p) -> (l c) p", p=P), rows_in)
                load(stage[L * KD:2 * L * KD, :], ln2_g.rearrange("l (c p) -> (l c) p", p=P), rows_in)
                load(stage[2 * L * KD:2 * L * KD + L, :], subln_g, rows_in)

            def later_params():
                for i in range(L):
                    load(w_fz[:, i, :, :], w_in[i, :, FZ:FZ + FOX].rearrange("(c p) n -> p c n", p=P), params_in)
                for i in range(L):
                    load(bf[:, i:i + 1], b_forget[i:i + 1, :].rearrange("l n -> n l"), params_in)
                for i, g in enumerate((q_norm_diff_g, k_norm_diff_g, q_norm_fox_g, k_norm_fox_g)):
                    load(qk_gain[:, i, :, :], to_all(g), params_in)

            def router_params():
                load(br[:, :, 0:G], to_all(b_router_group), late_in)
                load(br[:, :, G:G + E], to_all(b_router_expert), late_in)
                load(w_route[:, :, :, 0:G].rearrange("p l c n -> p (l c) n"),
                     w_router_group.rearrange("l (c p) n -> p (l c) n", p=P), late_in)
                load(w_route[:, :, :, G:G + E].rearrange("p l c n -> p (l c) n"),
                     w_router_expert.rearrange("l (c p) n -> p (l c) n", p=P), late_in)

            def pair_chunk(l, p, i):
                m = place_of(p, i)
                w = [w_exp_gate, w_exp_up, w_exp_down][i // 2][bass.ds(l * E + 2 * p, 2)]
                if i < 4:
                    src = w.rearrange("a (c k p) n -> p k (a c) n", k=2, p=P)[:, i % 2]
                else:
                    src = w[:, :, 512 * (i % 2):512 * (i % 2 + 1)].rearrange("a (c p) n -> p (a c) n", p=P)
                sp.dma_start(chunk_at[m].rearrange("p (c n) -> p c n", c=8), src).then_inc(landed[m], 16)

            def place_used(l, p, i):
                m = place_of(p, i)
                held = [(q, j) for q in range(p + 1) for j in range(6) if (q, j) < (p, i) and place_of(q, j) == m]
                if held:
                    return pair_used(l * NP + held[-1][0], held[-1][1])
                if m == "C":
                    return s_psum, l * MAPS + 2 * DIFF + 4
                if m == "A":
                    return front_used(l, FOX_OUT)
                if m == "B":
                    return front_used(l, FRONT - 1)
                return front_used(l, [n for n in range(FRONT) if m in (SLOT_OF[n], HI_SLOT[n])][-1])

            def front(l, first):
                for n in range(FRONT):
                    if n == W_O:
                        sp.wait_ge(*place_used(l, 0, 0))
                        pair_chunk(l, 0, 0)
                    held = [m for m in range(n) if SLOT_OF[m] == SLOT_OF[n]]
                    if held:
                        sp.wait_ge(*front_used(l, held[-1]))
                    elif not first:
                        sp.wait_ge(*pair_used(l * NP - 1, LATER_PAIRS.index(SLOT_OF[n])))
                    dst = by_k(SLOT_OF[n])
                    if n < 10:
                        src = of_layer(w_in, l)[:, :, cols[n]:cols[n] + 512].rearrange("a (c p) n -> p (a c) n", p=P)
                    elif n < W_O:
                        dst = by_f(SLOT_OF[n])
                        src = of_layer([w_diff_out, w_fox_out][n - 10], l).rearrange("a (c p) n -> p (a c) n", p=P)
                    else:
                        h = 512 * (n - W_O)
                        src = of_layer(w_o, l)[:, :, h:h + 512].rearrange("a (c p) n -> p (a c) n", p=P)
                    sp.dma_start(dst, src).then_inc(landed[SLOT_OF[n]], 16)
                    if first and n == 0:
                        later_params()
                    if first and n == 2:
                        router_params()

            def experts(l):
                for p in range(len(FIRST_PAIRS) + 1):
                    for i in range(6):
                        if (p, i) > (0, 0):
                            sp.wait_ge(*place_used(l, p, i))
                            pair_chunk(l, p, i)
                with sp.Fori(len(FIRST_PAIRS) + 1, NP) as p:
                    for i in range(6):
                        sp.wait_ge(*pair_used(l * NP + p - 1, i))
                        pair_chunk(l, p, i)
                most = sp.value_load(flags[0:1, 0:1], min_val=0, max_val=T)
                before = sp.value_load(flags[0:1, 1:2], min_val=0, max_val=L)
                with sp.If(most > CAP):
                    def load_expert(e):
                        for i in range(3):
                            w = [w_exp_gate, w_exp_up, w_exp_down][i]
                            src = w[bass.ds(l * E + e, 1)].rearrange("a (c p) n -> p (a c) n", p=P)
                            sp.dma_start(by_k(i) if i < 2 else by_f(i), src).then_inc(ov_loaded, 16)

                    sp.wait_ge(down_psum, l * (2 * NP) + 2 * NP)
                    load_expert(0)
                    with sp.Fori(1, E) as e:
                        sp.wait_ge(ov_down, before * (4 * E) + 4 * e)
                        load_expert(e)
                    sp.wait_ge(ov_down, before * (4 * E) + 4 * E)
                    sp.sem_inc(ov_passed, 1)

            first_params()
            front(0, True)
            with sp.Fori(0, L - 1) as l:
                experts(l)
                front(l + 1, False)
            experts(L - 1)
            sp.wait_ge(x_final, 1)
            sp.dma_start(out.rearrange("b (t p) d -> p (b t) d", p=P), xr[:, :, :]).then_inc(out_stored, 16)
            sp.wait_ge(out_stored, 16)

        @block.gpsimd
        def _(pool):
            pool.memset(ident[:, :], 0.0)
            pool.memset(tri[:, :], 1.0)
            pool.memset(tri_strict[:, :], 1.0)
            pool.memset(ones[:, :], 1.0)
            pool.memset(mask[:, :], 0.0)
            pool.memset(minus_half[:, :], -0.5)
            pool.memset(eps[:, :], EPS)
            for j in range(HALF):
                pool.memset(freq[:, j:j + 1], float(np.float32(THETA) ** np.float32(-2.0 * j / ROT)))
            pool.iota(slot_no[:, :], [[1, CAP]], 1, 0, allow_small_or_imprecise_dtypes=True)
            pool.iota(rank_w[:, :], [[-1, EG]], EG, 0, allow_small_or_imprecise_dtypes=True)
            pool.drain()
            pool.affine_select(out=ident[:, :], in_=ident[:, :], compare_op=ALU.not_equal, fill=1.0, base=0,
                               pattern=[[-1, P]], channel_multiplier=1)
            pool.affine_select(out=tri[:, :], in_=tri[:, :], compare_op=ALU.is_ge, fill=0.0, base=0,
                               pattern=[[1, P]], channel_multiplier=-1)
            pool.affine_select(out=tri_strict[:, :], in_=tri_strict[:, :], compare_op=ALU.is_gt, fill=0.0, base=0,
                               pattern=[[1, P]], channel_multiplier=-1)
            for at in (0, 2 * P):
                last = pool.affine_select(out=mask[:, at:at + P], in_=mask[:, at:at + P], compare_op=ALU.is_ge,
                                          fill=NEG, base=0, pattern=[[-1, P]], channel_multiplier=1)
            last.then_inc(consts_made, 1)
            pool.drain()
            with pool.Fori(0, L) as l:
                for k, n in enumerate(STATS):
                    pool.wait_ge(meansq_ready, l * len(STATS) + k + 1)
                    pool.tensor_tensor(meansq_eps[:, k, 0:n], meansq[:, k, 0:n], eps[:, 0:n], ALU.add)
                    pool.drain()
                    pool.tensor_tensor(rstd[:, k, 0:n], meansq_eps[:, k, 0:n], minus_half[:, 0:n],
                                       ALU.pow).then_inc(rstd_ready, 1)

        @block.scalar
        def _(act):
            act.wait_ge(lam_sums, 1)
            act.activation(lam_s[:, :, :], lam_s[:, :, :], ACT.Exp).then_inc(lam_exp, 1)
            act.wait_ge(consts_made, 1)
            act.activation(tri_strict_r[:, :], tri_strict[:, :], ACT.Copy)
            act.activation(ones_r[:, :], ones[:, :], ACT.Copy)
            act.wait_ge(gains_psum, 1)
            act.activation(gains[:, :], ps[:, 0, 0:2 * L * KD + L], ACT.Copy).then_inc(gains_sb, 1)
            act.wait_ge(angles_ready, 1)
            act.activation(sincos[:, :, :, :], angle[:, :, :, :], ACT.Sin).then_inc(sincos_ready, 1)
            act.drain()

            with act.Fori(0, L) as l:
                def split_hi(n, q, quarters):
                    if q == 0:
                        act.wait_ge(*front_full(l, n))
                        before = [m for m in range(n) if HI_SLOT[m] == HI_SLOT[n]]
                        if before:
                            act.wait_ge(*front_used(l, before[-1]))
                        elif n == W_O:
                            act.wait_ge(*front_used(l, 9))
                    act.activation(part_of(ring_split, HI_SLOT[n], q, quarters), part_of(ring, SLOT_OF[n], q, quarters),
                                   ACT.Copy).then_inc(w_hi, quarters)

                split_hi(0, 0, 2)
                split_hi(0, 2, 2)
                for b in range(4):
                    act.wait_ge(hT_psum, l * 8 + b + 1)
                    for c in (2 * b, 2 * b + 1):
                        last = act.activation(h_hi[:, c, :], ps[:, b, (c % 2) * T:(c % 2 + 1) * T], ACT.Copy,
                                              scale=gains[:, bass.ds(l * KD + c, 1)])
                    last.then_inc(h_hi_ready, 1)
                act.activation(gain2_now[:, :], gains[:, bass.ds(l * KD + L * KD, KD)], ACT.Copy)
                act.wait_ge(params_in, 16 * PARAMS)
                act.activation(w_fz_hi[:, :, :], w_fz[:, bass.ds(l, 1), :, :].rearrange("p a c n -> p (a c) n"),
                               ACT.Copy).then_inc(fz_w_hi, 1)
                split_hi(1, 0, 2)
                split_hi(1, 2, 2)
                for j in range(6):
                    for t in range(TT):
                        act.wait_ge(tok_psum, l * 12 + 2 * j + t + 1)
                        src = ps[:, t, :]
                        if j < 2:
                            dst = qk_diff[:, j, t, :]
                        elif j < 4:
                            dst, src = qk_fox[:, j - 2, t, :, 0:HD], src.rearrange("p (m d) -> p m d", m=8)
                        else:
                            dst = val[:, t, 512 * (j - 4):512 * (j - 3)]
                        act.activation(dst, src, ACT.Copy).then_inc(tok_sb, 1)
                    if j < 5:
                        split_hi(j + 2, 0, 2)
                        split_hi(j + 2, 2, 2)
                    if j == 1:
                        act.wait_ge(fz_bent, l + 1)
                        act.activation(fz_e[:, :], fz_n[:, :], ACT.Exp)
                        act.drain()
                        act.activation(fz_e[:, :], fz_e[:, :], ACT.Ln, bias=1.0).then_inc(fz_ln, 1)
                for m in range(FOX):
                    act.wait_ge(qkT_psum, l * 12 + 4 + m + 1)
                    act.activation(fT[0:AUG, m, :, :].rearrange("p k t -> p (k t)"), ps[0:AUG, 4 + m % 4, :],
                                   ACT.Copy).then_inc(fT_sb, 1)
                for s in range(MAPS + 3):
                    if s < MAPS:
                        buf = rows[:, s % 4, :]
                        act.wait_ge(max_ready, l * MAPS + s + 1)
                        act.activation(buf[:, 0:P], buf[:, 0:P], ACT.Exp, bias=neg_max[:, s, 0:1],
                                       accum_out=row_sum[:, s, 0:1])
                        act.activation(buf[:, P:3 * P], buf[:, P:3 * P], ACT.Exp, bias=neg_max[:, s, 1:2],
                                       accum_out=row_sum[:, s, 1:2]).then_inc(exp_done, 1)
                        act.wait_ge(gz_psum, l * 16 + s + 1)
                        act.activation(gT[:, s, :], ps[:, s % 2, 0:T], ACT.Tanh, scale=0.5).then_inc(gz_sb, 1)
                    if s == MAPS:
                        for b in range(2):
                            act.wait_ge(headT_psum, l * 4 + b + 1)
                            act.activation(head_hi[:, 2 * b:2 * b + 2, :].rearrange("p c t -> p (c t)"), ps[:, b, :],
                                           ACT.Copy, scale=sub_gain_now[:, :]).then_inc(head_hi_ready, 1)
                    u = last_unit(s - 2)
                    if u is not None:
                        act.wait_ge(pT_psum, l * UNITS + u + 1)
                        if u >= 2:
                            act.wait_ge(pv_psum, l * UNITS + u - 1)
                        act.activation(pT[:, u % 2, :], ps[:, 4 + u % 2, 0:3 * P], ACT.Copy).then_inc(pT_sb, 1)
                    if s in HI_STEP:
                        split_hi(*HI_STEP[s])
                split_hi(W_O, 0, 2)
                for b in range(2, 4):
                    act.wait_ge(headT_psum, l * 4 + b + 1)
                    act.activation(head_hi[:, 2 * b:2 * b + 2, :].rearrange("p c t -> p (c t)"), ps[:, 4 + b, :],
                                   ACT.Copy).then_inc(head_hi_ready, 1)
                split_hi(W_O, 2, 2)
                for b in range(4):
                    act.wait_ge(sum_ready, l * 4 + b + 1)
                    act.activation(merged_hi[:, 2 * b:2 * b + 2, :], gT[:, 2 * b:2 * b + 2, :],
                                   ACT.Copy).then_inc(merged_hi_ready, 1)
                    if b >= 2:
                        split_hi(W_O + 1, 2 * (b - 2), 2)
                for t in range(TT):
                    act.wait_ge(hT_psum, l * 8 + 4 + 2 * t + 2)
                    for c in range(KD // 2, KD):
                        last = act.activation(hT[:, c, P * t:P * (t + 1)], ps[:, 2 * t + 1, P * (c % 4):P * (c % 4 + 1)],
                                              ACT.Copy, scale=gain2_now[:, c:c + 1])
                    last.then_inc(hT_act, 1)
                act.wait_ge(centred, l + 1)
                act.activation(exp_g[:, :, :], exp_g[:, :, :], ACT.Exp)
                act.activation(exp_x[:, :, :, :], exp_x[:, :, :, :], ACT.Exp).then_inc(route_exp, 1)

                def pair(r):
                    act.wait_ge(gu_psum, 4 * r + 2)
                    act.activation(act_gate, ps[:, 2, :], ACT.Silu).then_inc(silu_done, 1)
                    act.wait_ge(hidT_psum, r + 1)
                    act.activation(hidT.rearrange("p f s -> p (f s)"), ps[:, 2, :], ACT.Copy).then_inc(hidT_sb, 1)
                    for h in range(2):
                        act.wait_ge(down_psum, 2 * r + (h + 1))
                        act.activation(down[:, 512 * h:512 * (h + 1)], ps[:, 4 + h, :], ACT.Copy).then_inc(down_sb, 1)

                with act.Fori(0, NP) as p:
                    pair(l * NP + p)

                most = act.value_load(flags[0:1, 0:1], min_val=0, max_val=T)
                before = act.value_load(flags[0:1, 1:2], min_val=0, max_val=L)
                with act.If(most > CAP):
                    with act.Fori(0, E) as e:
                        for f in range(KF):
                            act.wait_ge(ov_gu, before * (4 * E) + 4 * e + (f + 1))
                            act.activation(over_act[:, f, :], ps[:, f, 0:T], ACT.Silu).then_inc(ov_silu, 1)

        @block.vector
        def _(dve):
            done = dve.drain

            dve.memset(flag_f[:, :], 0.0)
            dve.wait_ge(consts_made, 1)
            dve.wait_ge(angles_in, 16 * ANGLES)
            dve.tensor_tensor(lam_p[:, 0, :, :], lam_v[:, 0, :, :], lam_v[:, 1, :, :], ALU.mult)
            dve.tensor_tensor(lam_p[:, 1, :, :], lam_v[:, 2, :, :], lam_v[:, 3, :, :], ALU.mult)
            done()
            dve.tensor_reduce(lam_s[:, :, :], lam_p[:, :, :, :], AX.X, ALU.add).then_inc(lam_sums, 1)
            dve.tensor_copy(pos_f[:, :], pos_i[:, :])
            done()
            for t in range(TT):
                dve.tensor_scalar(angle[:, 0, t, :], freq[:, :], pos_f[:, t:t + 1], None, ALU.mult)
            done()
            big = 12582912.0
            dve.tensor_scalar(turns[:, 0, :, :], angle[:, 0, :, :], 1.0 / (2 * math.pi), big, ALU.mult, ALU.add)
            dve.tensor_scalar(turns[:, 1, :, :], angle[:, 0, :, :], 1.0 / (2 * math.pi), 0.25, ALU.mult, ALU.add)
            done()
            dve.tensor_scalar(turns[:, 1, :, :], turns[:, 1, :, :], big, None, ALU.add)
            done()
            dve.tensor_scalar(turns[:, :, :, :], turns[:, :, :, :], -big, None, ALU.add)
            dve.tensor_copy(angle[:, 1, :, :], angle[:, 0, :, :])
            done()
            parts, rest = [], 2 * math.pi
            for step in (2.0 ** -5, 2.0 ** -16):
                parts.append(math.floor(rest / step) * step)
                rest -= parts[-1]
            parts.append(float(np.float32(rest)))
            for part in parts:
                dve.scalar_tensor_tensor(out=angle[:, :, :, :].rearrange("p a t j -> p (a t j)"),
                                         in0=turns[:, :, :, :].rearrange("p a t j -> p (a t j)"), scalar=-part,
                                         in1=angle[:, :, :, :].rearrange("p a t j -> p (a t j)"),
                                         op0=ALU.mult, op1=ALU.add)
                done()
            dve.tensor_scalar(angle[:, 1, :, :], angle[:, 1, :, :], math.pi / 2, None, ALU.add)
            done()
            dve.tensor_scalar(angle[:, :, :, :], angle[:, :, :, :], 3.1415925, -3.1415925, ALU.min,
                              ALU.max).then_inc(angles_ready, 1)
            dve.wait_ge(lam_exp, 1)
            dve.tensor_tensor(neg_lam[:, :], lam_s[:, 1, :], lam_s[:, 0, :], ALU.subtract)
            dve.wait_ge(gains_sb, 1)
            for l in range(L):
                dve.tensor_scalar(sub_gain[:, l:l + 1], gains[:, 2 * L * KD + l:2 * L * KD + l + 1],
                                  1.0 - lam_init(l), None, ALU.mult)
            done()
            for l in range(L):
                dve.tensor_scalar(neg_lam[:, l:l + 1], neg_lam[:, l:l + 1], -lam_init(l), None, ALU.add)
            dve.wait_ge(sincos_ready, 1)
            dve.wait_ge(x_loaded, 16)
            done()

            with dve.Fori(0, L) as l:
                def square_mean(k, t):
                    dve.tensor_tensor_reduce(out=hn[:, t, :], in0=xr[:, t, :], in1=xr[:, t, :], scale=1.0 / D, scalar=0.0,
                                             op0=ALU.mult, op1=ALU.add,
                                             accum_out=meansq[:, k + t, 0:1]).then_inc(meansq_ready, 1)

                def normed(k, t):
                    dve.wait_ge(rstd_ready, l * len(STATS) + (k + t + 1))
                    dve.tensor_scalar(hn[:, t, :], xr[:, t, :], rstd[:, k + t, 0:1], None, ALU.mult).then_inc(hn_ready, 1)

                def split_lo(n, q, quarters):
                    dve.wait_ge(w_hi, l * SPLITS + (QUARTERS * n + q + quarters))
                    dve.tensor_tensor(part_of(ring_split, SLOT_OF[n], q, quarters), part_of(ring, SLOT_OF[n], q, quarters),
                                      part_of(ring_split, HI_SLOT[n], q, quarters).bitcast(F32),
                                      ALU.subtract).then_inc(w_lo, quarters)

                dve.tensor_copy(sub_gain_now[:, :], sub_gain[:, bass.ds(l, 1)])
                for t in range(TT):
                    square_mean(NORM1, t)
                for t in range(TT):
                    normed(NORM1, t)
                split_lo(0, 0, 2)
                for b in range(4):
                    dve.wait_ge(h_hi_ready, l * 4 + b + 1)
                    for c in (2 * b, 2 * b + 1):
                        last = dve.scalar_tensor_tensor(out=h_lo[:, c, :], in0=ps[:, b, (c % 2) * T:(c % 2 + 1) * T],
                                                        scalar=gains[:, bass.ds(l * KD + c, 1)],
                                                        in1=h_hi[:, c, :].bitcast(F32), op0=ALU.mult, op1=ALU.subtract)
                    last.then_inc(h_lo_ready, 1)
                split_lo(0, 2, 2)
                dve.wait_ge(fz_w_hi, l + 1)
                dve.tensor_tensor(w_fz_lo[:, :, :], w_fz[:, bass.ds(l, 1), :, :].rearrange("p a c n -> p (a c) n"),
                                  w_fz_hi[:, :, :].bitcast(F32), ALU.subtract).then_inc(fz_w_lo, 1)
                split_lo(1, 0, 2)
                split_lo(1, 2, 2)

                def forget_bent():
                    dve.wait_ge(fz_psum, l + 1)
                    dve.tensor_scalar(fz_z[:, :], ps[0:FOX, 7, 0:T], bf[:, bass.ds(l, 1)], None, ALU.add)
                    done()
                    dve.tensor_scalar(fz_n[:, :], fz_z[:, :], -1.0, None, ALU.mult)
                    done()
                    dve.tensor_tensor(fz_n[:, :], fz_n[:, :], fz_z[:, :], ALU.min).then_inc(fz_bent, 1)
                    dve.tensor_scalar(fz_z[:, :], fz_z[:, :], 0.0, None, ALU.min)

                def forget_log():
                    dve.wait_ge(fz_ln, l + 1)
                    dve.tensor_tensor(fz_n[:, :], fz_z[:, :], fz_e[:, :], ALU.subtract).then_inc(logf_ready, 1)

                for j in range(4):
                    dve.wait_ge(tok_sb, l * 12 + 2 * j + 2)
                    if j == 0:
                        dve.wait_ge(params_in, 16 * PARAMS)
                    if j < 2:
                        heads = [qk_diff[:, j, t, :].rearrange("p (m d) -> p m d", m=8) for t in range(TT)]
                    else:
                        heads = [qk_fox[:, j - 2, t, :, 0:HD] for t in range(TT)]
                    sq = squares.rearrange("p (t m d) -> p t m d", t=TT, m=8)
                    for t in range(TT):
                        dve.scalar_tensor_tensor(out=sq[:, t], in0=heads[t], scalar=1.0 / HD, in1=heads[t],
                                                 op0=ALU.mult, op1=ALU.mult)
                    done()
                    k = QK0 + j
                    dve.tensor_reduce(meansq[:, k, :], squares.rearrange("p (m d) -> p m d", d=HD), AX.X,
                                      ALU.add).then_inc(meansq_ready, 1)
                    split_lo(j + 2, 0, 2)
                    split_lo(j + 2, 2, 2)
                    if j == 1:
                        forget_log()
                    dve.wait_ge(rstd_ready, l * len(STATS) + k + 1)
                    for t in range(TT):
                        scale = rstd[:, k, 8 * t:8 * (t + 1)].unsqueeze(2).broadcast_to([P, 8, HD])
                        dve.tensor_tensor(heads[t], heads[t], scale, ALU.mult)
                    done()
                    gain = qk_gain[:, j, bass.ds(l, 1), :].broadcast_to([P, 8, HD])
                    for t in range(TT):
                        last = dve.tensor_tensor(heads[t], heads[t], gain, ALU.mult)
                    if j < 2:
                        done()
                        for t in range(TT):
                            sin, cos = [sincos[:, i, t:t + 1, :].broadcast_to([P, 8, HALF]) for i in range(2)]
                            a, b = heads[t][:, :, 0:HALF], heads[t][:, :, HALF:ROT]
                            dve.tensor_tensor(rot[:, 0, t], a, cos, ALU.mult)
                            dve.tensor_tensor(rot[:, 1, t], b, sin, ALU.mult)
                            dve.tensor_tensor(rot[:, 2, t], b, cos, ALU.mult)
                            dve.tensor_tensor(rot[:, 3, t], a, sin, ALU.mult)
                        done()
                        for t in range(TT):
                            a, b = heads[t][:, :, 0:HALF], heads[t][:, :, HALF:ROT]
                            dve.tensor_tensor(a, rot[:, 0, t], rot[:, 1, t], ALU.subtract)
                            last = dve.tensor_tensor(b, rot[:, 2, t], rot[:, 3, t], ALU.add)
                    elif j == 3:
                        dve.wait_ge(cum_psum, l + 1)
                        for t in range(TT):
                            cum = ps[:, 7, CUM + FOX * t:CUM + FOX * (t + 1)]
                            dve.tensor_scalar(qk_fox[:, 0, t, :, HD], cum, 1.0 / SCALE, None, ALU.mult)
                            dve.memset(qk_fox[:, 0, t, :, HD + 1], 1.0)
                            dve.memset(qk_fox[:, 1, t, :, HD], 1.0)
                            last = dve.tensor_scalar(qk_fox[:, 1, t, :, HD + 1], cum, -1.0 / SCALE, None, ALU.mult)
                    last.then_inc(qk_ready, 1)
                    if j == 0:
                        forget_bent()
                    if j == 2:
                        dve.wait_ge(logfT_psum, l + 1)
                        dve.tensor_copy(log_f[:, :, :].rearrange("p t m -> p (t m)"),
                                        ps[:, 7, T:T + TT * FOX]).then_inc(logf_sb, 1)
                split_lo(6, 0, 2)
                split_lo(6, 2, 2)
                for b in range(4):
                    dve.wait_ge(qkT_psum, l * 12 + b + 1)
                    dve.tensor_copy(dT[:, b, :, :].rearrange("p k t -> p (k t)"), ps[:, 2 + b, :]).then_inc(dT_sb, 1)

                def head_low(b):
                    dve.wait_ge(head_hi_ready, l * 4 + b + 1)
                    hi, lo = [a[:, 2 * b:2 * b + 2, :].rearrange("p c t -> p (c t)") for a in (head_hi, head_lo)]
                    if b < 2:
                        dve.scalar_tensor_tensor(out=lo, in0=ps[:, b, :], scalar=sub_gain_now[:, :],
                                                 in1=hi.bitcast(F32), op0=ALU.mult,
                                                 op1=ALU.subtract).then_inc(head_lo_ready, 1)
                    else:
                        dve.tensor_tensor(lo, ps[:, 4 + b, :], hi.bitcast(F32),
                                          ALU.subtract).then_inc(head_lo_ready, 1)

                for s in range(MAPS + 3):
                    if s < MAPS:
                        buf = rows[:, s % 4, :]
                        dve.wait_ge(s_psum, l * MAPS + s + 1)
                        if s >= 4:
                            prev = s - 4 if s - 4 >= 2 * DIFF else 2 * ((s - 4) // 2) + 1
                            dve.wait_ge(pT_psum, l * UNITS + last_unit(prev) + 1)
                        dve.scalar_tensor_tensor(out=buf, in0=ps[:, 2 + s % 2, 0:3 * P], scalar=SCALE,
                                                 in1=mask[:, :], op0=ALU.mult, op1=ALU.add)
                        done()
                        dve.tensor_reduce(neg_max[:, s, 0:1], buf[:, 0:P], AX.X, ALU.max, negate=True)
                        dve.tensor_reduce(neg_max[:, s, 1:2], buf[:, P:3 * P], AX.X, ALU.max,
                                          negate=True).then_inc(max_ready, 1)
                    u = last_unit(s - 1)
                    if u is not None:
                        dve.wait_ge(exp_done, l * MAPS + s)
                        if u < DIFF:
                            m1, m2 = s - 2, s - 1
                            dve.reciprocal(row_inv[:, m1:m2 + 1, :], row_sum[:, m1:m2 + 1, :])
                            done()
                            dve.tensor_scalar(row_inv[:, m2, :], row_inv[:, m2, :], neg_lam[:, bass.ds(l, 1)], None,
                                              ALU.mult)
                            for q, (a, b) in enumerate(((0, P), (P, 3 * P))):
                                dve.tensor_scalar(rows[:, m1 % 4, a:b], rows[:, m1 % 4, a:b],
                                                  row_inv[:, m1, q:q + 1], None, ALU.mult)
                            done()
                            for q, (a, b) in enumerate(((0, P), (P, 3 * P))):
                                last = dve.scalar_tensor_tensor(
                                    out=rows[:, m2 % 4, a:b], in0=rows[:, m2 % 4, a:b], scalar=row_inv[:, m2, q:q + 1],
                                    in1=rows[:, m1 % 4, a:b], op0=ALU.mult, op1=ALU.add)
                            last.then_inc(p_ready, 1)
                        else:
                            dve.reciprocal(row_inv[:, s - 1, :], row_sum[:, s - 1, :])
                    u = last_unit(s - 3)
                    if u is not None:
                        done()
                        dve.wait_ge(pv_psum, l * UNITS + u + 1)
                        if u < DIFF:
                            dve.tensor_copy(hn[:, :, 128 * u:128 * (u + 1)],
                                            ps[:, 6 + u % 2, 0:256].rearrange("p (t d) -> p t d", t=TT)).then_inc(pv_sb, 1)
                        else:
                            m = u - DIFF
                            dve.tensor_tensor(hn[:, :, 512 + HD * m:512 + HD * (m + 1)],
                                              ps[:, 6 + u % 2, 0:128].rearrange("p (t d) -> p t d", t=TT),
                                              row_inv[:, s - 3, :].unsqueeze(2).broadcast_to([P, TT, HD]),
                                              ALU.mult).then_inc(pv_sb, 1)
                    if s == 11:
                        for t in range(TT):
                            dve.scalar_tensor_tensor(out=sub_squares[:, t, :], in0=hn[:, t, 0:512],
                                                     scalar=1.0 / (2 * HD), in1=hn[:, t, 0:512], op0=ALU.mult,
                                                     op1=ALU.mult)
                        done()
                        dve.tensor_reduce(meansq[:, SUBLN, 0:TT * DIFF],
                                          sub_squares.rearrange("p t (h d) -> p (t h) d", h=DIFF), AX.X,
                                          ALU.add).then_inc(meansq_ready, 1)
                    if s == 13:
                        dve.wait_ge(rstd_ready, l * len(STATS) + SUBLN + 1)
                        for t in range(TT):
                            o = hn[:, t, 0:512].rearrange("p (h d) -> p h d", h=DIFF)
                            sc = rstd[:, SUBLN, DIFF * t:DIFF * (t + 1)].unsqueeze(2).broadcast_to([P, DIFF, 2 * HD])
                            last = dve.tensor_tensor(o, o, sc, ALU.mult)
                        last.then_inc(subln_ready, 1)
                    if s in LO_STEP:
                        split_lo(*LO_STEP[s])
                    if s == MAPS:
                        for b in range(2):
                            head_low(b)

                def gated(branch, b):
                    g = gT[:, KD * branch + 2 * b:KD * branch + 2 * b + 2, :].rearrange("p c t -> p (c t)")
                    dve.wait_ge(y_psum, l * KD + (4 * branch + b + 1))
                    dve.scalar_tensor_tensor(out=g, in0=g, scalar=1.0, in1=ps[:, 4 + b if branch else DIFF_BANK[b], :],
                                             op0=ALU.add, op1=ALU.mult)

                def merged_low(b):
                    dve.wait_ge(merged_hi_ready, l * 4 + b + 1)
                    dve.tensor_tensor(merged_lo[:, 2 * b:2 * b + 2, :], gT[:, 2 * b:2 * b + 2, :],
                                      merged_hi[:, 2 * b:2 * b + 2, :].bitcast(F32),
                                      ALU.subtract).then_inc(merged_lo_ready, 1)

                for b in range(3):
                    gated(0, b)
                head_low(2)
                head_low(3)
                split_lo(W_O, 0, 2)
                gated(0, 3)
                split_lo(W_O, 2, 2)
                for b in range(4):
                    gated(1, b)
                    done()
                    dve.tensor_tensor(gT[:, 2 * b:2 * b + 2, :], gT[:, 2 * b:2 * b + 2, :],
                                      gT[:, KD + 2 * b:KD + 2 * b + 2, :], ALU.add).then_inc(sum_ready, 1)
                    if b:
                        merged_low(b - 1)
                merged_low(3)
                split_lo(W_O + 1, 0, 2)
                split_lo(W_O + 1, 2, 2)

                def residual(t, h):
                    dve.wait_ge(wo_psum, l * 4 + 2 * t + h + 1)
                    xh = xr[:, t, 512 * h:512 * (h + 1)]
                    dve.scalar_tensor_tensor(out=xh, in0=ps[:, 4 + 2 * t + h, :], scalar=0.5, in1=xh, op0=ALU.mult,
                                             op1=ALU.add)

                def transposed(t):
                    g2 = gains[:, bass.ds(l * KD + L * KD, KD // 2)].unsqueeze(2).broadcast_to([P, KD // 2, P])
                    dve.wait_ge(hT_psum, l * 8 + 4 + 2 * t + 1)
                    dve.tensor_tensor(hT[:, 0:KD // 2, P * t:P * (t + 1)],
                                      ps[:, 2 * t, :].rearrange("p (c s) -> p c s", c=4), g2,
                                      ALU.mult).then_inc(hT_dve, 1)

                for t in range(TT):
                    residual(t, 0)
                    if t:
                        transposed(t - 1)
                    residual(t, 1)
                    done()
                    square_mean(NORM2, t)
                    normed(NORM2, t)
                transposed(TT - 1)

                dve.wait_ge(late_in, 16 * LATE)
                dve.wait_ge(logits_psum, l + 1)
                for t in range(TT):
                    bias = br[:, bass.ds(l, 1), :].rearrange("p a n -> p (a n)")
                    dve.tensor_tensor(lg_x[:, t].rearrange("p g e -> p (g e)"), ps[:, 4 + t, G:G + E], bias[:, G:G + E],
                                      ALU.add)
                    dve.tensor_tensor(lg_g[:, t, :], ps[:, 4 + t, 0:G], bias[:, 0:G], ALU.add)
                done()

                def by_expert(a):
                    return a.rearrange("p t (g o) -> p (t g) o", o=1).broadcast_to([P, TT * G, EG])

                def flat(a):
                    return a[:, :, :, :].rearrange("p t g e -> p (t g) e")

                lx, ix, i1, rx, ex = flat(lg_x), flat(is_x), flat(is_1), flat(rest_x), flat(exp_x)
                ranks_x = rank_w[:, :].unsqueeze(1).broadcast_to([P, TT * G, EG])
                ranks_g = rank_w[:, 0:G].unsqueeze(1).broadcast_to([P, TT, G])
                bx = [best_x[:, :, :, i] for i in range(3)]

                def of_group(a):
                    return a.broadcast_to([P, TT, G])

                dve.tensor_reduce(bx[0], lg_x[:, :, :, :], AX.X, ALU.max)
                dve.tensor_reduce(best_g[:, :, 0:1], lg_g[:, :, :], AX.X, ALU.max)
                done()
                dve.tensor_tensor(i1, lx, by_expert(bx[0]), ALU.is_equal)
                dve.tensor_tensor(is_g[:, :, :], lg_g[:, :, :], of_group(best_g[:, :, 0:1]), ALU.is_equal)
                done()
                dve.tensor_tensor(i1, i1, ranks_x, ALU.mult)
                dve.tensor_tensor(is_g[:, :, :], is_g[:, :, :], ranks_g, ALU.mult)
                dve.tensor_tensor(ex, lx, by_expert(bx[0]), ALU.subtract)
                dve.tensor_tensor(exp_g[:, :, :], lg_g[:, :, :], of_group(best_g[:, :, 0:1]),
                                  ALU.subtract).then_inc(centred, 1)
                done()
                dve.tensor_reduce(rank_x[:, :, :], is_1[:, :, :, :], AX.X, ALU.max)
                dve.tensor_reduce(rank_g[:, :], is_g[:, :, :], AX.X, ALU.max)
                done()
                dve.tensor_tensor(i1, i1, by_expert(rank_x[:, :, :]), ALU.is_equal)
                dve.tensor_tensor(is_g[:, :, :], is_g[:, :, :], of_group(rank_g[:, :].unsqueeze(2)), ALU.is_equal)
                done()
                dve.scalar_tensor_tensor(out=rx, in0=i1, scalar=NEG, in1=lx, op0=ALU.mult, op1=ALU.add)
                done()
                dve.tensor_reduce(bx[1], rest_x[:, :, :, :], AX.X, ALU.max)
                done()
                dve.tensor_tensor(ix, rx, by_expert(bx[1]), ALU.is_equal)
                done()
                dve.tensor_tensor(ix, ix, ranks_x, ALU.mult)
                done()
                dve.tensor_reduce(rank_x[:, :, :], is_x[:, :, :, :], AX.X, ALU.max)
                done()
                dve.tensor_tensor(ix, ix, by_expert(rank_x[:, :, :]), ALU.is_equal)
                done()
                dve.tensor_tensor(ix, ix, i1, ALU.add)
                done()
                dve.tensor_tensor(flat(chosen), ix, by_expert(is_g[:, :, :]), ALU.mult).then_inc(chosen_ready, 1)
                dve.wait_ge(pos_psum, l + 1)
                takes = chosen[:, :, :, :].bitcast(F32).rearrange("p t g e -> p t (g e)")
                dve.scalar_tensor_tensor(out=place[:, :, :], in0=ps[:, 6, 0:TT * E].rearrange("p (t e) -> p t e", t=TT),
                                         scalar=1.0, in1=takes, op0=ALU.add, op1=ALU.mult)
                done()

                def make_pick(p):
                    pairs = place[:, :, bass.ds(2 * p, 2)].unsqueeze(3).broadcast_to([P, TT, 2, CAP])
                    for t in range(TT):
                        last = dve.tensor_tensor(pick[:, t, :].rearrange("p (e s) -> p e s", e=2),
                                                 slot_no[:, :].unsqueeze(1).broadcast_to([P, 2, CAP]), pairs[:, t],
                                                 ALU.is_equal)
                    last.then_inc(pick_ready, 1)

                def make_pick_gate(p):
                    for t in range(TT):
                        for e in range(2):
                            last = dve.tensor_scalar(pick_gate[:, t, CAP * e:CAP * (e + 1)], slot_no[:, :],
                                                     place[:, t, bass.ds(2 * p + e, 1)],
                                                     gate[:, t, bass.ds(2 * p + e, 1)], ALU.is_equal, ALU.mult)
                    last.then_inc(pg_ready, 1)

                def gathered(r):
                    g2 = gain2_now[:, :].rearrange("p (j k) -> p k j", k=2)
                    for k in range(2):
                        dve.wait_ge(gather_psum, 2 * r + (k + 1))
                        cs = slice(4 * k, 4 * k + 4)
                        dve.tensor_tensor(xg[:, cs, :], ps[:, k, :].rearrange("p (c s) -> p c s", c=4),
                                          g2[:, k, :].unsqueeze(2).broadcast_to([P, 4, P]), ALU.mult).then_inc(gather_sb, 1)

                def hidden(r):
                    dve.wait_ge(silu_done, r + 1)
                    dve.wait_ge(gu_psum, 4 * r + 4)
                    dve.tensor_tensor(hid, act_gate, ps[:, 3, :], ALU.mult).then_inc(hid_ready, 1)

                def spread_out(r):
                    dve.wait_ge(spread_psum, r + 1)
                    dve.tensor_copy(spread, ps[:, 3, 0:T]).then_inc(spread_sb, 1)

                def add_pair(r):
                    for g in range(4):
                        t, h = g // 2, g % 2
                        dve.wait_ge(comb_psum, 4 * r + (g + 1))
                        xh = xr[:, t, 512 * h:512 * (h + 1)]
                        dve.tensor_tensor(xh, xh, ps[:, 6 + h, :], ALU.add).then_inc(comb_added, 1)

                def add_last(r):
                    for h in range(2):
                        for t in range(TT):
                            dve.wait_ge(comb_psum, 4 * r + (2 * h + t + 1))
                            xh = xr[:, t, 512 * h:512 * (h + 1)]
                            dve.tensor_tensor(xh, xh, ps[:, LAST_BANK[h][t], :], ALU.add).then_inc(comb_added, 1)

                def pair(p, first, last):
                    r = l * NP + p
                    if not last:
                        make_pick(p + 1)
                    if not first:
                        add_pair(r - 1)
                    hidden(r)
                    spread_out(r)
                    if not last:
                        make_pick_gate(p + 1)
                        gathered(r + 1)

                make_pick(0)
                dve.wait_ge(route_exp, l + 1)
                dve.tensor_reduce(best_g[:, :, 1:2], exp_g[:, :, :], AX.X, ALU.add)
                dve.tensor_reduce(bx[2], exp_x[:, :, :, :], AX.X, ALU.add)
                done()
                dve.reciprocal(best_g[:, :, 1:2], best_g[:, :, 1:2])
                dve.reciprocal(bx[2], bx[2])
                done()
                dve.tensor_tensor(ex, ex, by_expert(bx[2]), ALU.mult)
                dve.tensor_tensor(is_g[:, :, :], is_g[:, :, :], of_group(best_g[:, :, 1:2]), ALU.mult)
                done()
                dve.tensor_tensor(ex, ex, ix, ALU.mult)
                done()
                dve.tensor_reduce(bx[2], exp_x[:, :, :, :], AX.X, ALU.add)
                done()
                dve.reciprocal(bx[2], bx[2])
                done()
                dve.tensor_tensor(ex, ex, by_expert(bx[2]), ALU.mult)
                done()
                dve.tensor_tensor(gate[:, :, :].rearrange("p t (g e) -> p (t g) e", g=G), ex, by_expert(is_g[:, :, :]),
                                  ALU.mult)
                dve.wait_ge(count_psum, l + 1)
                dve.tensor_reduce(cnt[:, :], ps[:, 7, 0:E], AX.X, ALU.max)
                done()
                make_pick_gate(0)
                dve.tensor_copy(flag_f[:, 0:1], cnt[0:1, :])
                dve.tensor_scalar(flag_f[:, 2:3], cnt[0:1, :], float(CAP), None, ALU.is_gt)
                dve.scalar_tensor_tensor(out=gate_over[:, :, :], in0=place[:, :, :], scalar=float(CAP),
                                         in1=gate[:, :, :], op0=ALU.is_gt, op1=ALU.mult)
                done()
                dve.tensor_copy(flags[:, :], flag_f[:, 0:2])
                done()
                dve.tensor_tensor(flag_f[:, 1:2], flag_f[:, 1:2], flag_f[:, 2:3], ALU.add)
                gathered(l * NP)
                pair(0, True, False)
                with dve.Fori(1, NP - 1) as p:
                    pair(p, False, False)
                pair(NP - 1, False, True)
                add_last(l * NP + NP - 1)

                most = dve.value_load(flags[0:1, 0:1], min_val=0, max_val=T)
                before = dve.value_load(flags[0:1, 1:2], min_val=0, max_val=L)
                with dve.If(most > CAP):
                    with dve.Fori(0, E) as e:
                        for f in range(KF):
                            dve.wait_ge(ov_silu, before * (4 * E) + 4 * e + (f + 1))
                            dve.tensor_tensor(over_hid[:, f, :], over_act[:, f, :], ps[:, f, T:2 * T],
                                              ALU.mult).then_inc(ov_hid, 1)
                        for g in range(4):
                            t, h = g // 2, g % 2
                            dve.wait_ge(ov_down, before * (4 * E) + 4 * e + (g + 1))
                            xh = xr[:, t, 512 * h:512 * (h + 1)]
                            dve.scalar_tensor_tensor(out=xh, in0=ps[:, 4 + g, :],
                                                     scalar=gate_over[:, t, bass.ds(e, 1)], in1=xh, op0=ALU.mult,
                                                     op1=ALU.add).then_inc(ov_added, 1)
                done()
            dve.drain().then_inc(x_final, 1)

        @block.tensor
        def _(pe):
            mm = nc.tensor.matmul

            def group(out_ap, pairs):
                for i, (a, b) in enumerate(pairs):
                    last = mm(out_ap, a, b, start=(i == 0), stop=(i == len(pairs) - 1))
                return last

            pe.wait_ge(consts_made, 1)
            pe.wait_ge(rows_in, 16 * ROWS)
            rows_n = 2 * L * KD + L
            nc.tensor.transpose(ps[:, 0, 0:rows_n], stage[:, :], ident[0:rows_n, 0:rows_n]).then_inc(gains_psum, 1)
            pe.wait_ge(gains_sb, 1)

            def group3(out_ap, parts, before=None):
                for i, ((a_hi, a_lo), (b_hi, b_lo)) in enumerate(parts):
                    if before:
                        before(i)
                    mm(out_ap, a_hi, b_hi, start=(i == 0), stop=False)
                    mm(out_ap, a_hi, b_lo, start=False, stop=False)
                    last = mm(out_ap, a_lo, b_hi, start=False, stop=(i == len(parts) - 1))
                return last

            with pe.Fori(0, L) as l:
                def transposes():
                    pe.wait_ge(hn_ready, l * 4 + 2)
                    for c in range(KD):
                        for t in range(TT):
                            last = nc.tensor.transpose(ps[:, c // 2, (c % 2) * T + t * P:(c % 2) * T + (t + 1) * P],
                                                       hn[:, t, P * c:P * (c + 1)], ident[:, :])
                        if c % 2:
                            last.then_inc(hT_psum, 1)

                def chunk(n, columns, by=by_k):
                    hi, lo = by(HI_SLOT[n], ring_split), by(SLOT_OF[n], ring_split)
                    return [(hi[:, c, columns], lo[:, c, columns]) for c in range(hi.shape[1])]

                def split_done(n, quarters):
                    pe.wait_ge(w_lo, l * SPLITS + (QUARTERS * n + quarters))

                transposes()
                def h_tile(t):
                    return [(h_hi[:, c, P * t:P * (t + 1)], h_lo[:, c, P * t:P * (t + 1)]) for c in range(KD)]

                def project(j, also=None):
                    def before(c):
                        if j == 0 and c % 2 == 0:
                            pe.wait_ge(h_lo_ready, l * 4 + (c // 2 + 1))
                        if c % 4 == 0:
                            split_done(j, 2 + c // 2)
                    for t in range(TT):
                        if also and t == TT - 1:
                            pe.wait_ge(also, l + 1)
                        if j >= 1:
                            pe.wait_ge(tok_sb, l * 12 + 2 * (j - 1) + t + 1)
                        group3(ps[:, t, :], list(zip(h_tile(t), chunk(j, slice(0, 512)))),
                               before if t == 0 else None).then_inc(tok_psum, 1)

                project(0)
                pe.wait_ge(fz_w_lo, l + 1)
                group3(ps[0:FOX, 7, 0:T], [((w_fz_hi[:, c, :], w_fz_lo[:, c, :]), (h_hi[:, c, :], h_lo[:, c, :]))
                                           for c in range(KD)]).then_inc(fz_psum, 1)
                project(1)
                project(2)
                project(3, logf_ready)
                for t in range(TT):
                    last = nc.tensor.transpose(ps[:, 7, T + FOX * t:T + FOX * (t + 1)], fz_n[:, P * t:P * (t + 1)],
                                               ident[0:FOX, 0:FOX])
                last.then_inc(logfT_psum, 1)
                project(4)
                pe.wait_ge(logf_sb, l + 1)
                group(ps[:, 7, CUM:CUM + FOX], [(tri[:, :], log_f[:, 0, :])])
                group(ps[:, 7, CUM + FOX:CUM + 2 * FOX],
                      [(ones[:, :], log_f[:, 0, :]), (tri[:, :], log_f[:, 1, :])]).then_inc(cum_psum, 1)
                pe.wait_ge(qk_ready, l * 4 + 2)
                for b in range(4):
                    for k in range(2):
                        for t in range(TT):
                            last = nc.tensor.transpose(ps[:, 2 + b, T * k + P * t:T * k + P * (t + 1)],
                                                       qk_diff[:, k, t, P * b:P * (b + 1)], ident[:, :])
                    last.then_inc(qkT_psum, 1)
                project(5)
                pe.wait_ge(qk_ready, l * 4 + 4)
                pe.wait_ge(dT_sb, l * 4 + 4)
                for m in range(FOX):
                    if m >= 4:
                        pe.wait_ge(fT_sb, l * FOX + m - 3)
                    for k in range(2):
                        for t in range(TT):
                            last = nc.tensor.transpose(ps[0:AUG, 4 + m % 4, T * k + P * t:T * k + P * (t + 1)],
                                                       qk_fox[:, k, t, m, :], ident[:, :])
                    last.then_inc(qkT_psum, 1)

                def head_transposes(b):
                    for c in (2 * b, 2 * b + 1):
                        for t in range(TT):
                            last = nc.tensor.transpose(
                                ps[:, b if b < 2 else 4 + b, (c % 2) * T + P * t:(c % 2) * T + P * (t + 1)],
                                hn[:, t, P * c:P * (c + 1)], ident[:, :])
                    last.then_inc(headT_psum, 1)

                def branch(i, b):
                    heads = [(head_hi[:, 4 * i + c, :], head_lo[:, 4 * i + c, :]) for c in range(KF)]
                    bank = 4 + b if i else DIFF_BANK[b]
                    for j in (2 * b, 2 * b + 1):
                        last = group3(ps[:, bank, T * (j % 2):T * (j % 2 + 1)],
                                      list(zip(chunk(DIFF_OUT + i, slice(P * j, P * (j + 1)), by_f), heads)))
                    last.then_inc(y_psum, 1)

                for s in range(MAPS + 3):
                    if s < MAPS:
                        if s < 2 * DIFF:
                            m = s // 2 + DIFF * (s % 2)
                            half = slice(HD * (m % 2), HD * (m % 2 + 1))
                            q, k = dT[half, m // 2, 0, :], dT[half, m // 2, 1, :]
                        else:
                            q, k = fT[0:AUG, s - 2 * DIFF, 0, :], fT[0:AUG, s - 2 * DIFF, 1, :]
                        if s >= 2:
                            pe.wait_ge(max_ready, l * MAPS + s - 1)
                        if s == 2 * DIFF:
                            pe.wait_ge(fT_sb, l * FOX + FOX)
                        group(ps[:, 2 + s % 2, 0:P], [(q[:, 0:P], k[:, 0:P])])
                        group(ps[:, 2 + s % 2, P:3 * P], [(q[:, P:T], k)]).then_inc(s_psum, 1)
                        n = 6 + s // 4
                        if s % 4 == 0:
                            split_done(n, QUARTERS)
                        if s >= 2:
                            pe.wait_ge(gz_sb, l * 16 + s - 1)
                        else:
                            pe.wait_ge(tok_sb, l * 12 + 11 + s)
                        group3(ps[:, s % 2, 0:T], list(zip(chunk(n, slice(P * (s % 4), P * (s % 4 + 1))),
                                                           [(h_hi[:, c, :], h_lo[:, c, :]) for c in range(KD)]))
                               ).then_inc(gz_psum, 1)
                    if s == MAPS:
                        pe.wait_ge(subln_ready, l + 1)
                        pe.wait_ge(gz_sb, l * 16 + 16)
                        head_transposes(0)
                        head_transposes(1)
                    u = last_unit(s - 2)
                    if u is not None:
                        if u < DIFF:
                            pe.wait_ge(p_ready, l * DIFF + u + 1)
                            if u == 0:
                                pe.wait_ge(fT_sb, l * FOX + FOX)
                        else:
                            pe.wait_ge(exp_done, l * MAPS + s - 1)
                        for i in range(3):
                            last = nc.tensor.transpose(ps[:, 4 + u % 2, P * i:P * (i + 1)],
                                                       rows[:, (s - 2) % 4, P * i:P * (i + 1)], ident[:, :])
                        last.then_inc(pT_psum, 1)
                    u = last_unit(s - 3)
                    if u is not None:
                        pe.wait_ge(pT_sb, l * UNITS + u + 1)
                        if u >= 2:
                            pe.wait_ge(pv_sb, l * UNITS + u - 1)
                        v0, dv = (2 * HD * u, 2 * HD) if u < DIFF else (512 + HD * (u - DIFF), HD)
                        b = pT[:, u % 2, :]
                        group(ps[:, 6 + u % 2, 0:dv], [(b[:, 0:P], val[:, 0, v0:v0 + dv])])
                        group(ps[:, 6 + u % 2, dv:2 * dv], [(b[:, P:2 * P], val[:, 0, v0:v0 + dv]),
                                                           (b[:, 2 * P:3 * P], val[:, 1, v0:v0 + dv])]).then_inc(pv_psum, 1)
                    if s == MAPS:
                        split_done(DIFF_OUT, QUARTERS)
                        pe.wait_ge(head_lo_ready, l * 4 + 2)
                        branch(0, 0)
                    if s == MAPS + 1:
                        branch(0, 1)
                branch(0, 2)
                pe.wait_ge(pv_sb, l * UNITS + UNITS)
                head_transposes(2)
                head_transposes(3)
                branch(0, 3)
                split_done(FOX_OUT, QUARTERS)
                pe.wait_ge(head_lo_ready, l * 4 + 4)
                for b in range(4):
                    branch(1, b)
                def normed_transposes(t):
                    pe.wait_ge(hn_ready, l * 4 + 2 + t + 1)
                    for c in range(KD):
                        last = nc.tensor.transpose(ps[:, 2 * t + c // 4, P * (c % 4):P * (c % 4 + 1)],
                                                   hn[:, t, P * c:P * (c + 1)], ident[:, :])
                        if c % 4 == 3:
                            last.then_inc(hT_psum, 1)

                def router_logits(t):
                    pe.wait_ge(hT_act, l * 2 + t + 1)
                    pe.wait_ge(hT_dve, l * 2 + t + 1)
                    last = group(ps[:, 4 + t, 0:G + E],
                                 [(hT[:, c, P * t:P * (t + 1)],
                                   w_route[:, bass.ds(l, 1), c, :].rearrange("p a n -> p (a n)")) for c in range(KD)])
                    if t == TT - 1:
                        last.then_inc(logits_psum, 1)

                for g in range(4):
                    t, h = g // 2, g % 2

                    def before(c):
                        if h == 0 and c % 2 == 0:
                            pe.wait_ge(merged_lo_ready, l * 4 + (c // 2 + 1))
                        if c % 4 == 0:
                            split_done(W_O + h, 2 + c // 2)
                    m = [(merged_hi[:, c, P * t:P * (t + 1)], merged_lo[:, c, P * t:P * (t + 1)]) for c in range(KD)]
                    group3(ps[:, 4 + g, :], list(zip(m, chunk(W_O + h, slice(0, 512)))),
                           before if t == 0 else None).then_inc(wo_psum, 1)
                    if g == 2:
                        normed_transposes(0)
                pe.wait_ge(late_in, 16 * LATE)
                router_logits(0)
                normed_transposes(1)
                router_logits(1)
                pe.wait_ge(chosen_ready, l + 1)
                ch = chosen[:, :, :, :].rearrange("p t g e -> p (t g e)")
                mm(ps[:, 6, 0:TT * E], tri_strict_r[:, :], ch, start=True, stop=False)
                mm(ps[:, 6, E:TT * E], ones_r[:, :], ch[:, 0:E], start=False, stop=True).then_inc(pos_psum, 1)
                group(ps[:, 7, 0:E], [(ones_r[:, :], ch[:, 0:E]), (ones_r[:, :], ch[:, E:2 * E])]).then_inc(count_psum, 1)

                def gather(r):
                    pe.wait_ge(pick_ready, r + 1)
                    for k in range(2):
                        for j in range(KD // 2):
                            c = 2 * j + k
                            last = group(ps[:, k, P * j:P * (j + 1)],
                                         [(hn[:, t, P * c:P * (c + 1)], pick[:, t, :]) for t in range(TT)])
                        last.then_inc(gather_psum, 1)

                def both(bank, parts):
                    for i, (a, b) in enumerate(parts):
                        for e in range(2):
                            half = slice(CAP * e, CAP * (e + 1))
                            last = mm(ps[half, bank, :], a[:, half], b[e], start=(i == 0), stop=(i == len(parts) - 1))
                        yield i, last

                def pair(p, first, last):
                    r = l * NP + p
                    if first:
                        gather(r)
                    pe.wait_ge(gather_sb, 2 * r + 1)

                    def weights(i):
                        w = chunk_at[place_of(p, i)]
                        w = w.rearrange("p (a c n) -> p a c n", a=2, c=4)
                        return [[w[:, e, c, :] for e in range(2)] for c in range(4)]

                    for i in range(2):
                        pe.wait_ge(*pair_full(l, p, 2 * i))
                        ws = weights(2 * i) + weights(2 * i + 1)
                        for c, done_c in both(2 + i, [(xg[:, c, :], ws[c]) for c in range(KD)]):
                            if c == 3:
                                done_c.then_inc(gu_psum, 1)
                                pe.wait_ge(*pair_full(l, p, 2 * i + 1))
                                if i == 0:
                                    pe.wait_ge(gather_sb, 2 * r + 2)
                        done_c.then_inc(gu_psum, 1)
                        if i == 0 and not first:
                            combine(r - 1, p)
                    pe.wait_ge(hid_ready, r + 1)
                    for f in range(KF):
                        last_t = nc.tensor.transpose(ps[:, 2, P * f:P * (f + 1)], hid[:, P * f:P * (f + 1)], ident[:, :])
                    last_t.then_inc(hidT_psum, 1)
                    pe.wait_ge(pg_ready, r + 1)
                    for t in range(TT):
                        last_t = nc.tensor.transpose(ps[:, 3, P * t:P * (t + 1)], pick_gate[:, t, :], ident[:, :])
                    last_t.then_inc(spread_psum, 1)
                    if not last:
                        gather(r + 1)
                    pe.wait_ge(hidT_sb, r + 1)
                    for h in range(2):
                        pe.wait_ge(*pair_full(l, p, 4 + h))
                        for f, done_f in both(4 + h, [(hidT[:, f, :], weights(4 + h)[f]) for f in range(KF)]):
                            pass
                        done_f.then_inc(down_psum, 1)
                        if last:
                            combine_last(r, h)

                def combine_last(r, h):
                    if h == 0:
                        pe.wait_ge(comb_added, 4 * r)
                        pe.wait_ge(spread_sb, r + 1)
                    pe.wait_ge(down_sb, 2 * r + h + 1)
                    for t in range(TT):
                        group(ps[:, LAST_BANK[h][t], :], [(spread[:, P * t:P * (t + 1)], down[:, 512 * h:512 * (h + 1)])]
                              ).then_inc(comb_psum, 1)

                def combine(r, after):
                    if not is_pair(after, 1):
                        pe.wait_ge(comb_added, 4 * r)
                    pe.wait_ge(down_sb, 2 * r + 2)
                    pe.wait_ge(spread_sb, r + 1)
                    for g in range(4):
                        t, h = g // 2, g % 2
                        if g >= 2:
                            pe.wait_ge(comb_added, 4 * r + (g - 1))
                        group(ps[:, 6 + h, :], [(spread[:, P * t:P * (t + 1)], down[:, 512 * h:512 * (h + 1)])]
                              ).then_inc(comb_psum, 1)

                pair(0, True, False)
                for p in range(1, len(FIRST_PAIRS)):
                    pair(p, False, False)
                with pe.Fori(len(FIRST_PAIRS), NP - 1) as p:
                    pair(p, False, False)
                pair(NP - 1, False, True)

                most = pe.value_load(flags[0:1, 0:1], min_val=0, max_val=T)
                before = pe.value_load(flags[0:1, 1:2], min_val=0, max_val=L)
                with pe.If(most > CAP):
                    def over(e, first):
                        n = before * (4 * E) + 4 * e
                        if first:
                            pe.wait_ge(comb_added, l * (4 * NP) + 4 * NP)
                        pe.wait_ge(ov_loaded, before * (48 * E) + 48 * e + 48)
                        for f in range(KF):
                            for i in range(2):
                                last = group(ps[:, f, T * i:T * (i + 1)],
                                             [(by_k(i)[:, c, P * f:P * (f + 1)], hT[:, c, :]) for c in range(KD)])
                            last.then_inc(ov_gu, 1)
                        pe.wait_ge(ov_hid, n + 4)
                        if not first:
                            pe.wait_ge(ov_added, n)
                        for g in range(4):
                            t, h = g // 2, g % 2
                            group(ps[:, 4 + g, :], [(over_hid[:, f, P * t:P * (t + 1)],
                                                     by_f(2)[:, f, 512 * h:512 * (h + 1)]) for f in range(KF)]
                                  ).then_inc(ov_down, 1)

                    over(0, True)
                    with pe.Fori(1, E) as e:
                        over(e, False)


_INS = ['x', 'positions', 'ln1_g', 'w_in', 'b_forget', 'q_norm_diff_g', 'k_norm_diff_g', 'lam_q1', 'lam_k1', 'lam_q2',
        'lam_k2', 'subln_g', 'q_norm_fox_g', 'k_norm_fox_g', 'w_diff_out', 'w_fox_out', 'w_o', 'ln2_g',
        'w_router_group', 'b_router_group', 'w_router_expert', 'b_router_expert', 'w_exp_gate', 'w_exp_up',
        'w_exp_down']


def kernel(**inputs):
    import numpy as _np
    import concourse.bacc as _bacc
    from concourse import mybir as _mybir
    from concourse.bass_utils import run_bass_kernel_spmd as _run

    nc = _bacc.Bacc("TRN2", target_bir_lowering=False, num_devices=1)
    arrays, args = {}, []
    for name in _INS:
        a = _np.ascontiguousarray(inputs[name])
        if name.startswith("w_exp"):
            a = a.reshape(-1, *a.shape[3:])
        arrays[f"in_{name}_dram"] = a
        args.append(nc.dram_tensor(f"in_{name}_dram", a.shape, _mybir.dt.from_np(a.dtype), kind="ExternalInput").ap())
    args.append(nc.dram_tensor("out_dram", (1, T, D), _mybir.dt.float32, kind="ExternalOutput").ap())
    hybrid_trunk(nc, *args)
    r = _run(nc, [arrays], core_ids=[0])
    return r.results[0]["out_dram"]
```
